# Optimizing a Trainium2 kernel written in Bass

```python
import math
import jax, jax.numpy as jnp
from jax import lax
import numpy as np

D_MODEL = 1024
BATCH = 1
SEQ = 512
DEPTH = 1

HEAD_DIM = 64
MIX_WIDTH = D_MODEL
N_HEADS_A = (MIX_WIDTH // 2) // HEAD_DIM
N_HEADS_B = (MIX_WIDTH // 2) // HEAD_DIM
D_NOPE = HEAD_DIM
D_ROPE = HEAD_DIM // 2
KV_RANK = 2 * HEAD_DIM
V_DIM = HEAD_DIM
IDX_HEADS = 8
IDX_DIM = HEAD_DIM
TOPK_MAX = 256
Q_BLOCK = 128
DILATED_PATTERNS = ((128, 1), (512, 4), (2048, 16))
CROSS_HEADS = 4
CROSS_HEAD_DIM = D_MODEL // CROSS_HEADS
MEM_TOKENS = 256
D_FF = 4 * D_MODEL
ROPE_THETA = 10000.0
NORM_EPS = 1e-6

IN_SIZES = (N_HEADS_A * D_NOPE,
            N_HEADS_A * D_ROPE,
            KV_RANK,
            D_ROPE,
            IDX_HEADS * IDX_DIM,
            IDX_DIM,
            IDX_HEADS,
            3 * N_HEADS_B * HEAD_DIM)
IN_COLS = 512 + 256 + 128 + 32 + 512 + 64 + 8 + 1536 if D_MODEL == 1024 else int(np.sum(IN_SIZES))


def rmsnorm(x, g):
    xf = x.astype(jnp.float32)
    y = xf * lax.rsqrt(jnp.mean(xf * xf, axis=-1, keepdims=True) + NORM_EPS)
    return (y * g.astype(jnp.float32)).astype(x.dtype)

def rope(x):
    S, d = x.shape[1], x.shape[-1]
    inv = ROPE_THETA ** (-jnp.arange(0, d, 2, dtype=jnp.float32) / d)
    ang = jnp.arange(S, dtype=jnp.float32)[:, None] * inv[None, :]
    cos = jnp.cos(ang)[None, :, None, :].astype(x.dtype)
    sin = jnp.sin(ang)[None, :, None, :].astype(x.dtype)
    x1, x2 = jnp.split(x, 2, axis=-1)
    return jnp.concatenate([x1 * cos - x2 * sin, x2 * cos + x1 * sin], axis=-1)

def dsa_sparse_attention(q_nope, q_rope, c_kv, k_rope, q_idx, k_idx, w_idx, w_uk, w_uv):
    B, S = q_nope.shape[0], q_nope.shape[1]
    topk = min(TOPK_MAX, S // 4)
    nb = S // Q_BLOCK
    scale = (D_NOPE + D_ROPE) ** -0.5
    q_lat = jnp.einsum('bshn,hnc->bshc', q_nope, w_uk)
    w_eff = w_idx.astype(jnp.float32) * (IDX_HEADS ** -0.5) * (IDX_DIM ** -0.5)
    key_pos = jnp.arange(S)
    gather = jax.vmap(lambda table, ix: table[ix])

    def to_blocks(a):
        return jnp.moveaxis(a.reshape((B, nb, Q_BLOCK) + a.shape[2:]), 1, 0)

    def block(args):
        ql, qr, qi, wi, blk = args
        q_pos = blk * Q_BLOCK + jnp.arange(Q_BLOCK)
        causal = key_pos[None, :] <= q_pos[:, None]
        logits = jnp.einsum('bqhd,bsd->bhqs', qi, k_idx).astype(jnp.float32)
        index = jnp.einsum('bhqs,bqh->bqs', jax.nn.relu(logits), wi)
        index = jnp.where(causal[None], index, -jnp.inf)
        _, sel = lax.top_k(index, topk)
        valid = sel <= q_pos[None, :, None]
        c_sel = gather(c_kv, sel)
        r_sel = gather(k_rope, sel)
        s = (jnp.einsum('bqhc,bqkc->bhqk', ql, c_sel)
             + jnp.einsum('bqhr,bqkr->bhqk', qr, r_sel)).astype(jnp.float32) * scale
        s = jnp.where(valid[:, None], s, -jnp.inf)
        p = jax.nn.softmax(s, axis=-1).astype(c_sel.dtype)
        return jnp.einsum('bhqk,bqkc->bqhc', p, c_sel)

    o_lat = lax.map(block, (to_blocks(q_lat), to_blocks(q_rope), to_blocks(q_idx),
                            to_blocks(w_eff), jnp.arange(nb)))
    o_lat = jnp.moveaxis(o_lat, 0, 1).reshape(B, S, N_HEADS_A, KV_RANK)
    return jnp.einsum('bshc,hcv->bshv', o_lat, w_uv)

def dilated_pattern(q, k, v, window, dilation):
    B, H, S, d = q.shape
    n = S // dilation
    w_sub = window // dilation
    nb = -(-n // Q_BLOCK)
    pad = nb * Q_BLOCK - n

    def split(a):
        a = a.reshape(B, H, n, dilation, d).transpose(0, 1, 3, 2, 4)
        a = jnp.pad(a, ((0, 0), (0, 0), (0, 0), (0, pad), (0, 0)))
        return a.reshape(B, H, dilation, nb, Q_BLOCK, d)

    def with_prev(a):
        prev = jnp.concatenate([jnp.zeros_like(a[:, :, :, :1]), a[:, :, :, :-1]], axis=3)
        return jnp.concatenate([prev, a], axis=4)

    qb = split(q)
    kk = with_prev(split(k))
    vv = with_prev(split(v))
    s = jnp.einsum('bhrnqd,bhrnkd->bhrnqk', qb, kk).astype(jnp.float32) * (d ** -0.5)
    rel = (jnp.arange(Q_BLOCK)[:, None] + Q_BLOCK) - jnp.arange(2 * Q_BLOCK)[None, :]
    band = (rel >= 0) & (rel <= w_sub)
    has_prev = (jnp.arange(nb)[:, None, None] > 0) | (jnp.arange(2 * Q_BLOCK)[None, None, :] >= Q_BLOCK)
    mask = band[None] & has_prev
    s = jnp.where(mask, s, -jnp.inf)
    lse = jax.nn.logsumexp(s, axis=-1)
    p = jnp.exp(s - lse[..., None]).astype(v.dtype)
    o = jnp.einsum('bhrnqk,bhrnkd->bhrnqd', p, vv)

    def merge(a, tail):
        a = a.reshape((B, H, dilation, nb * Q_BLOCK) + tail)[:, :, :, :n]
        return jnp.swapaxes(a, 2, 3).reshape((B, H, S) + tail)

    return merge(o, (d,)), merge(lse, ())

def dilated_attention(q, k, v):
    outs, lses = [], []
    for window, dilation in DILATED_PATTERNS:
        o, l = dilated_pattern(q, k, v, window, dilation)
        outs.append(o)
        lses.append(l)
    alpha = jax.nn.softmax(jnp.stack(lses, axis=0), axis=0).astype(q.dtype)
    return jnp.sum(alpha[..., None] * jnp.stack(outs, axis=0), axis=0)

def first_inputs(seed: int = 0) -> dict:
    key = jax.random.key(seed)
    ks = jax.random.split(key, 20)
    f32 = jnp.float32

    def w(k, shape, fan_in):
        return jax.random.normal(k, shape, f32) * (fan_in ** -0.5)

    def gain(k, shape):
        return 1.0 + 0.02 * jax.random.normal(k, shape, f32)

    L = DEPTH
    return {
        "x": jax.random.normal(ks[0], (BATCH, SEQ, D_MODEL), f32),
        "mem": jax.random.normal(ks[1], (BATCH, MEM_TOKENS, D_MODEL), f32),
        "norm_mix_g": gain(ks[2], (L, D_MODEL)),
        "w_in": w(ks[3], (L, D_MODEL, IN_COLS), D_MODEL),
        "kv_norm_g": gain(ks[4], (L, KV_RANK)),
        "w_uk": w(ks[5], (L, N_HEADS_A, D_NOPE, KV_RANK), D_NOPE),
        "w_uv": w(ks[6], (L, N_HEADS_A, KV_RANK, V_DIM), KV_RANK),
        "w_out": w(ks[7], (L, N_HEADS_A * V_DIM + N_HEADS_B * HEAD_DIM, D_MODEL), MIX_WIDTH),
        "norm_cross_g": gain(ks[8], (L, D_MODEL)),
        "norm_mem_g": gain(ks[9], (L, D_MODEL)),
        "w_q_cross": w(ks[10], (L, D_MODEL, CROSS_HEADS * CROSS_HEAD_DIM), D_MODEL),
        "w_kv_cross": w(ks[11], (L, D_MODEL, 2 * CROSS_HEADS * CROSS_HEAD_DIM), D_MODEL),
        "w_o_cross": w(ks[12], (L, CROSS_HEADS * CROSS_HEAD_DIM, D_MODEL), CROSS_HEADS * CROSS_HEAD_DIM),
        "norm_mlp_g": gain(ks[13], (L, D_MODEL)),
        "w_up": w(ks[14], (L, D_MODEL, D_FF), D_MODEL),
        "w_down": w(ks[15], (L, D_FF, D_MODEL), D_FF),
        "norm_final_g": gain(ks[16], (D_MODEL,)),
    }

def first_block(x, mem, norm_mix_g, w_in, kv_norm_g, w_uk, w_uv, w_out, norm_cross_g, norm_mem_g,
              w_q_cross, w_kv_cross, w_o_cross, norm_mlp_g, w_up, w_down, norm_final_g):
    B, S, _ = x.shape
    M = mem.shape[1]
    split_at = [int(c) for c in np.cumsum(IN_SIZES)[:-1]]
    for l in range(DEPTH):
        h = rmsnorm(x, norm_mix_g[l])
        proj = h @ w_in[l]
        p_qn, p_qr, p_ckv, p_kr, p_qi, p_ki, p_wi, p_qkv = jnp.split(proj, split_at, axis=-1)
        q_nope = p_qn.reshape(B, S, N_HEADS_A, D_NOPE)
        q_rope = rope(p_qr.reshape(B, S, N_HEADS_A, D_ROPE))
        c_kv = rmsnorm(p_ckv, kv_norm_g[l])
        k_rope = rope(p_kr[:, :, None, :])[:, :, 0]
        q_idx = rope(p_qi.reshape(B, S, IDX_HEADS, IDX_DIM))
        k_idx = rope(p_ki[:, :, None, :])[:, :, 0]
        o_a = dsa_sparse_attention(q_nope, q_rope, c_kv, k_rope, q_idx, k_idx, p_wi, w_uk[l], w_uv[l])
        qkv = p_qkv.reshape(B, S, 3, N_HEADS_B, HEAD_DIM)
        q_b = rope(qkv[:, :, 0]).transpose(0, 2, 1, 3)
        k_b = rope(qkv[:, :, 1]).transpose(0, 2, 1, 3)
        v_b = qkv[:, :, 2].transpose(0, 2, 1, 3)
        o_b = dilated_attention(q_b, k_b, v_b).transpose(0, 2, 1, 3)
        heads = jnp.concatenate([o_a.reshape(B, S, N_HEADS_A * V_DIM),
                                 o_b.reshape(B, S, N_HEADS_B * HEAD_DIM)], axis=-1)
        x = x + heads @ w_out[l]
        hc = rmsnorm(x, norm_cross_g[l])
        m = rmsnorm(mem, norm_mem_g[l])
        qc = (hc @ w_q_cross[l]).reshape(B, S, CROSS_HEADS, CROSS_HEAD_DIM)
        kvc = (m @ w_kv_cross[l]).reshape(B, M, 2, CROSS_HEADS, CROSS_HEAD_DIM)
        sc = jnp.einsum('bshd,bmhd->bhsm', qc, kvc[:, :, 0]).astype(jnp.float32) * (CROSS_HEAD_DIM ** -0.5)
        pc = jax.nn.softmax(sc, axis=-1).astype(x.dtype)
        oc = jnp.einsum('bhsm,bmhd->bshd', pc, kvc[:, :, 1]).reshape(B, S, CROSS_HEADS * CROSS_HEAD_DIM)
        x = x + oc @ w_o_cross[l]
        hm = rmsnorm(x, norm_mlp_g[l])
        x = x + jnp.square(jax.nn.relu(hm @ w_up[l])) @ w_down[l]
    return rmsnorm(x, norm_final_g)


DEPTH_2 = 2

GRID_W = 64
CTX_LEN = 256
MIX_WIDTH_2 = D_MODEL
S5_WIDTH = (3 * MIX_WIDTH_2) // 4
FNET_WIDTH = MIX_WIDTH_2 - S5_WIDTH
S5_H = 16
S5_GROUPS = S5_WIDTH // S5_H
S5_P = 64
FNET_GROUPS = 4
FNET_GW = FNET_WIDTH // FNET_GROUPS
POOL_WIDTH = MIX_WIDTH_2 // 2
CONV_WIDTH = MIX_WIDTH_2 - POOL_WIDTH
POOL_WINDOWS = (2, 4, 8, 16)
POOL_GROUPS = len(POOL_WINDOWS)
POOL_GW = POOL_WIDTH // POOL_GROUPS
CONV_K = 3
N_EVEN = (DEPTH_2 + 1) // 2
N_ODD = DEPTH_2 // 2
EVEN_IN = S5_WIDTH + FNET_WIDTH + MIX_WIDTH_2
ODD_IN = POOL_WIDTH + 3 * CONV_WIDTH + MIX_WIDTH_2
STEP_MIN = 1e-3
STEP_MAX = 1e-1
EPS = 1e-6
POS_BASE = 10000.0


def rmsnorm_2(x, g):
    xf = x.astype(jnp.float32)
    y = xf * lax.rsqrt(jnp.mean(xf * xf, axis=-1, keepdims=True) + EPS)
    return (y * g.astype(jnp.float32)).astype(x.dtype)

def ada_params(cond, w, b):
    m = jax.nn.silu(cond) @ w + b
    return jnp.split(m, 3, axis=-1)

def sincos_2d(n_tok, dim):
    rows = n_tok // GRID_W
    r = jnp.arange(rows, dtype=jnp.float32)
    col = jnp.arange(GRID_W, dtype=jnp.float32)
    rr, cc = jnp.meshgrid(r, col, indexing='ij')
    rr = rr.reshape(-1, 1)
    cc = cc.reshape(-1, 1)
    quarter = dim // 4
    omega = POS_BASE ** (-jnp.arange(quarter, dtype=jnp.float32) / quarter)
    return jnp.concatenate([jnp.sin(rr * omega), jnp.cos(rr * omega),
                            jnp.sin(cc * omega), jnp.cos(cc * omega)], axis=-1)

def _linear_recurrence(e1, e2):
    a1, b1 = e1
    a2, b2 = e2
    return a2 * a1, a2 * b1 + b2

def s5_direction(u, lam_re, lam_im, log_step, b_re, b_im, c_re, c_im):
    f32 = jnp.float32
    lam = lax.complex(lam_re.astype(f32), lam_im.astype(f32))
    step = jnp.exp(log_step.astype(f32))[:, None]
    lam_bar = jnp.exp(lam * step)
    b_bar = ((lam_bar - 1.0) / lam)[..., None] * lax.complex(b_re.astype(f32), b_im.astype(f32))
    bu = lax.complex(jnp.einsum('btgh,gph->btgp', u, b_bar.real),
                     jnp.einsum('btgh,gph->btgp', u, b_bar.imag))
    a = jnp.broadcast_to(lam_bar, bu.shape)
    _, s = lax.associative_scan(_linear_recurrence, (a, bu), axis=1)
    return (jnp.einsum('btgp,ghp->btgh', s.real, c_re.astype(f32))
            - jnp.einsum('btgp,ghp->btgh', s.imag, c_im.astype(f32)))

def s5_bidir(u_lat, u_ctx, need_ctx, lam_re, lam_im, log_step, b_re, b_im, c_re, c_im, d_skip):
    bsz, t_lat, _ = u_lat.shape
    t_ctx = u_ctx.shape[1]
    ul = u_lat.astype(jnp.float32).reshape(bsz, t_lat, S5_GROUPS, S5_H)
    uc = u_ctx.astype(jnp.float32).reshape(bsz, t_ctx, S5_GROUPS, S5_H)
    yf = s5_direction(jnp.concatenate([uc, ul], axis=1),
                      lam_re[0], lam_im[0], log_step[0], b_re[0], b_im[0], c_re[0], c_im[0])
    yb = s5_direction(jnp.concatenate([jnp.flip(uc, 1), jnp.flip(ul, 1)], axis=1),
                      lam_re[1], lam_im[1], log_step[1], b_re[1], b_im[1], c_re[1], c_im[1])
    d = d_skip.astype(jnp.float32)
    y_lat = yf[:, t_ctx:] + jnp.flip(yb[:, t_ctx:], 1) + d * ul
    y_lat = y_lat.reshape(bsz, t_lat, S5_WIDTH)
    if not need_ctx:
        return y_lat, None
    y_ctx = yf[:, :t_ctx] + jnp.flip(yb[:, :t_ctx], 1) + d * uc
    return y_lat, y_ctx.reshape(bsz, t_ctx, S5_WIDTH)

def fnet_mix(u, f_w):
    bsz, t, _ = u.shape
    g = u.astype(jnp.float32).reshape(bsz, t, FNET_GROUPS, FNET_GW).transpose(0, 2, 1, 3)
    f = jnp.fft.fft2(g, axes=(-2, -1), norm='ortho').real
    y = jnp.einsum('bgtc,gcd->btgd', f, f_w.astype(jnp.float32))
    return y.reshape(bsz, t, FNET_WIDTH)

def even_branch_out(ya, ub, z, glu_w, glu_b, f_w, w_out):
    ya = jax.nn.gelu(ya)
    ya = ya * jax.nn.sigmoid(ya @ glu_w.astype(jnp.float32) + glu_b.astype(jnp.float32))
    yb = fnet_mix(ub, f_w)
    y = jnp.concatenate([ya, yb], axis=-1).astype(z.dtype) * jax.nn.silu(z)
    return y @ w_out

def even_mixer(hl, hc, need_ctx, w_in, w_out, lam_re, lam_im, log_step, b_re, b_im,
               c_re, c_im, d_skip, glu_w, glu_b, f_w):
    pl = hl @ w_in
    pc = hc @ w_in if need_ctx else hc @ w_in[:, :S5_WIDTH]
    ya_l, ya_c = s5_bidir(pl[..., :S5_WIDTH], pc[..., :S5_WIDTH], need_ctx,
                          lam_re, lam_im, log_step, b_re, b_im, c_re, c_im, d_skip)
    out_l = even_branch_out(ya_l, pl[..., S5_WIDTH:MIX_WIDTH_2], pl[..., MIX_WIDTH_2:],
                            glu_w, glu_b, f_w, w_out)
    if not need_ctx:
        return out_l, None
    out_c = even_branch_out(ya_c, pc[..., S5_WIDTH:MIX_WIDTH_2], pc[..., MIX_WIDTH_2:],
                            glu_w, glu_b, f_w, w_out)
    return out_l, out_c

def centered_mean(v, window):
    bsz, t, ch = v.shape
    s = jnp.concatenate([jnp.zeros((bsz, 1, ch), v.dtype), jnp.cumsum(v, axis=1)], axis=1)
    pos = jnp.arange(t)
    lo = jnp.clip(pos - window // 2, 0, t)
    hi = jnp.clip(pos + window // 2, 0, t)
    total = jnp.take(s, hi, axis=1) - jnp.take(s, lo, axis=1)
    return total / (hi - lo).astype(v.dtype)[None, :, None]

def pool_mix(u, p_w, p_scale):
    bsz, t, _ = u.shape
    g = u.astype(jnp.float32).reshape(bsz, t, POOL_GROUPS, POOL_GW)
    pooled = jnp.stack([centered_mean(g[:, :, i], POOL_WINDOWS[i]) - g[:, :, i]
                        for i in range(POOL_GROUPS)], axis=2)
    y = jnp.einsum('btgc,gcd->btgd', pooled, p_w.astype(jnp.float32)).reshape(bsz, t, POOL_WIDTH)
    return (y * p_scale.astype(jnp.float32)).astype(u.dtype)

def short_conv(v, w):
    return lax.conv_general_dilated(v, w[:, None, :].astype(v.dtype), window_strides=(1,),
                                    padding=[(CONV_K // 2, CONV_K // 2)],
                                    dimension_numbers=('NWC', 'WIO', 'NWC'),
                                    feature_group_count=v.shape[-1])

def odd_mixer(h, w_in, w_out, p_w, p_scale, conv_w):
    p = h @ w_in
    o1 = POOL_WIDTH
    o2 = o1 + CONV_WIDTH
    o3 = o2 + CONV_WIDTH
    o4 = o3 + CONV_WIDTH
    y_c = pool_mix(p[..., :o1], p_w, p_scale)
    c_gate, x_path, b_gate, z = p[..., o1:o2], p[..., o2:o3], p[..., o3:o4], p[..., o4:]
    y_d = b_gate * short_conv(c_gate * x_path, conv_w)
    y = jnp.concatenate([y_c, y_d], axis=-1) * jax.nn.silu(z)
    return y @ w_out

def second_inputs(seed: int = 0) -> dict:
    key = jax.random.key(seed)
    ks = jax.random.split(key, 26)
    f32 = jnp.float32
    D = D_MODEL

    def nrm(k, shape, s):
        return jax.random.normal(k, shape, f32) * s

    s5_state_shape = (N_EVEN, 2, S5_GROUPS, S5_P)
    return {
        'x': nrm(ks[0], (BATCH, SEQ, D), 1.0),
        'c': nrm(ks[1], (BATCH, D), 1.0),
        'ctx': nrm(ks[2], (BATCH, CTX_LEN, D), 1.0),
        'c_ctx': nrm(ks[3], (D,), 1.0),
        'norm_g': 1.0 + nrm(ks[4], (DEPTH_2, D), 0.02),
        'ada_w': nrm(ks[5], (DEPTH_2, D, 3 * D), 0.5 * D ** -0.5),
        'ada_b': nrm(ks[6], (DEPTH_2, 3 * D), 0.02),
        'even_w_in': nrm(ks[7], (N_EVEN, D, EVEN_IN), D ** -0.5),
        'even_w_out': nrm(ks[8], (N_EVEN, MIX_WIDTH_2, D), MIX_WIDTH_2 ** -0.5),
        's5_lam_re': -0.5 + nrm(ks[9], s5_state_shape, 0.01),
        's5_lam_im': jnp.pi * jnp.arange(S5_P, dtype=f32) + nrm(ks[10], s5_state_shape, 0.01),
        's5_log_step': jax.random.uniform(ks[11], (N_EVEN, 2, S5_GROUPS), f32,
                                          math.log(STEP_MIN), math.log(STEP_MAX)),
        's5_b_re': nrm(ks[12], (N_EVEN, 2, S5_GROUPS, S5_P, S5_H), (2 * S5_H) ** -0.5),
        's5_b_im': nrm(ks[13], (N_EVEN, 2, S5_GROUPS, S5_P, S5_H), (2 * S5_H) ** -0.5),
        's5_c_re': nrm(ks[14], (N_EVEN, 2, S5_GROUPS, S5_H, S5_P), S5_P ** -0.5),
        's5_c_im': nrm(ks[15], (N_EVEN, 2, S5_GROUPS, S5_H, S5_P), S5_P ** -0.5),
        's5_d': 1.0 + nrm(ks[16], (N_EVEN, S5_GROUPS, S5_H), 0.1),
        's5_glu_w': nrm(ks[17], (N_EVEN, S5_WIDTH, S5_WIDTH), S5_WIDTH ** -0.5),
        's5_glu_b': nrm(ks[18], (N_EVEN, S5_WIDTH), 0.02),
        'fnet_w': nrm(ks[19], (N_EVEN, FNET_GROUPS, FNET_GW, FNET_GW), FNET_GW ** -0.5),
        'odd_w_in': nrm(ks[20], (N_ODD, D, ODD_IN), D ** -0.5),
        'odd_w_out': nrm(ks[21], (N_ODD, MIX_WIDTH_2, D), MIX_WIDTH_2 ** -0.5),
        'pool_w': nrm(ks[22], (N_ODD, POOL_GROUPS, POOL_GW, POOL_GW), POOL_GW ** -0.5),
        'pool_scale': 1.0 + nrm(ks[23], (N_ODD, POOL_WIDTH), 0.1),
        'conv_w': nrm(ks[24], (N_ODD, CONV_K, CONV_WIDTH), CONV_K ** -0.5),
        'final_g': 1.0 + nrm(ks[25], (D,), 0.02),
    }

def second_block(x, c, ctx, c_ctx, norm_g, ada_w, ada_b, even_w_in, even_w_out,
              s5_lam_re, s5_lam_im, s5_log_step, s5_b_re, s5_b_im, s5_c_re, s5_c_im,
              s5_d, s5_glu_w, s5_glu_b, fnet_w, odd_w_in, odd_w_out, pool_w,
              pool_scale, conv_w, final_g):
    n_tok = x.shape[1]
    xl = x + sincos_2d(n_tok, x.shape[-1]).astype(x.dtype)[None]
    xc = ctx
    need_ctx = [any(j % 2 == 0 for j in range(l + 1, DEPTH_2)) for l in range(DEPTH_2)]
    for l in range(DEPTH_2):
        i = l // 2
        shift, scale, gate = ada_params(c, ada_w[l], ada_b[l])
        hl = rmsnorm_2(xl, norm_g[l]) * (1.0 + scale[:, None]) + shift[:, None]
        use_ctx_in = (l % 2 == 0) or need_ctx[l]
        if use_ctx_in:
            shift_c, scale_c, gate_c = ada_params(c_ctx, ada_w[l], ada_b[l])
            hc = rmsnorm_2(xc, norm_g[l]) * (1.0 + scale_c) + shift_c
        if l % 2 == 0:
            out_l, out_c = even_mixer(hl, hc, need_ctx[l], even_w_in[i], even_w_out[i],
                                      s5_lam_re[i], s5_lam_im[i], s5_log_step[i],
                                      s5_b_re[i], s5_b_im[i], s5_c_re[i], s5_c_im[i],
                                      s5_d[i], s5_glu_w[i], s5_glu_b[i], fnet_w[i])
        else:
            out_l = odd_mixer(hl, odd_w_in[i], odd_w_out[i], pool_w[i], pool_scale[i], conv_w[i])
            out_c = (odd_mixer(hc, odd_w_in[i], odd_w_out[i], pool_w[i], pool_scale[i], conv_w[i])
                     if need_ctx[l] else None)
        xl = xl + gate[:, None] * out_l.astype(xl.dtype)
        if need_ctx[l]:
            xc = xc + gate_c * out_c.astype(xc.dtype)
    return rmsnorm_2(xl, final_g)


def setup_inputs(seed=0):
    out = dict(first_inputs(seed))
    for name, value in second_inputs(seed + 1).items():
        if name != "x":
            out[name + "_2"] = value
    return out


def reference(
    x, mem, norm_mix_g, w_in, kv_norm_g, w_uk, w_uv, w_out, norm_cross_g, norm_mem_g, w_q_cross,
    w_kv_cross, w_o_cross, norm_mlp_g, w_up, w_down, norm_final_g, c_2, ctx_2, c_ctx_2,
    norm_g_2, ada_w_2, ada_b_2, even_w_in_2, even_w_out_2, s5_lam_re_2, s5_lam_im_2,
    s5_log_step_2, s5_b_re_2, s5_b_im_2, s5_c_re_2, s5_c_im_2, s5_d_2, s5_glu_w_2, s5_glu_b_2,
    fnet_w_2, odd_w_in_2, odd_w_out_2, pool_w_2, pool_scale_2, conv_w_2, final_g_2,
):
    x = first_block(
        x, mem, norm_mix_g, w_in, kv_norm_g, w_uk, w_uv, w_out, norm_cross_g, norm_mem_g,
        w_q_cross, w_kv_cross, w_o_cross, norm_mlp_g, w_up, w_down, norm_final_g,
    )
    return second_block(
        x, c_2, ctx_2, c_ctx_2, norm_g_2, ada_w_2, ada_b_2, even_w_in_2, even_w_out_2,
        s5_lam_re_2, s5_lam_im_2, s5_log_step_2, s5_b_re_2, s5_b_im_2, s5_c_re_2, s5_c_im_2,
        s5_d_2, s5_glu_w_2, s5_glu_b_2, fnet_w_2, odd_w_in_2, odd_w_out_2, pool_w_2,
        pool_scale_2, conv_w_2, final_g_2,
    )


_drawn_inputs = setup_inputs


def setup_inputs(seed=0):
    import zlib

    import numpy as np

    out = dict(_drawn_inputs(seed))
    spreads = {}
    factors = {'norm_mix_g': 3.369,
     'kv_norm_g': 8.0,
     'norm_cross_g': 8.0,
     'norm_mem_g': 8.0,
     'norm_mlp_g': 3.66,
     'norm_final_g': 3.396,
     'ctx_2': 64.0,
     'c_ctx_2': 64.0,
     'norm_g_2': 8.0,
     'ada_b_2': 3.788,
     's5_lam_re_2': 64.0,
     's5_lam_im_2': 38.976,
     's5_log_step_2': 55.712,
     's5_b_re_2': 48.64,
     's5_b_im_2': 45.264,
     's5_c_re_2': 51.76,
     's5_c_im_2': 54.728,
     's5_d_2': 7.582,
     's5_glu_w_2': 2.945,
     's5_glu_b_2': 42.579,
     'pool_scale_2': 40.98,
     'final_g_2': 7.983}
    for name, (base, spread) in spreads.items():
        noise = np.random.default_rng([zlib.crc32(name.encode()), seed]).standard_normal(out[name].shape)
        drawn = base * np.exp(spread * noise) if base else spread * noise
        out[name] = __import__('jax').numpy.asarray(drawn.astype(out[name].dtype))
    for name, factor in factors.items():
        out[name] = (out[name] * factor).astype(out[name].dtype)
    return out
```

```python
from contextlib import ExitStack

import numpy as np
import concourse.bass as bass
from concourse import mybir

ALU = mybir.AluOpType
ACT = mybir.ActivationFunctionType
AX = mybir.AxisListType.X
F32 = mybir.dt.float32

P = 128
D = 1024
DT = D // P
SEQ = 512
TT = SEQ // P
MEM = 256
CTX = 256
HEADS = 8
FF = 4096
TOPK = 128
EPS = 1e-6
OFF = -1e30
TAKEN = -3e38
SLOTS = 3
ARENA = 29696
RING = 6
SCALE_A = float(96) ** -0.5
SCALE_B = float(64) ** -0.5
SCALE_C = float(256) ** -0.5

GRID_W = 64
POOL_WINDOWS = (2, 4, 8, 16)
GROUPS = 48
PAIRS = GROUPS // 2
DK = 2 * PAIRS
CH = 8
NCH = (CTX + SEQ) // CH
NCTX = CTX // CH
NLAT = SEQ // CH
TWO_PI = (6.28125, 0.0019350051879882812, 2 * np.pi - 6.28125 - 0.0019350051879882812)
ROUND = 12582912.0

VEC_ROWS = [("norm_mix_g", 8), ("norm_cross_g", 8), ("norm_mem_g", 8), ("norm_mlp_g", 8), ("norm_final_g", 8),
            ("norm_g_2", 16), ("final_g_2", 8), ("pool_scale_2", 4), ("s5_glu_b_2", 6), ("conv_w_2", 12),
            ("c_2", 8), ("c_ctx_2", 8)]
VEC = {}
for _n, _r in VEC_ROWS:
    VEC[_n] = sum(r for _, r in VEC_ROWS[:len(VEC)])
VEC_N = sum(r for _, r in VEC_ROWS)


def constants():
    f = np.float32
    out = {"k_ident": np.eye(P, dtype=f)}
    t = np.arange(SEQ, dtype=f)
    tabs = []
    for d in (64, 32):
        inv = (f(10000.0) ** (-np.arange(0, d, 2, dtype=f) / f(d))).astype(f)
        p = np.arange(P)
        ang = (t[None, :] * inv[p % (d // 2)][:, None]).astype(f)
        sign = np.where((p % d) < d // 2, -1.0, 1.0)[:, None]
        tabs += [np.cos(ang.astype(np.float64)), sign * np.sin(ang.astype(np.float64))]
    out["k_rope"] = np.stack(tabs, 1).astype(f)
    perm = np.zeros((P, 2, P), f)
    for n, d in enumerate((64, 32)):
        for p in range(P):
            perm[(p // d) * d + (p % d + d // 2) % d, n, p] = 1
    out["k_perm"] = perm
    q, k = np.arange(P)[:, None], np.arange(P)[None, :]
    out["k_causal"] = np.where(k <= q, 0.0, OFF).astype(f)
    tiles = []
    for delta in (3, 2, 1, 0):
        d = delta * P + q - k
        c = ((d >= 0) & (d <= 128)) * 1.0 + ((d >= 0) & (d % 4 == 0)) + ((d >= 0) & (d % 16 == 0))
        tiles.append(np.where(c > 0, np.log(np.maximum(c, 1)) / SCALE_B, OFF))
    out["k_dilated"] = np.concatenate(tiles, 1).astype(f)
    quarter = D // 4
    omega = f(10000.0) ** (-np.arange(quarter, dtype=f) / f(quarter))
    rr = (np.arange(SEQ) // GRID_W).astype(f)[:, None] * omega
    cc = (np.arange(SEQ) % GRID_W).astype(f)[:, None] * omega
    rr, cc = rr.astype(np.float64), cc.astype(np.float64)
    out["k_pos"] = np.concatenate([np.sin(rr), np.cos(rr), np.sin(cc), np.cos(cc)], 1).T.astype(f).copy()
    t = np.arange(SEQ)
    a = 2 * np.pi * (np.outer(t, t) % SEQ) / SEQ
    out["k_dft"] = np.stack([np.cos(a), -np.sin(a)], 1).astype(np.float64) / np.sqrt(SEQ * 64)
    out["k_dft"] = out["k_dft"].astype(f)
    c = np.arange(64)
    a = 2 * np.pi * (np.outer(c, c) % 64) / 64
    two = np.eye(2)
    out["k_dftc"] = np.concatenate([np.kron(two, np.cos(a)), np.kron(two, np.sin(a))], 1).astype(f)
    rc = [1.0 / (np.minimum(t + w // 2, SEQ) - np.maximum(t - w // 2, 0)) for w in POOL_WINDOWS]
    out["k_rcount"] = np.stack(rc).astype(f)
    return out


class Tiles:

    def __init__(self):
        self.index, self.owner, self.count = {}, [], []
        self.totals = {"act": 0, "dve": 0}

    def add(self, stage, n, owner):
        for i in range(n):
            self.index[stage, i] = len(self.owner)
            self.owner.append(owner)
            self.totals[owner] += 1
            self.count.append(self.totals[owner])
            if isinstance(stage, tuple) and stage[0] in ("up", "down", "ada"):
                self.index[stage] = self.index[stage, i]


def units():
    return [(kind, b, h) for kind in "BA" for b in range(TT) for h in range(HEADS)]


LAG_T, LAG_V = 2, 4


def plan_tiles():
    t = Tiles()
    t.add("vec", 3, "act")
    t.add("xin", DT, "act")
    t.add("mix_ssq", 1, "act")
    t.add("ckv", TT, "act")
    t.add("kir", 2, "act")
    t.add("kirp", 2, "dve")
    t.add("ckvT", 1, "act")
    rope_pair(t, "qi", 4)
    t.add("idx", 24, "act")
    rope_pair(t, "qr", 2)
    t.add("qn", 4, "act")
    rope_pair(t, "qb", 4)
    rope_pair(t, "kb", 4)
    t.add("vb", TT, "act")
    t.add("qlat", HEADS, "act")
    us = units()
    for s in range(len(us) + LAG_V):
        if s < len(us):
            t.add(("S", s), 1, "dve")
        if 0 <= s - LAG_T < len(us):
            t.add(("T", s - LAG_T), 1, "act")
    t.add("oa", 4, "act")
    t.add("out", DT, "dve")
    t.add("memT", DT, "dve")
    t.add("kc", DT, "act")
    t.add("vc", 4, "act")
    t.add("cross_ssq", 1, "act")
    t.add("qc", DT, "act")
    for s in range(16 + 3):
        if s < 16:
            t.add(("CS", s), 1, "dve")
        if 0 <= s - 2 < 16:
            t.add(("CT", s - 2), 1, "act")
    t.add("oc", DT, "dve")
    t.add("mlp_ssq", 1, "act")
    for i in range(8):
        for j in range(4):
            t.add(("up", 4 * i + j), 1, "act")
        t.add(("ada", ADA_AFTER_UP[i]), 1, "dve")
        for m in range(DT if i else 0):
            t.add(("down", 8 * (i - 1) + m), 1, "dve")
        if i in ADA_AFTER_DOWN:
            t.add(("ada", ADA_AFTER_DOWN[i]), 1, "dve")
        if i == 1:
            t.add("cT", 3, "act")
            t.add("lamT", 2, "act")
        if i >= 2:
            t.add(("kk", i - 2), 1, "dve")
        if i == 5:
            t.add("ctxT", 4, "act")
            t.add("ctx_ssq", 1, "act")
    for m in range(DT):
        t.add(("down", 56 + m), 1, "dve")
    t.add("fin_ssq", 1, "act")
    t.add("uc", 6, "act")
    t.add("ev_ssq", 1, "act")
    t.add("ul", 6, "act")
    t.add("ub", 2, "act")
    for bl in range(7):
        if bl < 6:
            for q in range(4):
                t.add(("wt", 4 * bl + q), 1, "act")
        if bl >= 1:
            for q in range(4):
                t.add(("v", 4 * (bl - 1) + q), 1, "act")
    t.add("pq", TT, "act")
    t.add("ft", 2, "act")
    t.add("yb", 2, "act")
    t.add("z", DT, "act")
    t.add("ys", 6, "act")
    t.add("glu", 6, "act")
    t.add("eo", DT, "dve")
    t.add("od_ssq", 1, "act")
    t.add("pool", 4, "act")
    t.add("cg", 4, "act")
    t.add("xp", 4, "dve")
    t.add("bg", 4, "act")
    t.add("zo", DT, "act")
    t.add("pm", 4, "dve")
    t.add("oo", DT, "dve")
    t.add("end_ssq", 1, "act")
    t.add("yout", DT, "act")
    return t


ADA_AFTER_UP = [0, 1, 2, 3, 4, 6, 8, 10]
ADA_AFTER_DOWN = {4: 5, 5: 7, 6: 9, 7: 11}


def rope_pair(t, stage, n):
    for i in range(n + 1):
        if i < n:
            t.index[stage, i] = len(t.owner)
            t.owner.append("act"); t.totals["act"] += 1; t.count.append(t.totals["act"])
        if i >= 1:
            t.index[stage + "p", i - 1] = len(t.owner)
            t.owner.append("dve"); t.totals["dve"] += 1; t.count.append(t.totals["dve"])


CHUNKS = ["kv", "qi", "qr", "qn", "qb", "kb", "vb", "mla", "out0", "out1", "kc0", "kc1", "vc0", "vc1",
          "qc0", "qc1", "oc0", "oc1"]
for _i in range(8):
    CHUNKS += [f"up{_i}", f"ad{ADA_AFTER_UP[_i]}"] + ([f"dn{_i - 1}"] if _i else [])
    CHUNKS += [f"ad{ADA_AFTER_DOWN[_i]}"] if _i in ADA_AFTER_DOWN else []
CHUNKS += ["dn7", "pos", "ev0", "ev1", "fch", "dft"]
CHUNKS += ["none"] * (-len(CHUNKS) % SLOTS)
CHUNKS += ["wbuf", "none", "none", "ev2", "ev3", "none", "Ta", "Tb", "sbuf", "glu0", "glu1", "eo0", "eo1"] + [f"od{_i}" for _i in range(6)] + ["pw", "oo0", "oo1"]



def occupant(n):
    n -= SLOTS
    while CHUNKS[n] == "none":
        n -= SLOTS
    return CHUNKS[n]


LAST_TILE = {"kv": ("kir", 1), "qi": ("qi", 3), "qr": ("qr", 1), "qn": ("qn", 3), "qb": ("qb", 3), "kb": ("kb", 3),
             "vb": ("vb", 3), "mla": ("oa", 3), "vc0": ("vc", 1), "vc1": ("vc", 3)}
for _s in ("out", "kc", "qc", "oc", "up"):
    LAST_TILE.update({f"{_s}{_i}": (_s, 4 * _i + 3) for _i in range(8 if _s == "up" else 2)})
LAST_TILE.update({f"dn{_i}": ("down", 8 * _i + 7) for _i in range(8)})
LAST_TILE.update({"ev0": ("ul", 3), "ev1": ("ub", 1), "ev2": ("z", 3), "ev3": ("z", 7), "fch": ("yb", 1),
                  "dft": ("ft", 1), "wbuf": (("v", 23), 0), "sbuf": ("ys", 5),
                  "glu0": ("glu", 2), "glu1": ("glu", 5), "eo0": ("eo", 3), "eo1": ("eo", 7), "pw": ("pm", 3),
                  "od0": ("pool", 3), "od1": ("cg", 3), "od2": ("xp", 3), "od3": ("bg", 3), "od4": ("zo", 3),
                  "od5": ("zo", 7), "oo0": ("oo", 3), "oo1": ("oo", 7)})

ROPES = [("kir", i) for i in range(2)] + [("qi", i) for i in range(4)] + [("qr", i) for i in range(2)] \
    + [("qb", i) for i in range(4)] + [("kb", i) for i in range(4)]


def build(nc, A, out, UPTO=99):
    T = plan_tiles()
    u_dram = nc.dram_tensor("u_dram", (768, CH, NCH), F32, kind="Internal").ap()
    k_dram = nc.dram_tensor("k_dram", (16, GROUPS, 2 * CH - 1, 16), F32, kind="Internal").ap()
    y_dram = nc.dram_tensor("y_dram", (6, P, 512), F32, kind="Internal").ap()

    def chunk_sources():
        win = A["w_in"][0].rearrange("(j p) n -> p j n", p=P)

        def cols(w, a, n):
            return [(lambda s: s.rearrange("p (j n) -> p j n", j=DT)[:, :, 0:n],
                     w.rearrange("(j p) n -> p j n", p=P)[:, :, a:a + n])]

        def put(a, n, src):
            return (lambda s: s.rearrange("p (j n) -> p j n", j=DT)[:, :, a:a + n], src)

        c = {}
        c["kv"] = [put(0, 128, win[:, :, 768:896]), put(128, 8, win[:, :, 1504:1512])]
        c["kv"] += [put(136 + 64 * i, 64, win[:, :, 1440:1504]) for i in range(2)]
        c["kv"] += [put(264 + 32 * i, 32, win[:, :, 896:928]) for i in range(4)]
        c["qi"] = [put(0, 512, win[:, :, 928:1440])]
        c["qr"] = [put(0, 256, win[:, :, 512:768])]
        c["qn"] = [put(0, 512, win[:, :, 0:512])]
        for i, n in enumerate(("qb", "kb", "vb")):
            c[n] = [put(0, 512, win[:, :, 1512 + 512 * i:2024 + 512 * i])]
        c["mla"] = [(lambda s: s[:, 0:512].rearrange("p (g c) -> p g c", g=4),
                     A["w_uk"][0].rearrange("(g e) n c -> (e n) g c", e=2)),
                    (lambda s: s[:, 512:1024].rearrange("p (h v) -> p h v", h=HEADS),
                     A["w_uv"][0].rearrange("h c v -> c h v"))]
        for i in range(2):
            c[f"out{i}"] = cols(A["w_out"][0], 512 * i, 512)
            c[f"qc{i}"] = cols(A["w_q_cross"][0], 512 * i, 512)
            c[f"oc{i}"] = cols(A["w_o_cross"][0], 512 * i, 512)
            c[f"kc{i}"] = cols(A["w_kv_cross"][0], 512 * i, 512)
            c[f"vc{i}"] = cols(A["w_kv_cross"][0], 1024 + 512 * i, 512)
        for i in range(8):
            c[f"up{i}"] = cols(A["w_up"][0], 512 * i, 512)
        for i in range(8):
            c[f"dn{i}"] = [(lambda s: s.rearrange("p (j n) -> p j n", j=4),
                            A["w_down"][0, 512 * i:512 * i + 512].rearrange("(j p) n -> p j n", p=P))]
        for i in range(12):
            c[f"ad{i}"] = cols(A["ada_w_2"][i // 6], 512 * (i % 6), 512)
        c["pos"] = [put(0, 512, A["k_pos"].rearrange("(j p) n -> p j n", p=P))]
        for i in range(4):
            c[f"ev{i}"] = cols(A["even_w_in_2"][0], 512 * i, 512)
        c["fch"] = [(lambda s: s[:, 0:256], A["k_dftc"])]
        for e in range(2):
            c["fch"].append((lambda s, e=e: s[64 * e:64 * e + 64, 256:512].rearrange("p (i d) -> p i d", i=2)
                             [:, :, 64 * e:64 * e + 64],
                             A["fnet_w_2"][0].rearrange("(i e) c d -> e c i d", e=2)[e]))
        c["dft"] = [(lambda s: s.rearrange("p (t w n) -> p t w n", t=TT, w=2),
                     A["k_dft"].rearrange("(t p) w n -> p t w n", p=P))]
        c["wbuf"], c["none"], c["sbuf"] = [], [], []
        for name, lo, hi in (("Ta", 0, 32), ("Tb", 32, GROUPS)):
            c[name] = [(lambda s, tau=tau, lo=lo, hi=hi: s[16 * tau:16 * tau + 16, 0:P * (hi - lo)]
                        .rearrange("h (g n) -> h g n", n=P),
                        k_dram[:, lo:hi, tau:tau + CH, :].rearrange("h g t n -> h g (t n)")) for tau in range(CH)]
        for i in range(2):
            c[f"glu{i}"] = [(lambda s: s[:, 0:2304].rearrange("p (j n) -> p j n", j=6),
                             A["s5_glu_w_2"][0].rearrange("(j p) n -> p j n", p=P)[:, :, 384 * i:384 * i + 384])]
            c[f"eo{i}"] = cols(A["even_w_out_2"][0], 512 * i, 512)
            c[f"oo{i}"] = cols(A["odd_w_out_2"][0], 512 * i, 512)
        for i in range(6):
            c[f"od{i}"] = cols(A["odd_w_in_2"][0], 512 * i, 512)
        c["pw"] = [(lambda s: s[:, 0:512].rearrange("p (g d) -> p g d", g=4), A["pool_w_2"][0].rearrange("g c d -> c g d"))]
        return c

    sources = chunk_sources()
    chunk_at = {n: i for i, n in enumerate(CHUNKS)}
    landed, so_far = [], [0] * SLOTS
    for i, n in enumerate(CHUNKS):
        so_far[i % SLOTS] += 16 * len(sources[n])
        landed.append(so_far[i % SLOTS])

    with ExitStack() as ctx:
        def sb(name, shape):
            return ctx.enter_context(nc.sbuf_tensor(name, shape, F32))

        class Sems(dict):
            def __missing__(self, name):
                self[name] = ctx.enter_context(nc.semaphore(name))
                return self[name]

        sem = Sems()
        ident = sb("ident", [P, P])
        ones = sb("ones", [P, P])
        vec = sb("vec", [P, P])
        vecT = sb("vecT", [P, P])
        adab = sb("adab", [48, P])
        adabT = sb("adabT", [P, 48])
        skip = sb("skip", [GROUPS, 16])
        skipT = sb("skipT", [16, GROUPS])
        eps = sb("eps", [P, 1])
        stat = sb("stat", [P, 4, 64])
        std2 = sb("std2", [P, CTX])
        cond = sb("cond", [P, 2, DT])
        part = sb("part", [P, 2, SEQ])
        ada = sb("ada", [P, 2, 24, 2])
        gsc = sb("gsc", [P, 3, DT])
        stepn = sb("stepn", [DK, 2])
        xT = sb("xT", [P, DT, SEQ])
        hT = sb("hT", [P, DT, SEQ])
        std = sb("std", [P, SEQ])
        ring = sb("ring", [P, SLOTS, 4096])
        arena = sb("arena", [P, ARENA])
        bank = [ctx.enter_context(nc.psum_tensor(f"bank{i}", [P, 512], F32)) for i in range(8)]

        def area(at, *shape):
            n = int(np.prod(shape))
            names = "abcd"[:len(shape)]
            v = arena[:, at:at + n]
            if len(shape) == 1:
                return v
            pat = f"p ({' '.join(names)}) -> p {' '.join(names)}"
            return v.rearrange(pat, **dict(zip(names, shape)))

        qnT = area(0, 4, SEQ)
        qiT = area(2048, 4, SEQ)
        olatT = area(0, HEADS, SEQ)
        qlatT = area(4096, HEADS, SEQ)
        xnat = area(4096, TT, D)
        qrT = area(8192, 2, SEQ)
        krT = area(9216, SEQ)
        kiT = area(9728, SEQ)
        qbT = area(10240, 4, SEQ)
        kbT = area(12288, 4, SEQ)
        vnat = area(14336, TT, 512)
        ckvn = area(16384, TT, P)
        ckvT = area(16896, SEQ)
        PTA = area(17408, TT, HEADS, P)
        perm = area(17408, 2, P)
        work = area(21504, 3, SEQ)
        pick = area(23040, 3, SEQ)
        rope = area(24576, 4, SEQ)
        prob = area(24576, 4, SEQ)
        tmp = area(26624, 4, SEQ)
        PTB = area(26624, 2, SEQ)
        dilated = area(28672, SEQ)
        causal = area(29184, P)
        wnat = area(29312, TT, HEADS)
        top8 = area(29344, 8)
        kvg = area(29352, P)
        memn = area(0, 2, D)
        mT = area(2048, DT, MEM)
        kcT = area(4096, DT, MEM)
        vcn = area(6144, 2, D)
        qcT = area(8192, DT, SEQ)
        cprob = area(12288, 4, MEM)
        CPT = area(13312, 2, 2, SEQ)
        uT = area(0, 2, 4, SEQ)
        pwn = area(4096, 20, P)[0:DK]
        cn = area(6656, 12, P)
        kt = area(8192, GROUPS, 16)
        k0 = area(8960, GROUPS, 16)
        K = area(9728, 2, 768)
        bin_ = area(11264, 2, DK, 16)
        tmpn = area(11264, 16, P)
        G = area(13360, 2, 2, 8, P)
        ctxn = area(17456, 2, D)
        hcT = area(17456, DT, CTX)
        ctxT = area(19504, DT, CTX)
        cb = area(21552, DK, 2, 32)
        g1 = area(24624, 8, 8, 16)
        pwT = area(25664, 20, DK)
        bbar = area(26624, 2, DK, 16)
        cc = area(28160, 2, DK, 16)
        uP = area(0, 6, CH, NCH)
        U = area(4656, GROUPS, NCH)
        zT = area(9264, DT, SEQ)
        CA = G
        g2 = area(22112, 8, 8, 16)
        ubT = area(23136, 2, SEQ)
        m8 = area(24160, 2, 2, 2, PAIRS)
        V_AT = (0, 17456)
        VC = NCH + 1
        Vf, Vb = [area(at, 2, PAIRS, VC) for at in V_AT]
        hflat = hT[:, :, :].rearrange("p a b -> p (a b)")
        pq = ring[:, chunk_at["fch"] % SLOTS, 512:2560].rearrange("p (t i n) -> p t i n", t=TT, i=2)
        ftT = ring[:, chunk_at["fch"] % SLOTS, 2560:3584].rearrange("p (i n) -> p i n", i=2)
        Y = hflat[:, 0:3072].rearrange("p (g n) -> p g n", g=GROUPS)
        yP = area(4656, 6, SEQ)
        pairS = ring[:, chunk_at["sbuf"] % SLOTS, :].rearrange("p (r d c k e n) -> p r d c k e n", r=2, d=2, c=2, k=4, e=2)
        yg = area(17456, 6, SEQ)
        sg = area(13360, 2, SEQ)
        rc = area(0, 4, SEQ)
        gb = area(2048, 4, SEQ + 16)
        sw = area(4160, 2, SEQ + 16)
        pooled = area(5216, 4, SEQ)
        cgT = area(7264, 4, SEQ)
        cx = area(9312, 4, SEQ + 2)
        bgT = area(11368, 4, SEQ)
        zoT = area(13416, DT, SEQ)
        yT = area(17512, DT, SEQ)
        onat = area(21608, TT, D)

        def bank_free(eng, stage, i=0):
            n = T.index[stage, i]
            if n >= RING:
                eng.wait_ge(sem["taken_by_" + T.owner[n - RING]], T.count[n - RING])
            return bank[n % RING]

        def filled(eng, stage, i=0):
            n = T.index[stage, i]
            eng.wait_ge(sem["tile_filled"], n + 1)
            return bank[n % RING]

        def taken(eng, stage, i=0):
            n = T.index[stage, i]
            eng.wait_ge(sem["taken_by_" + T.owner[n]], T.count[n])

        def chunk_used(eng, name):
            if name == "pos":
                eng.wait_ge(sem["pos_added"], DT)
            elif name in ("Ta", "Tb"):
                eng.wait_ge(sem["chunk_products_done"], 1)
            elif name[:2] == "ad":
                eng.wait_ge(sem["ada_summed"], int(name[2:]) + 1)
            else:
                eng.wait_ge(sem["tile_filled"], T.index[LAST_TILE[name]] + 1)

        def weights(eng, name):
            n = chunk_at[name]
            eng.wait_ge(sem[f"slot{n % SLOTS}_landed"], landed[n])
            return ring[:, n % SLOTS, :]

        def roped(eng, n):
            stage, i = ROPES[n]
            taken(eng, stage + "p", i)

        def g(name, j=0):
            return vecT[:, VEC[name] + j:VEC[name] + j + 1]

        def powers(d, lo, n, m):
            v = pwT[:, 2 * lo:2 * lo + 16, PAIRS * d + m:PAIRS * d + m + n].rearrange("p (j c) k -> p c k j", c=2)
            if d == 0:
                v = v[:, :, :, ::-1]
            return [v[:, c, :, :].unsqueeze(3).broadcast_to([P, n, 8, 16]) for c in range(2)]

        def make_ca(eng, then, bl, temp, name, n):
            for d in range(2):
                pr, pi = powers(d, 1, 4, 4 * bl)
                c_r, c_i = [cc[:, c, PAIRS * d + 4 * bl:PAIRS * d + 4 * bl + 4, :].unsqueeze(2)
                            .broadcast_to([P, 4, 8, 16]) for c in range(2)]
                re, im = [CA[:, bl % 2, c, 4 * d:4 * d + 4, :].rearrange("p k (j h) -> p k j h", h=16) for c in range(2)]
                t_r, t_i = temp[:, 0:4], temp[:, 4:8]
                eng.tensor_tensor(out=t_r, in0=pr, in1=c_r, op=ALU.mult)
                eng.tensor_tensor(out=re, in0=pi, in1=c_i, op=ALU.mult)
                eng.tensor_tensor(out=t_i, in0=pr, in1=c_i, op=ALU.mult)
                then(eng.tensor_tensor(out=im, in0=pi, in1=c_r, op=ALU.mult))
                eng.tensor_tensor(out=re, in0=t_r, in1=re, op=ALU.subtract).then_inc(sem[name], 1)
                then(eng.tensor_tensor(out=im, in0=t_i, in1=im, op=ALU.add))
                eng.tensor_scalar(im, im, -1.0, None, ALU.mult).then_inc(sem[name], 1)
                eng.wait_ge(sem[name], 2 * (n - 1 + d))

        block = ctx.enter_context(nc.Block())
        us = units()

        def u_back(eng, i):
            eng.wait_ge(sem["k_out"], 16 * (2 * CH - 1))
            eng.wait_ge(sem[f"u_out{i}"], 16)
            for tau in range(CH):
                eng.dma_start(U[16 * tau:16 * tau + 16, 8 * i:8 * i + 8, :],
                              u_dram[P * i:P * i + P, tau, :].rearrange("(g h) c -> h g c", h=16))\
                    .then_inc(sem[f"u_in{i}"], 16)

        def y_back(sp, i):
            sp.wait_ge(sem[f"ys_out{i}"], 16)
            for k in range(CH):
                sp.dma_start(yP[16 * k:16 * k + 16, i, :].rearrange("h (t c) -> h t c", t=CH),
                             y_dram[i].rearrange("(t h) (g c) -> g h t c", t=CH, g=8)[k]).then_inc(sem[f"ys_in{i}"], 16)

        @block.sync
        def _(sp):

            sp.dma_start(ident[:, :], A["k_ident"]).then_inc(sem["ident_in"], 16)
            rows = 0
            for name, r in VEC_ROWS:
                src = A[name]
                flat = src.rearrange({1: "(r n) -> r n", 2: "a (r n) -> (a r) n",
                                      3: "a b (r n) -> (a b r) n"}[len(src.shape)], n=P)
                sp.dma_start(vec[rows:rows + r, :], flat).then_inc(sem["vec_in"], 16)
                rows += r
            sp.dma_start(adab[:, :], A["ada_b_2"].rearrange("a (r n) -> (a r) n", n=P)).then_inc(sem["vec_in"], 16)
            sp.dma_start(skip[:, :], A["s5_d_2"][0]).then_inc(sem["vec_in"], 16)
            sp.dma_start(perm, A["k_perm"]).then_inc(sem["tables_in"], 16)
            sp.dma_start(rope, A["k_rope"]).then_inc(sem["tables_in"], 16)
            sp.dma_start(dilated, A["k_dilated"]).then_inc(sem["tables_in"], 16)
            sp.dma_start(causal, A["k_causal"]).then_inc(sem["tables_in"], 16)
            sp.dma_start(kvg, A["kv_norm_g"].broadcast_to([P, P])).then_inc(sem["tables_in"], 16)
            for n, name in enumerate(CHUNKS):
                if name == "none":
                    continue
                if n >= SLOTS:
                    chunk_used(sp, occupant(n))
                if name == "kc0":
                    taken(sp, "oa", 3)
                    sp.dma_start(memn, A["mem"][0].rearrange("(t p) n -> p t n", p=P)).then_inc(sem["mem_in"], 16)
                if name == "ad0":
                    taken(sp, "oc", 7)
                    sp.dma_start(ctxn, A["ctx_2"][0].rearrange("(t p) n -> p t n", p=P)).then_inc(sem["ctx_in"], 16)
                    for e in range(2):
                        for c, b in enumerate(("s5_b_re_2", "s5_b_im_2")):
                            sp.dma_start(bin_[64 * e:64 * e + 64, c, :, :],
                                         A[b][0].rearrange("d (k e) p h -> e p (d k) h", e=2)[e]).then_inc(sem["b_in"], 16)
                    for c, b in enumerate(("s5_lam_re_2", "s5_lam_im_2")):
                        sp.dma_start(pwn[:, 18 + c, :], A[b][0].rearrange("d (k e) p -> (d k) (e p)", e=2))\
                            .then_inc(sem["lam_in"], 16)
                    for c, b in enumerate(("s5_c_re_2", "s5_c_im_2")):
                        for i in range(12):
                            d, kb, e = i // 6, i // 2 % 3, i % 2
                            sp.dma_start(cn[:, 6 * c + 3 * d + kb, 64 * e:64 * e + 64],
                                         A[b][0, d, 16 * kb:16 * kb + 16].rearrange("(k e) h p -> e k h p", e=2)[e])\
                                .then_inc(sem["c_in"], 16)
                    sp.dma_start(stepn[:, :], A["s5_log_step_2"][0].rearrange("d (k e) -> (d k) e", e=2))\
                        .then_inc(sem["lam_in"], 16)
                if name == "Ta":
                    sp.wait_ge(sem["k_out"], 16 * (2 * CH - 1))
                if name == "od0":
                    taken(sp, "eo", 7)
                    sp.dma_start(rc, A["k_rcount"].rearrange("(a w) n -> a w n", a=1).broadcast_to([P, 4, SEQ]))\
                        .then_inc(sem["rc_in"], 16)
                for view, src in sources[name]:
                    sp.dma_start(view(ring[:, n % SLOTS, :]), src).then_inc(sem[f"slot{n % SLOTS}_landed"], 16)
                if name == "fch":
                    for i in range(6):
                        taken(sp, "uc", i)
                        taken(sp, "ul", i)
                        sp.dma_start(u_dram[P * i:P * i + P], uP[:, i, :, :]).then_inc(sem[f"u_out{i}"], 16)
                        if i % 2:
                            u_back(sp, i - 1)
                if name == "glu1":
                    for i in range(6):
                        taken(sp, "ys", i)
                        sp.dma_start(y_dram[i], Y[:, 8 * i:8 * i + 8, :]).then_inc(sem[f"ys_out{i}"], 16)
                        if i % 2:
                            y_back(sp, i)
            for t in range(TT):
                taken(sp, "yout", 2 * t + 1)
                sp.dma_start(out[0, P * t:P * t + P, :], onat[:, t, :]).then_inc(sem["y_out"], 16)
            sp.wait_ge(sem["y_out"], 16 * TT)

        @block.gpsimd
        def _(pool):
            pool.memset(ones[:, :], 1.0).then_inc(sem["ones_set"], 1)
            pool.memset(eps[:, :], EPS).then_inc(sem["ones_set"], 1)
            taken(pool, "oc", 7)
            pool.memset(cb, 0.0).then_inc(sem["cb_zero"], 1)
            taken(pool, ("kk", 5))
            pool.dma_start(kt[0:16], K[112:128, 0, :].rearrange("p (g h) -> p g h", h=16)).then_inc(sem["k_moved"], 16)
            for i in range(CH - 1):
                for d in range(2):
                    rows = 16 * (i + d)
                    pool.dma_start(k_dram[:, :, CH * d + i, :],
                                   K[rows:rows + 16, d, :].rearrange("h (g n) -> h g n", n=16)).then_inc(sem["k_out"], 16)
            pool.wait_ge(sem["k0_ready"], 1)
            pool.dma_start(k_dram[:, :, CH - 1, :], k0[0:16]).then_inc(sem["k_out"], 16)
            for i in (1, 3, 5):
                u_back(pool, i)
            pool_steps = [0]

            def then(ins):
                pool_steps[0] += 1
                ins.then_inc(sem["pool_step"], 1)
                pool.wait_ge(sem["pool_step"], pool_steps[0])

            filled(pool, ("wt", 23))
            for bl in range(2):
                make_ca(pool, then, bl, g2, "ca_by_pool", 2 * bl + 2)
            chunk_used(pool, occupant(chunk_at["sbuf"]))
            pool.memset(ring[:, chunk_at["sbuf"] % SLOTS, :], 0.0).then_inc(sem["states_zero"], 1)
            for i in (0, 2, 4):
                y_back(pool, i)

        @block.tensor
        def _(pe):
            def mm(o, l, r, first, last):
                return pe.matmul(o, l, r, start=first, stop=last)

            def linear(stage, i, w, col, m, rhs, ready=None, kt=DT, stride=512):
                ps = bank_free(pe, stage, i)
                wv = w.rearrange("p (j n) -> p j n", n=stride)
                for j in range(kt):
                    if ready is not None:
                        ready(j)
                    ins = mm(ps[0:m, :], wv[:, j, col:col + m], rhs(j), j == 0, j == kt - 1)
                return ins.then_inc(sem["tile_filled"], 1)

            def natural(stage, i, w, n, lhs, ready=None):
                ps = bank_free(pe, stage, i)
                wv = w.rearrange("p (j n) -> p j n", n=512)
                for j in range(DT):
                    if ready is not None:
                        ready(j)
                    ins = mm(ps[:, 0:n], lhs(j), wv[:, j, 0:n], j == 0, j == DT - 1)
                return ins.then_inc(sem["tile_filled"], 1)

            def ssq(name):
                ps = bank_free(pe, name + "_ssq")
                pe.wait_ge(sem["ones_set"], 2)
                for j in range(DT):
                    pe.wait_ge(sem[name + "_squares"], j + 1)
                    ins = mm(ps[:, :], ones[:, :], hT[:, j, :], j == 0, j == DT - 1)
                ins.then_inc(sem["tile_filled"], 1)

            def normed(name):
                return lambda j: pe.wait_ge(sem[name + "_normed"], j + 1)

            def h(j):
                return hT[:, j, :]

            pe.wait_ge(sem["ident_in"], 16)
            pe.wait_ge(sem["vec_in"], 16 * (len(VEC_ROWS) + 2))
            for i, (rows, n) in enumerate(((vec, VEC_N), (adab, 48), (skip, GROUPS))):
                ps = bank_free(pe, "vec", i)
                pe.transpose(ps[0:rows.shape[1], 0:n], rows[0:n, :], ident[0:n, 0:n]).then_inc(sem["tile_filled"], 1)
            pe.wait_ge(sem["x_in"], 16 * TT)
            for j in range(DT):
                ps = bank_free(pe, "xin", j)
                for t in range(TT):
                    ins = pe.transpose(ps[:, P * t:P * t + P], xnat[:, t, P * j:P * j + P], ident[:, :])
                ins.then_inc(sem["tile_filled"], 1)
            ssq("mix")
            w = weights(pe, "kv")
            for t in range(TT):
                natural("ckv", t, w, 136, lambda j: hT[:, j, P * t:P * t + P], normed("mix"))
            for i in range(2):
                last = linear("kir", i, w, 136 + 128 * i, P, h)
            pe.wait_ge(sem["tables_in"], 16 * 5)

            def swap(stage, i, raw, which, done):
                taken(pe, stage, i)
                ps = bank_free(pe, stage + "p", i)
                mm(ps[:, :], perm[:, which, :], raw, True, True).then_inc(sem["tile_filled"], 1)

            for i in range(2):
                swap("kir", i, tmp[:, i, :], i, 0)
            pe.wait_ge(sem["ckv_normed"], TT)
            ps = bank_free(pe, "ckvT")
            for t in range(TT):
                ins = pe.transpose(ps[:, P * t:P * t + P], ckvn[:, t, :], ident[:, :])
            ins.then_inc(sem["tile_filled"], 1)

            def rope_proj(stage, n, which, base):
                w = weights(pe, stage)
                for i in range(n + 1):
                    if i < n:
                        linear(stage, i, w, 128 * i, P, h)
                    if i >= 1:
                        swap(stage, i - 1, tmp[:, (base + i - 1) % 4, :], which, 0)

            rope_proj("qi", 4, 0, 2)
            for n in range(24):
                b, hd = 1 + n // 8, n % 8
                if n == 0:
                    taken(pe, "qip", 3)
                    taken(pe, "kirp", 1)
                ps = bank_free(pe, "idx", n)
                rows = slice(64 * (hd % 2), 64 * (hd % 2) + 64)
                mm(ps[:, 0:P * (b + 1)], qiT[rows, hd // 2, P * b:P * b + P], kiT[rows, 0:P * (b + 1)], True, True)\
                    .then_inc(sem["tile_filled"], 1)
            rope_proj("qr", 2, 1, 6)
            w = weights(pe, "qn")
            for i in range(4):
                linear("qn", i, w, 128 * i, P, h)
            rope_proj("qb", 4, 0, 8)
            rope_proj("kb", 4, 0, 12)
            w = weights(pe, "vb")
            for t in range(TT):
                natural("vb", t, w, 512, lambda j: hT[:, j, P * t:P * t + P])
            w = weights(pe, "mla")
            for hd in range(HEADS):
                taken(pe, "qn", hd // 2)
                ps = bank_free(pe, "qlat", hd)
                rows = slice(64 * (hd % 2), 64 * (hd % 2) + 64)
                mm(ps[:, :], w[rows, 128 * (hd // 2):128 * (hd // 2) + 128], qnT[rows, hd // 2, :], True, True)\
                    .then_inc(sem["tile_filled"], 1)

            taken(pe, "kbp", 3)
            taken(pe, "vb", 3)
            for s in range(len(us) + LAG_V):
                if s < len(us):
                    kind, b, hd = us[s]
                    keys = P * (b + 1)
                    ps = bank_free(pe, ("S", s))
                    if kind == "B":
                        rows = slice(64 * (hd % 2), 64 * (hd % 2) + 64)
                        mm(ps[:, 0:keys], qbT[rows, hd // 2, P * b:P * b + P], kbT[rows, hd // 2, 0:keys], True, True)\
                            .then_inc(sem["tile_filled"], 1)
                    else:
                        if b == 0:
                            taken(pe, "qlat", hd)
                        rows = slice(32 * (hd % 4), 32 * (hd % 4) + 32)
                        mm(ps[:, 0:keys], qlatT[:, hd, P * b:P * b + P], ckvT[:, 0:keys], True, False)
                        pe.matmul(ps[:, 0:keys], qrT[rows, hd // 4, P * b:P * b + P], krT[rows, 0:keys], start=False,
                                  stop=True, tile_position=(32 * (hd % 4), 0)).then_inc(sem["tile_filled"], 1)
                u = s - LAG_T
                if 0 <= u < len(us):
                    pe.wait_ge(sem["prob_scaled"], u + 1)
                    ps = bank_free(pe, ("T", u))
                    for kb in range(us[u][1] + 1):
                        ins = pe.transpose(ps[:, P * kb:P * kb + P], prob[:, u % 4, P * kb:P * kb + P], ident[:, :])
                    ins.then_inc(sem["tile_filled"], 1)
                u = s - LAG_V
                if u < 0:
                    continue
                kind, b, hd = us[u]
                if kind == "B":
                    taken(pe, ("T", u))
                    if hd == 0 and b >= 2:
                        pe.wait_ge(sem["dilated_taken"], b - 1)
                    rows = slice(64 * (hd % 2), 64 * (hd % 2) + 64)
                    for kb in range(b + 1):
                        ins = mm(bank[6 + b % 2][rows, P * (hd // 2):P * (hd // 2) + P],
                                 vnat[:, kb, 64 * hd:64 * hd + 64], PTB[:, u % 2, P * kb:P * kb + P], kb == 0, kb == b)
                    ins.then_inc(sem["dilated_out"], 1)
                elif hd % 4 == 3:
                    n = 2 * b + hd // 4
                    taken(pe, ("T", u))
                    if n < 2:
                        pe.wait_ge(sem["dilated_taken"], 3 + n)
                    else:
                        pe.wait_ge(sem["latent_taken"], n - 1)
                    for kb in range(b + 1):
                        ins = mm(bank[6 + n % 2][:, :], ckvn[:, kb, :],
                                 PTA[:, kb, hd - 3:hd + 1, :], kb == 0, kb == b)
                    ins.then_inc(sem["latent_out"], 1)
            pe.wait_ge(sem["latent_taken"], 8)
            for i in range(4):
                ps = bank_free(pe, "oa", i)
                for e in range(2):
                    ins = mm(ps[64 * e:64 * e + 64, :], w[:, 512 + 64 * (2 * i + e):576 + 64 * (2 * i + e)],
                             olatT[:, 2 * i + e, :], True, True)
                ins.then_inc(sem["tile_filled"], 1)
            taken(pe, "oa", 3)

            def proj(stage, names, rhs, ready=None):
                for i in range(DT):
                    if i % 4 == 0:
                        w = weights(pe, names[i // 4])
                    linear(stage, i, w, 128 * (i % 4), P, rhs, ready if i == 0 else None)

            proj("out", ("out0", "out1"), h)
            pe.wait_ge(sem["mem_scaled"], 2)
            for j in range(DT):
                ps = bank_free(pe, "memT", j)
                for t in range(2):
                    ins = pe.transpose(ps[:, P * t:P * t + P], memn[:, t, P * j:P * j + P], ident[:, :])
                ins.then_inc(sem["tile_filled"], 1)
            for i in range(DT):
                if i % 4 == 0:
                    w = weights(pe, f"kc{i // 4}")
                ps = bank_free(pe, "kc", i)
                wv = w.rearrange("p (j n) -> p j n", n=512)
                for j in range(DT):
                    taken(pe, "memT", j)
                    ins = mm(ps[:, 0:MEM], wv[:, j, 128 * (i % 4):128 * (i % 4) + 128], mT[:, j, :], j == 0, j == DT - 1)
                ins.then_inc(sem["tile_filled"], 1)
            for c in range(2):
                w = weights(pe, f"vc{c}")
                for t in range(2):
                    natural("vc", 2 * c + t, w, 512, lambda j: mT[:, j, P * t:P * t + P])
            ssq("cross")
            proj("qc", ("qc0", "qc1"), h, normed("cross"))
            for s in range(16 + 3):
                if s < 16:
                    hd, b = s // 4, s % 4
                    taken(pe, "qc", 2 * hd + 1)
                    taken(pe, "kc", 7)
                    ps = bank_free(pe, ("CS", s))
                    for e in range(2):
                        ins = mm(ps[:, 0:MEM], qcT[:, 2 * hd + e, P * b:P * b + P], kcT[:, 2 * hd + e, :], e == 0, e == 1)
                    ins.then_inc(sem["tile_filled"], 1)
                u = s - 2
                if 0 <= u < 16:
                    pe.wait_ge(sem["cross_scaled"], u + 1)
                    ps = bank_free(pe, ("CT", u))
                    for kb in range(2):
                        ins = pe.transpose(ps[:, P * kb:P * kb + P], cprob[:, u % 4, P * kb:P * kb + P], ident[:, :])
                    ins.then_inc(sem["tile_filled"], 1)
                u = s - 3
                if u >= 0 and u % 4 == 3:
                    hd = u // 4
                    taken(pe, ("CT", u))
                    if hd >= 1:
                        pe.wait_ge(sem["cross_taken"], 2 * hd)
                    for e in range(2):
                        for kb in range(2):
                            ins = mm(bank[6 + e][:, :], vcn[:, kb, 256 * hd + 128 * e:256 * hd + 128 * e + 128],
                                     CPT[:, hd % 2, kb, :], kb == 0, kb == 1)
                        ins.then_inc(sem["cross_out"], 1)
            pe.wait_ge(sem["cross_taken"], 8)
            proj("oc", ("oc0", "oc1"), h)
            ssq("mlp")
            def ada_tile(n):
                ps = bank_free(pe, ("ada", n))
                conds = 2 if n < 6 else 1
                pe.wait_ge(sem["ada_summed"], n + 1)
                for q in range(4):
                    for c in range(conds):
                        ins = mm(ps[:, 2 * q + c:2 * q + c + 1], part[:, c, P * q:P * q + P], ones[:, 0:1], True, True)
                ins.then_inc(sem["tile_filled"], 1)

            def down(i):
                w = weights(pe, f"dn{i}").rearrange("p (j n) -> p j n", n=D)
                for m in range(DT):
                    ps = bank_free(pe, ("down", 8 * i + m))
                    for j in range(4):
                        if m == 0:
                            pe.wait_ge(sem["relu_squared"], 4 * i + j + 1)
                        ins = mm(ps[:, :], w[:, j, P * m:P * m + P], uT[:, i % 2, j, :], j == 0, j == 3)
                    ins.then_inc(sem["tile_filled"], 1)

            for i in range(8):
                w = weights(pe, f"up{i}")
                for j in range(4):
                    linear(("up", 4 * i + j), 0, w, 128 * j, P, h, normed("mlp"))
                ada_tile(ADA_AFTER_UP[i])
                if i:
                    down(i - 1)
                if i in ADA_AFTER_DOWN:
                    ada_tile(ADA_AFTER_DOWN[i])
                if i == 1:
                    pe.wait_ge(sem["c_in"], 16 * 24)
                    for q in range(3):
                        ps = bank_free(pe, "cT", q)
                        for k in range(4):
                            ins = pe.transpose(ps[:, P * k:P * k + P], cn[:, 4 * q + k, :], ident[:, :])
                        ins.then_inc(sem["tile_filled"], 1)
                    pe.wait_ge(sem["poles_ready"], 1)
                    for q in range(2):
                        ps = bank_free(pe, "lamT", q)
                        for k in range(10):
                            ins = pe.transpose(ps[:, DK * k:DK * k + DK], pwn[:, 10 * q + k, :], ident[0:DK, 0:DK])
                        ins.then_inc(sem["tile_filled"], 1)
                if i >= 2:
                    bl = i - 2
                    pe.wait_ge(sem["cb_ready"], 4)
                    pe.wait_ge(sem["g_ready"], bl + 1)
                    ps = bank_free(pe, ("kk", bl))
                    for k in range(8):
                        for c in range(2):
                            ins = mm(ps[:, 32 * k:32 * k + 32], G[:, bl % 2, c, k, :], cb[:, 8 * bl + k, c, :],
                                     c == 0, c == 1)
                    ins.then_inc(sem["tile_filled"], 1)
                if i == 5:
                    pe.wait_ge(sem["ctx_in"], 16)
                    for q in range(4):
                        ps = bank_free(pe, "ctxT", q)
                        for k in range(4):
                            j, t = 2 * q + k // 2, k % 2
                            ins = pe.transpose(ps[:, P * k:P * k + P], ctxn[:, t, P * j:P * j + P], ident[:, :])
                        ins.then_inc(sem["tile_filled"], 1)
                    ps = bank_free(pe, "ctx_ssq")
                    for j in range(DT):
                        pe.wait_ge(sem["ctx_squares"], j + 1)
                        ins = mm(ps[:, 0:CTX], ones[:, :], hcT[:, j, :], j == 0, j == DT - 1)
                    ins.then_inc(sem["tile_filled"], 1)
            down(7)

            ssq("fin")
            for i in range(6):
                w = weights(pe, f"ev{i // 4}").rearrange("p (j n) -> p j n", n=512)
                ps = bank_free(pe, "uc", i)
                for j in range(DT):
                    pe.wait_ge(sem["ctx_normed"], j + 1)
                    ins = mm(ps[:, 0:CTX], w[:, j, 128 * (i % 4):128 * (i % 4) + 128], hcT[:, j, :], j == 0, j == DT - 1)
                ins.then_inc(sem["tile_filled"], 1)
            ssq("ev")
            for i in range(8):
                stage, k = ("ul", i) if i < 6 else ("ub", i - 6)
                linear(stage, k, weights(pe, f"ev{i // 4}"), 128 * (i % 4), P, h, normed("ev"))
            W = weights(pe, "wbuf").rearrange("p (r k c n) -> p r k c n", r=2, k=8, c=2)
            for bl in range(7):
                if bl < 6:
                    pe.wait_ge(sem["g_ready"], 7 + bl)
                    for q in range(4):
                        ps = bank_free(pe, ("wt", 4 * bl + q))
                        for i in range(4):
                            k, c = 2 * q + i // 2, i % 2
                            ins = pe.transpose(ps[:, P * i:P * i + P], G[:, bl % 2, c, k, :], ident[:, :])
                        ins.then_inc(sem["tile_filled"], 1)
                if bl >= 1:
                    for i in range(2):
                        pe.wait_ge(sem[f"u_in{2 * ((bl - 1) % 3) + i}"], 16 * CH)
                    for q in range(4):
                        taken(pe, ("wt", 4 * (bl - 1) + q))
                        ps = bank_free(pe, ("v", 4 * (bl - 1) + q))
                        for k in (2 * q, 2 * q + 1):
                            pair = (8 * (bl - 1) + k) % PAIRS
                            for c in range(2):
                                for e in range(2):
                                    at = 192 * (k % 2) + 96 * c
                                    ins = mm(ps[64 * e:64 * e + 64, at:at + NCH], W[:, (bl - 1) % 2, k, c, 64 * e:64 * e + 64],
                                             U[:, 2 * pair + e, :], True, True)
                        ins.then_inc(sem["tile_filled"], 1)
            w = weights(pe, "fch")
            pe.wait_ge(sem["fch_zero"], 1)
            for t in range(TT):
                ps = bank_free(pe, "pq", t)
                for i in range(2):
                    taken(pe, "ub", i)
                    ins = mm(ps[:, 256 * i:256 * i + 256], ubT[:, i, P * t:P * t + P], w[:, 0:256], True, True)
                ins.then_inc(sem["tile_filled"], 1)
            d = weights(pe, "dft").rearrange("p (t w n) -> p t w n", t=TT, w=2)
            for i in range(2):
                ps = bank_free(pe, "ft", i)
                for t in range(TT):
                    taken(pe, "pq", t)
                    for c in range(2):
                        ins = mm(ps[:, :], pq[:, t, i, P * c:P * c + P], d[:, t, c, :], t == 0 and c == 0,
                                 t == TT - 1 and c == 1)
                ins.then_inc(sem["tile_filled"], 1)
            for i in range(2):
                taken(pe, "ft", i)
                ps = bank_free(pe, "yb", i)
                mm(ps[:, :], w[:, 256 + P * i:256 + P * i + P], ftT[:, i, :], True, True).then_inc(sem["tile_filled"], 1)
            for i in range(DT):
                linear("z", i, weights(pe, f"ev{2 + i // 4}"), 128 * (i % 4), P, h)
            span = ring[:, 0:2, :].rearrange("p s n -> p (s n)")[:, 0:CH * 768].rearrange("p (g n) -> p g n", g=GROUPS)
            for bl in range(6):
                ps = bank_free(pe, "ys", bl)
                weights(pe, "Ta" if bl < 4 else "Tb")
                for k in range(8):
                    ins = mm(ps[:, NLAT * k:NLAT * k + NLAT], span[:, 8 * bl + k, :], U[:, 8 * bl + k, NCTX:], k == 0, False)
            ins.then_inc(sem["chunk_products_done"], 1)
            for bl in range(6):
                ps = bank_free(pe, "ys", bl)
                pe.wait_ge(sem["states_placed"], 4 * (bl + 1))
                if bl < 2:
                    pe.wait_ge(sem["ca_by_pool"], 4 * (bl + 1))
                else:
                    pe.wait_ge(sem["ca_by_dve"], 4 * (bl - 1))
                for k in range(4):
                    for d in range(2):
                        for c in range(2):
                            ins = pe.matmul(ps[:, P * k:P * k + P], CA[:, bl % 2, c, 4 * d + k, :],
                                            pairS[:, bl % 2, d, c, k, :, :].rearrange("p e n -> p (e n)"),
                                            start=False, stop=(k == 3 and d == 1 and c == 1))
                ins.then_inc(sem["tile_filled"], 1)
            for i in range(6):
                w = weights(pe, f"glu{i // 3}")
                linear("glu", i, w[:, 0:2304], 128 * (i % 3), P, lambda j: yg[:, j, :],
                       lambda j: pe.wait_ge(sem["gelu_done"], j + 1), kt=6, stride=384)

            def gated(j):
                if j < 6:
                    pe.wait_ge(sem["glu_gated"], j + 1)
                else:
                    pe.wait_ge(sem["fnet_gated"], j - 5)

            proj("eo", ("eo0", "eo1"), lambda j: hT[:, j, :] if j < 6 else zT[:, j, :], gated)
            ssq("od")
            for n, (stage, k) in enumerate((("pool", 4), ("cg", 4), ("xp", 4), ("bg", 4), ("zo", 8))):
                for i in range(k):
                    linear(stage, i, weights(pe, f"od{n + i // 4}"), 128 * (i % 4), P, h, normed("od"))
            w = weights(pe, "pw")
            for i in range(4):
                pe.wait_ge(sem["pooled"], i + 1)
                ps = bank_free(pe, "pm", i)
                mm(ps[:, :], w[:, P * i:P * i + P], pooled[:, i, :], True, True).then_inc(sem["tile_filled"], 1)
            proj("oo", ("oo0", "oo1"), lambda j: yT[:, j, :], lambda j: taken(pe, "pm", j) if j < 4 else pe.wait_ge(sem["odd_gated"], j - 3))
            ssq("end")
            for q in range(DT):
                t, half = q // 2, q % 2
                ps = bank_free(pe, "yout", q)
                for i in range(4):
                    j = 4 * half + i
                    pe.wait_ge(sem["end_normed"], j + 1)
                    ins = pe.transpose(ps[:, P * i:P * i + P], hT[:, j, P * t:P * t + P], ident[:, :])
                ins.then_inc(sem["tile_filled"], 1)

        @block.scalar
        def _(act):
            TA = sem["taken_by_act"]

            def squares(name, ready):
                for j in range(DT):
                    ready(j)
                    act.activation(hT[:, j, :], xT[:, j, :], ACT.Square).then_inc(sem[name + "_squares"], 1)

            def root(name):
                ps = filled(act, name + "_ssq")
                act.activation(std[:, :], ps[:, :], ACT.Sqrt, scale=1.0 / D, bias=eps[:, 0:1]).then_inc(TA, 1)

            def copy(stage, i, dst, scale=1.0, m=P, n=512):
                ps = filled(act, stage, i)
                act.activation(dst, ps[0:m, 0:n], ACT.Copy, scale=scale).then_inc(TA, 1)

            for t in range(TT):
                act.dma_start(xnat[:, t, :], A["x"][0, P * t:P * t + P, :]).then_inc(sem["x_in"], 16)
            copy("vec", 0, vecT[:, 0:VEC_N], n=VEC_N)
            copy("vec", 1, adabT[:, :], n=48)
            copy("vec", 2, skipT[:, :], m=16, n=GROUPS)
            for j in range(DT):
                copy("xin", j, xT[:, j, :])
            act.wait_ge(sem["ones_set"], 2)
            squares("mix", lambda j: taken(act, "xin", j))
            root("mix")
            for t in range(TT):
                ps = filled(act, "ckv", t)
                act.activation(wnat[:, t, :], ps[:, 128:136], ACT.Copy, scale=float(8 ** -0.5 * 64 ** -0.5))
                act.activation(ckvn[:, t, :], ps[:, 0:128], ACT.Copy).then_inc(TA, 1)
            for i in range(2):
                copy("kir", i, tmp[:, i, :])
            for t in range(TT):
                taken(act, "ckv", t)
                if t >= 1:
                    act.wait_ge(sem["ckv_squares"], t)
                act.activation(tmp[:, 3, 0:128], ckvn[:, t, :], ACT.Square, accum_out=stat[:, 0, t:t + 1])\
                    .then_inc(sem["ckv_squares"], 1)
            act.wait_ge(sem["ckv_squares"], TT)
            act.activation(stat[:, 1, 0:TT], stat[:, 0, 0:TT], ACT.Sqrt, scale=1.0 / 128, bias=eps[:, 0:1])\
                .then_inc(sem["ckv_root"], 1)
            copy("ckvT", 0, ckvT)

            def rope_copy(stage, n, base):
                for i in range(n):
                    if base + i >= 4:
                        roped(act, base + i - 4)
                    copy(stage, i, tmp[:, (base + i) % 4, :])

            rope_copy("qi", 4, 2)
            for n in range(24):
                b = 1 + n // 8
                ps = filled(act, "idx", n)
                if n < 4:
                    roped(act, 2 + n)
                else:
                    act.wait_ge(sem["index_added"], n - 3)
                act.activation(tmp[:, n % 4, 0:P * (b + 1)], ps[:, 0:P * (b + 1)], ACT.Relu).then_inc(TA, 1)
            act.wait_ge(sem["index_added"], 24)
            rope_copy("qr", 2, 6)
            for i in range(4):
                copy("qn", i, qnT[:, i, :])
            rope_copy("qb", 4, 8)
            rope_copy("kb", 4, 12)
            for t in range(TT):
                copy("vb", t, vnat[:, t, :])
            for hd in range(HEADS):
                copy("qlat", hd, qlatT[:, hd, :])
            for s in range(len(us) + LAG_V):
                u = s - 1
                if 0 <= u < len(us):
                    kind, b, hd = us[u]
                    keys = P * (b + 1)
                    act.wait_ge(sem["neg_max"], u + 1)
                    act.activation(prob[:, u % 4, 0:keys], prob[:, u % 4, 0:keys], ACT.Exp, bias=stat[:, 1, u:u + 1],
                                   scale=SCALE_A if kind == "A" else SCALE_B,
                                   accum_out=stat[:, 2, u:u + 1]).then_inc(sem["exp_done"], 1)
                u = s - LAG_T
                if 0 <= u < len(us):
                    kind, b, hd = us[u]
                    ps = filled(act, ("T", u))
                    if kind == "B":
                        if u >= 2:
                            act.wait_ge(sem["dilated_out"], u - 1)
                        else:
                            roped(act, 15)
                        dst = PTB[:, u % 2, 0:P * (b + 1)]
                        act.activation(dst, ps[:, 0:P * (b + 1)], ACT.Copy).then_inc(TA, 1)
                    else:
                        if b >= 1:
                            act.wait_ge(sem["latent_out"], 2 * b - 1 + hd // 4)
                        dst = PTA[:, 0:b + 1, hd, :]
                        act.activation(dst, ps[:, 0:P * (b + 1)].rearrange("p (k q) -> p k q", q=P), ACT.Copy)\
                            .then_inc(TA, 1)
            for i in range(4):
                copy("oa", i, hT[:, i, :])
            act.wait_ge(sem["mem_in"], 16)
            taken(act, "oa", 3)
            for t in range(2):
                if t:
                    act.wait_ge(sem["mem_squares"], t)
                act.activation(area(8192, D), memn[:, t, :], ACT.Square, accum_out=stat[:, 0, t:t + 1])\
                    .then_inc(sem["mem_squares"], 1)
            act.wait_ge(sem["mem_squares"], 2)
            act.activation(stat[:, 1, 0:2], stat[:, 0, 0:2], ACT.Sqrt, scale=1.0 / D, bias=eps[:, 0:1])\
                .then_inc(sem["mem_root"], 1)
            act.wait_ge(sem["mem_rstd"], 1)
            for t in range(2):
                act.activation(memn[:, t, :], memn[:, t, :], ACT.Copy, scale=stat[:, 2, t:t + 1])\
                    .then_inc(sem["mem_scaled"], 1)
            filled(act, "out", 7)
            squares("cross", lambda j: taken(act, "out", j))
            for i in range(DT):
                copy("kc", i, kcT[:, i, :], n=MEM)
            for c in range(2):
                for t in range(2):
                    copy("vc", 2 * c + t, vcn[:, t, 512 * c:512 * c + 512])
            root("cross")
            for i in range(DT):
                copy("qc", i, qcT[:, i, :])
            for s in range(16 + 3):
                u = s - 1
                if 0 <= u < 16:
                    act.wait_ge(sem["cross_neg_max"], u + 1)
                    act.activation(cprob[:, u % 4, :], cprob[:, u % 4, :], ACT.Exp, bias=stat[:, 1, u:u + 1],
                                   scale=SCALE_C, accum_out=stat[:, 2, u:u + 1]).then_inc(sem["cross_exp"], 1)
                u = s - 2
                if 0 <= u < 16:
                    hd, b = u // 4, u % 4
                    ps = filled(act, ("CT", u))
                    if hd >= 2:
                        act.wait_ge(sem["cross_out"], 2 * (hd - 1))
                    act.activation(CPT[:, hd % 2, :, P * b:P * b + P], ps[:, 0:MEM].rearrange("p (k q) -> p k q", q=P),
                                   ACT.Copy).then_inc(TA, 1)
            filled(act, "oc", 7)
            squares("mlp", lambda j: taken(act, "oc", j))
            root("mlp")
            act.activation(cond[:, 0, :], vecT[:, VEC["c_2"]:VEC["c_2"] + DT], ACT.Silu)
            act.activation(cond[:, 1, :], vecT[:, VEC["c_ctx_2"]:VEC["c_ctx_2"] + DT], ACT.Silu)\
                .then_inc(sem["cond_ready"], 1)
            def hidden(i):
                for j in range(4):
                    ps = filled(act, ("up", 4 * i + j))
                    if i >= 2:
                        filled(act, ("down", 8 * (i - 2) + 7))
                    act.activation(uT[:, i % 2, j, :], ps[:, :], ACT.Relu).then_inc(TA, 1)

            def shift(name, buf, layer, c):
                for j in range(DT):
                    act.wait_ge(sem[name + "_scaled"], j + 1)
                    act.activation(buf[:, j, :], buf[:, j, :], ACT.Identity, bias=ada[:, layer, j, c:c + 1])\
                        .then_inc(sem[name + "_normed"], 1)

            for i in range(8):
                hidden(i)
                if i == 0:
                    act.wait_ge(sem["lam_in"], 16 * 3)
                    act.activation(stepn[:, :], stepn[:, :], ACT.Exp).then_inc(sem["step_ready"], 1)
                    act.wait_ge(sem["angle_ready"], 1)
                    act.activation(tmpn[0:DK, 2, :], tmpn[0:DK, 0, :], ACT.Exp)
                    act.activation(tmpn[0:DK, 3, :], tmpn[0:DK, 1, :], ACT.Sin, scale=0.5)
                    act.activation(tmpn[0:DK, 4, :], tmpn[0:DK, 1, :], ACT.Sin).then_inc(sem["sines_ready"], 1)
                if i == 1:
                    for q in range(3):
                        copy("cT", q, area(28160 + 512 * q, 512))
                    for q in range(2):
                        copy("lamT", q, area(25664 + 480 * q, 480), n=480)
                if i == 5:
                    for q in range(4):
                        copy("ctxT", q, ctxT[:, 2 * q:2 * q + 2, :].rearrange("p a n -> p (a n)"))
                    for j in range(DT):
                        taken(act, "ctxT", j // 2)
                        act.activation(hcT[:, j, :], ctxT[:, j, :], ACT.Square).then_inc(sem["ctx_squares"], 1)
                    ps = filled(act, "ctx_ssq")
                    act.activation(std2[:, :], ps[:, 0:CTX], ACT.Sqrt, scale=1.0 / D, bias=eps[:, 0:1]).then_inc(TA, 1)
            shift("ctx", hcT, 0, 1)
            squares("fin", lambda j: taken(act, ("down", 56 + j)))
            root("fin")

            def chunked(stage, i, at, n):
                ps = filled(act, stage, i)
                act.activation(uP[:, i, :, at:at + n], ps[:, 0:CH * n].rearrange("p (c t) -> p t c", t=CH), ACT.Copy)\
                    .then_inc(TA, 1)

            for i in range(6):
                chunked("uc", i, 0, NCTX)
            filled(act, "fin_ssq")
            squares("ev", lambda j: act.wait_ge(sem["pos_added"], j + 1))
            root("ev")
            shift("ev", hT, 0, 0)
            for i in range(6):
                chunked("ul", i, NCTX, NLAT)
            for i in range(2):
                copy("ub", i, ubT[:, i, :])
            W = ring[:, chunk_at["wbuf"] % SLOTS, :].rearrange("p (r n) -> p r n", r=2)
            chunk_used(act, occupant(chunk_at["wbuf"]))
            for i in range(6):
                act.wait_ge(sem[f"u_out{i}"], 16)
            for bl in range(7):
                if bl < 6:
                    for q in range(4):
                        if bl >= 2:
                            filled(act, ("v", 4 * (bl - 2) + q))
                        copy(("wt", 4 * bl + q), 0, W[:, bl % 2, 512 * q:512 * q + 512])
                if bl >= 1:
                    for q in range(4):
                        ps = filled(act, ("v", 4 * (bl - 1) + q))
                        dk = 8 * (bl - 1) + 2 * q
                        V = Vf if dk < PAIRS else Vb
                        act.activation(V[:, :, dk % PAIRS:dk % PAIRS + 2, 0:NCH],
                                       ps[:, 0:384].rearrange("p (k c n) -> p c k n", k=2, c=2), ACT.Copy).then_inc(TA, 1)
            for t in range(TT):
                ps = filled(act, "pq", t)
                act.activation(pq[:, t, :, :].rearrange("p a n -> p (a n)"), ps[:, :], ACT.Copy).then_inc(TA, 1)
            for i in range(2):
                copy("ft", i, ftT[:, i, :])
            for i in range(2):
                copy("yb", i, ubT[:, i, :])
            act.wait_ge(sem["k_out"], 16 * (2 * CH - 1))
            for i in range(DT):
                ps = filled(act, "z", i)
                act.activation(zT[:, i, :], ps[:, :], ACT.Silu).then_inc(TA, 1)
            def place_states(bl):
                for e in range(2):
                    rows = slice(64 * e, 64 * e + 64)
                    for d, (V, at) in enumerate(((Vf, NCTX - 1), (Vb, NCTX + 1))):
                        act.activation(pairS[rows, bl % 2, d, :, :, e, :], V[rows, :, 4 * bl:4 * bl + 4, at:at + NLAT],
                                       ACT.Copy).then_inc(sem["states_placed"], 1)

            act.wait_ge(sem["scanned"], 1)
            act.wait_ge(sem["states_zero"], 1)
            place_states(0)
            place_states(1)
            for bl in range(6):
                ps = filled(act, "ys", bl)
                act.activation(Y[:, 8 * bl:8 * bl + 8, :], ps[:, :].rearrange("p (k n) -> p k n", k=8), ACT.Copy)\
                    .then_inc(TA, 1)
                if bl + 2 < 6:
                    place_states(bl + 2)
            for i in range(6):
                act.wait_ge(sem[f"ys_in{i}"], 16 * CH)
                act.activation(yg[:, i, :].rearrange("p (c t) -> p t c", t=CH)[:, ::-1, :],
                               yP[:, i, :].rearrange("p (t c) -> p t c", t=CH), ACT.Gelu_apprx_tanh)\
                    .then_inc(sem["gelu_done"], 1)
            for i in range(6):
                ps = filled(act, "glu", i)
                if i >= 2:
                    act.wait_ge(sem["glu_gated"], i - 1)
                act.activation(sg[:, i % 2, :], ps[:, :], ACT.Sigmoid, bias=g("s5_glu_b_2", i)).then_inc(TA, 1)
            filled(act, "eo", 7)
            squares("od", lambda j: taken(act, "eo", j))
            root("od")
            shift("od", hT, 1, 0)
            for i in range(4):
                copy("pool", i, gb[:, i, 8:8 + SEQ])
            for i in range(4):
                copy("cg", i, cgT[:, i, :])
            for i in range(4):
                copy("bg", i, bgT[:, i, :])
            for i in range(DT):
                ps = filled(act, "zo", i)
                act.activation(zoT[:, i, :], ps[:, :], ACT.Silu).then_inc(TA, 1)
            filled(act, "zo", 7)
            squares("end", lambda j: taken(act, "oo", j))
            root("end")
            for q in range(DT):
                t, half = q // 2, q % 2
                ps = filled(act, "yout", q)
                act.activation(onat[:, t, 512 * half:512 * half + 512], ps[:, :], ACT.Copy).then_inc(TA, 1)

        @block.vector
        def _(dve):
            TD = sem["taken_by_dve"]
            steps = [0]

            def mark(ins):
                steps[0] += 1
                ins.then_inc(sem["dve_step"], 1)
                return steps[0]

            def then(ins):
                dve.wait_ge(sem["dve_step"], mark(ins))

            def norm(name, gain, k=0):
                taken(dve, name + "_ssq")
                then(dve.reciprocal(std[:, :], std[:, :]))
                taken(dve, "vec", 2)
                for j in range(DT):
                    dve.scalar_tensor_tensor(out=hT[:, j, :], in0=xT[:, j, :], scalar=g(gain, k + j), in1=std[:, :],
                                             op0=ALU.mult, op1=ALU.mult).then_inc(sem[name + "_normed"], 1)

            norm("mix", "norm_mix_g")
            dve.wait_ge(sem["tables_in"], 16 * 5)

            def rotate(stage, i, n, which, dst):
                raw = tmp[:, n % 4, :]
                taken(dve, stage, i)
                n = mark(dve.tensor_tensor(out=dst, in0=raw, in1=rope[:, 2 * which, :], op=ALU.mult))
                ps = filled(dve, stage + "p", i)
                dve.wait_ge(sem["dve_step"], n)
                then(dve.tensor_tensor(out=raw, in0=rope[:, 2 * which + 1, :], in1=ps[:, :], op=ALU.mult))
                dve.tensor_tensor(out=dst, in0=dst, in1=raw, op=ALU.add).then_inc(TD, 1)

            for i in range(2):
                rotate("kir", i, i, i, (kiT, krT)[i])
            dve.wait_ge(sem["ckv_root"], 1)
            then(dve.reciprocal(stat[:, 2, 0:TT], stat[:, 1, 0:TT]))
            for t in range(TT):
                dve.scalar_tensor_tensor(out=ckvn[:, t, :], in0=ckvn[:, t, :], scalar=stat[:, 2, t:t + 1], in1=kvg,
                                         op0=ALU.mult, op1=ALU.mult).then_inc(sem["ckv_normed"], 1)
            for i in range(4):
                rotate("qi", i, 2 + i, 0, qiT[:, i, :])
            for n in range(24):
                b, hd = 1 + n // 8, n % 8
                keys = P * (b + 1)
                taken(dve, "idx", n)
                o = work[:, b - 1, 0:keys]
                if hd == 0:
                    ins = dve.tensor_scalar(o, tmp[:, n % 4, 0:keys], wnat[:, b, hd:hd + 1], None, ALU.mult)
                else:
                    dve.wait_ge(sem["index_added"], n)
                    ins = dve.scalar_tensor_tensor(out=o, in0=tmp[:, n % 4, 0:keys], scalar=wnat[:, b, hd:hd + 1],
                                                   in1=o, op0=ALU.mult, op1=ALU.add)
                ins.then_inc(sem["index_added"], 1)

            def topk():
                for b in range(1, TT):
                    keys = P * (b + 1)
                    o = work[:, b - 1, 0:keys]
                    diag = work[:, b - 1, P * b:keys]
                    dve.wait_ge(sem["index_added"], 8 * b)
                    then(dve.tensor_tensor(out=diag, in0=diag, in1=causal, op=ALU.add))
                    for r in range(TOPK // 8):
                        then(dve.max(top8, o))
                        then(dve.match_replace(o, top8, o, TAKEN))
                        yield
                    then(dve.tensor_scalar(pick[:, b - 1, 0:keys], o, -2e38, OFF, ALU.is_ge, ALU.mult))

            rounds = topk()

            def some_rounds(n):
                for _ in range(n):
                    next(rounds, None)

            for i in range(2):
                rotate("qr", i, 6 + i, 1, qrT[:, i, :])
                some_rounds(4)
            for st, dst, base in (("qb", qbT, 8), ("kb", kbT, 12)):
                for i in range(4):
                    rotate(st, i, base + i, 0, dst[:, i, :])
                    some_rounds(5)
            for _ in rounds:
                pass

            def soften(u):
                keys = P * (us[u][1] + 1)
                dve.wait_ge(sem["exp_done"], u + 1)
                then(dve.reciprocal(stat[:, 3, u:u + 1], stat[:, 2, u:u + 1]))
                dve.tensor_scalar(prob[:, u % 4, 0:keys], prob[:, u % 4, 0:keys], stat[:, 3, u:u + 1], None, ALU.mult)\
                    .then_inc(sem["prob_scaled"], 1)

            for s in range(len(us) + LAG_V):
                if s < len(us):
                    kind, b, hd = us[s]
                    keys = P * (b + 1)
                    if s == 0:
                        taken(dve, "kbp", 3)
                    if s >= 4:
                        filled(dve, ("T", s - 4))
                    ps = filled(dve, ("S", s))
                    if kind == "B":
                        bias = dilated[:, P * (3 - b):512]
                    else:
                        bias = causal if b == 0 else pick[:, b - 1, 0:keys]
                    dve.tensor_tensor_reduce(prob[:, s % 4, 0:keys], bias, ps[:, 0:keys], 1.0, -3e38, ALU.add, ALU.max,
                                             stat[:, 0, s:s + 1]).then_inc(TD, 1)
                    taken(dve, ("S", s))
                    dve.tensor_scalar(stat[:, 1, s:s + 1], stat[:, 0, s:s + 1],
                                      -(SCALE_A if kind == "A" else SCALE_B), None, ALU.mult).then_inc(sem["neg_max"], 1)
                if 1 <= s <= len(us):
                    soften(s - 1)
                u = s - LAG_V
                if u < 0:
                    continue
                kind, b, hd = us[u]
                if kind == "B" and hd == 7:
                    dve.wait_ge(sem["dilated_out"], 8 * (b + 1))
                    dve.tensor_copy(hT[:, 4:8, P * b:P * b + P],
                                    bank[6 + b % 2][:, :].rearrange("p (g q) -> p g q", q=P))\
                        .then_inc(sem["dilated_taken"], 1)
                elif kind == "A" and hd % 4 == 3:
                    n = 2 * b + hd // 4
                    dve.wait_ge(sem["latent_out"], n + 1)
                    dve.tensor_copy(olatT[:, hd - 3:hd + 1, P * b:P * b + P],
                                    bank[6 + n % 2][:, :].rearrange("p (g q) -> p g q", q=P))\
                        .then_inc(sem["latent_taken"], 1)

            def add_residual(stage):
                for i in range(DT):
                    ps = filled(dve, stage, i)
                    dve.tensor_tensor(out=xT[:, i, :], in0=xT[:, i, :], in1=ps[:, :], op=ALU.add).then_inc(TD, 1)

            dve.wait_ge(sem["mem_root"], 1)
            dve.reciprocal(stat[:, 2, 0:2], stat[:, 1, 0:2]).then_inc(sem["mem_rstd"], 1)
            add_residual("out")
            for j in range(DT):
                ps = filled(dve, "memT", j)
                dve.tensor_scalar(mT[:, j, :], ps[:, 0:MEM], g("norm_mem_g", j), None, ALU.mult).then_inc(TD, 1)
            taken(dve, "out", 7)
            norm("cross", "norm_cross_g")
            for s in range(16 + 3):
                if s < 16:
                    if s >= 4:
                        filled(dve, ("CT", s - 4))
                    ps = filled(dve, ("CS", s))
                    dve.tensor_scalar(cprob[:, s % 4, :], ps[:, 0:MEM], 1.0, None, ALU.mult).then_inc(TD, 1)
                    taken(dve, ("CS", s))
                    then(dve.tensor_reduce(stat[:, 0, s:s + 1], cprob[:, s % 4, :], AX, ALU.max))
                    dve.tensor_scalar(stat[:, 1, s:s + 1], stat[:, 0, s:s + 1], -SCALE_C, None, ALU.mult)\
                        .then_inc(sem["cross_neg_max"], 1)
                u = s - 1
                if 0 <= u < 16:
                    dve.wait_ge(sem["cross_exp"], u + 1)
                    then(dve.reciprocal(stat[:, 3, u:u + 1], stat[:, 2, u:u + 1]))
                    dve.tensor_scalar(cprob[:, u % 4, :], cprob[:, u % 4, :], stat[:, 3, u:u + 1], None, ALU.mult)\
                        .then_inc(sem["cross_scaled"], 1)
                u = s - 3
                if u >= 0 and u % 4 == 3:
                    for e in range(2):
                        dve.wait_ge(sem["cross_out"], 2 * (u // 4) + e + 1)
                        dve.tensor_copy(hT[:, 2 * (u // 4) + e, :], bank[6 + e][:, :]).then_inc(sem["cross_taken"], 1)
            add_residual("oc")
            taken(dve, "oc", 7)
            norm("mlp", "norm_mlp_g")
            def sum_ada(n):
                w = weights(dve, f"ad{n}").rearrange("p (j n) -> p j n", n=512)
                dve.wait_ge(sem["cond_ready"], 1)
                conds = range(2 if n < 6 else 1)
                for j in range(DT):
                    for c in conds:
                        if j == 0:
                            ins = dve.tensor_scalar(part[:, c, :], w[:, j, :], cond[:, c, j:j + 1], None, ALU.mult)
                        else:
                            ins = dve.scalar_tensor_tensor(out=part[:, c, :], in0=w[:, j, :], scalar=cond[:, c, j:j + 1],
                                                           in1=part[:, c, :], op0=ALU.mult, op1=ALU.add)
                        if j < DT - 1:
                            step = mark(ins)
                    if j < DT - 1:
                        dve.wait_ge(sem["dve_step"], step)
                ins.then_inc(sem["ada_summed"], 1)

            def add_ada(n):
                layer, at = n // 6, 4 * (n % 6)
                conds = 2 if n < 6 else 1
                ps = filled(dve, ("ada", n))
                bias = adabT[:, 24 * layer + at:24 * layer + at + 4].unsqueeze(2).broadcast_to([P, 4, conds])
                dve.tensor_tensor(out=ada[:, layer, at:at + 4, 0:conds], in0=bias,
                                  in1=ps[:, 0:8].rearrange("p (a c) -> p a c", c=2)[:, :, 0:conds], op=ALU.add)\
                    .then_inc(TD, 1)

            def square_hidden(i):
                for j in range(4):
                    taken(dve, ("up", 4 * i + j))
                    u = uT[:, i % 2, j, :]
                    dve.tensor_tensor(out=u, in0=u, in1=u, op=ALU.mult).then_inc(sem["relu_squared"], 1)

            def add_down(i):
                for m in range(DT):
                    ps = filled(dve, ("down", 8 * i + m))
                    dve.tensor_tensor(out=xT[:, m, :], in0=xT[:, m, :], in1=ps[:, :], op=ALU.add).then_inc(TD, 1)

            sum_ada(0)
            square_hidden(0)
            add_ada(0)
            lr, li = pwn[:, 18, :], pwn[:, 19, :]
            x = [tmpn[0:DK, i, :] for i in range(16)]
            MUL, ADD, SUB = ALU.mult, ALU.add, ALU.subtract

            def tt(o, a, b, op):
                return dve.tensor_tensor(out=o, in0=a, in1=b, op=op)

            dve.wait_ge(sem["b_in"], 64)
            then(dve.tensor_copy(bbar, bin_))
            dve.wait_ge(sem["step_ready"], 1)
            step = stepn[:, :].unsqueeze(2).broadcast_to([DK, 2, 64])
            two = lambda v: v.rearrange("p (e n) -> p e n", e=2)
            then(tt(two(x[0]), two(lr), step, MUL))
            then(tt(two(x[5]), two(li), step, MUL))
            then(dve.tensor_scalar(x[6], x[5], float(1 / (2 * np.pi)), ROUND, MUL, ADD))
            then(dve.tensor_scalar(x[6], x[6], ROUND, None, SUB))
            for piece in TWO_PI:
                then(dve.scalar_tensor_tensor(out=x[5], in0=x[6], scalar=-float(piece), in1=x[5], op0=MUL, op1=ADD))
            dve.tensor_scalar(x[1], x[5], 3.1415925, -3.1415925, ALU.min, ALU.max).then_inc(sem["angle_ready"], 1)
            dve.wait_ge(sem["sines_ready"], 1)
            then(tt(x[3], x[3], x[3], MUL))
            then(dve.tensor_scalar(x[3], x[3], -2.0, 1.0, MUL, ADD))
            dve.memset(pwn[:, 0, :], 1.0)
            dve.memset(pwn[:, 1, :], 0.0)
            tt(pwn[:, 2, :], x[2], x[3], MUL)
            then(tt(pwn[:, 3, :], x[2], x[4], MUL))
            ar, ai = pwn[:, 2, :], pwn[:, 3, :]

            def times(o_r, o_i, a, b, c, d, sign=1):
                tt(x[7], a, c, MUL)
                tt(x[8], b, d, MUL)
                tt(x[9], a, d, MUL)
                then(tt(x[10], b, c, MUL))
                tt(o_r, x[7], x[8], SUB if sign > 0 else ADD)
                then(tt(o_i, x[10], x[9], ADD if sign > 0 else SUB))

            for n in range(2, 9):
                times(pwn[:, 2 * n, :], pwn[:, 2 * n + 1, :], pwn[:, 2 * n - 2, :], pwn[:, 2 * n - 1, :], ar, ai)
            tt(x[11], lr, lr, MUL)
            then(tt(x[12], li, li, MUL))
            then(tt(x[11], x[11], x[12], ADD))
            then(dve.reciprocal(x[11], x[11]))
            then(dve.tensor_scalar(x[12], ar, -1.0, None, ADD))
            times(x[13], x[14], x[12], ai, lr, li, -1)
            tt(pwn[:, 18, :], x[13], x[11], MUL)
            tt(pwn[:, 19, :], x[14], x[11], MUL).then_inc(sem["poles_ready"], 1)

            def gain(n, layer, c):
                then(dve.scalar_tensor_tensor(out=gsc[:, n, :], in0=ada[:, layer, 8:16, c], scalar=1.0,
                                              in1=vecT[:, VEC["norm_g_2"] + 8 * layer:VEC["norm_g_2"] + 8 * layer + 8],
                                              op0=ADD, op1=MUL))

            def context():
                gain(0, 0, 0)
                gain(1, 0, 1)
                taken(dve, "ctx_ssq")
                then(dve.reciprocal(std2[:, :], std2[:, :]))
                for j in range(DT):
                    dve.scalar_tensor_tensor(out=hcT[:, j, :], in0=ctxT[:, j, :], scalar=gsc[:, 1, j:j + 1],
                                             in1=std2[:, :], op0=MUL, op1=MUL).then_inc(sem["ctx_scaled"], 1)

            def make_g(bl, n):
                d, m = bl // 3, 8 * (bl % 3)
                pr, pi = powers(d, 0, 8, m)
                b_r, b_i = [bbar[:, c, 8 * bl:8 * bl + 8, :].unsqueeze(2).broadcast_to([P, 8, 8, 16]) for c in range(2)]
                re, im = [G[:, bl % 2, c, :, :].rearrange("p k (j h) -> p k j h", h=16) for c in range(2)]
                tt(g1, pr, b_r, MUL)
                then(tt(re, pi, b_i, MUL))
                then(tt(re, g1, re, SUB))
                tt(g1, pr, b_i, MUL)
                then(tt(im, pi, b_r, MUL))
                tt(im, g1, im, ADD).then_inc(sem["g_ready"], 1)
                dve.wait_ge(sem["g_ready"], n)

            for i in range(1, 8):
                sum_ada(ADA_AFTER_UP[i])
                square_hidden(i)
                add_ada(ADA_AFTER_UP[i])
                if i == 2:
                    taken(dve, "cT", 2)
                    dve.wait_ge(sem["cb_zero"], 1)
                    for e in range(2):
                        rows = slice(64 * e, 64 * e + 64)
                        for c in range(2):
                            dve.tensor_scalar(cb[rows, :, c, 16 * e:16 * e + 16], cc[rows, c, :, :], 1.0 - 2 * c, None, MUL)\
                                .then_inc(sem["cb_ready"], 1)
                    taken(dve, "lamT", 1)
                    fr, fi = [pwT[:, 18 + c, :].unsqueeze(2).broadcast_to([P, DK, 16]) for c in range(2)]
                    br, bi = bbar[:, 0, :, :], bbar[:, 1, :, :]
                    t1, t2 = bin_[:, 0, :, :], bin_[:, 1, :, :]
                    then(tt(t1, br, fi, MUL))
                    then(tt(t2, bi, fr, MUL))
                    then(tt(t1, t1, t2, ADD))
                    then(tt(t2, bi, fi, MUL))
                    then(tt(br, br, fr, MUL))
                    tt(br, br, t2, SUB)
                    then(dve.tensor_copy(bi, t1))
                if i >= 2:
                    make_g(i - 2, i - 1)
                if i in ADA_AFTER_DOWN:
                    sum_ada(ADA_AFTER_DOWN[i])
                add_down(i - 1)
                if i in ADA_AFTER_DOWN:
                    add_ada(ADA_AFTER_DOWN[i])
                if i >= 2:
                    ps = filled(dve, ("kk", i - 2))
                    dve.tensor_copy(K[:, (i - 2) // 3, 256 * ((i - 2) % 3):256 * ((i - 2) % 3) + 256], ps[:, 0:256])\
                        .then_inc(TD, 1)
                if i == 5:
                    taken(dve, ("ada", 3))
                    context()
            dve.wait_ge(sem["k_moved"], 16)
            then(tt(k0[0:16], kt[0:16], K[0:16, 1, :].rearrange("p (g h) -> p g h", h=16), ADD))
            then(tt(kt[0:16], ident[0:16, 0:16].unsqueeze(1).broadcast_to([16, GROUPS, 16]),
                    skipT[:, :].unsqueeze(2).broadcast_to([16, GROUPS, 16]), MUL))
            tt(k0[0:16], k0[0:16], kt[0:16], ADD).then_inc(sem["k0_ready"], 1)
            add_down(7)
            taken(dve, ("ada", 11))
            gain(2, 1, 0)
            taken(dve, "fin_ssq")
            then(dve.reciprocal(std[:, :], std[:, :]))
            pos = weights(dve, "pos").rearrange("p (j n) -> p j n", j=DT)
            for j in range(DT):
                n = mark(dve.scalar_tensor_tensor(out=xT[:, j, :], in0=xT[:, j, :], scalar=g("norm_final_g", j),
                                                  in1=std[:, :], op0=MUL, op1=MUL))
                dve.wait_ge(sem["dve_step"], n)
                tt(xT[:, j, :], xT[:, j, :], pos[:, j, :], ADD).then_inc(sem["pos_added"], 1)

            def modulated(name, k):
                taken(dve, name + "_ssq")
                then(dve.reciprocal(std[:, :], std[:, :]))
                for j in range(DT):
                    dve.scalar_tensor_tensor(out=hT[:, j, :], in0=xT[:, j, :], scalar=gsc[:, k, j:j + 1], in1=std[:, :],
                                             op0=MUL, op1=MUL).then_inc(sem[name + "_scaled"], 1)

            dve.wait_ge(sem["pos_added"], DT)
            modulated("ev", 0)
            n = chunk_at["fch"]
            chunk_used(dve, occupant(n))
            fw = ring[:, n % SLOTS, 256:512].rearrange("p (i d) -> p i d", i=2)
            dve.memset(fw[0:64, :, 64:128], 0.0)
            dve.memset(fw[64:128, :, 0:64], 0.0).then_inc(sem["fch_zero"], 1)
            for bl in range(6):
                if bl >= 2:
                    filled(dve, ("wt", 4 * (bl - 2) + 3))
                make_g(bl, 7 + bl)
            taken(dve, ("v", 23))

            def both(qf, qb, swap=False):
                at, other = V_AT[0] + qf, V_AT[1] + qb
                c = PAIRS * VC
                if swap:
                    return bass.AP(tensor=arena, offset=at + c, ap=[[ARENA, P], [other - at, 2], [-c, 2], [VC, PAIRS]])
                return bass.AP(tensor=arena, offset=at, ap=[[ARENA, P], [other - at, 2], [c, 2], [VC, PAIRS]])

            a8 = area(24352, 2, 2, 2, PAIRS)
            for d in range(2):
                for c in range(2):
                    dve.tensor_copy(a8[:, 0, d, c, :], pwT[:, 16, PAIRS * d:PAIRS * d + PAIRS])
                    n = mark(dve.tensor_scalar(a8[:, 1, d, c, :], pwT[:, 17, PAIRS * d:PAIRS * d + PAIRS],
                                               2.0 * c - 1, None, MUL))
            dve.wait_ge(sem["dve_step"], n)

            def scan_step(now, before):
                tt(m8[:, 0], both(*before), a8[:, 0], MUL)
                then(tt(m8[:, 1], both(*before, swap=True), a8[:, 1], MUL))
                o = both(*now)
                then(tt(o, o, m8[:, 0], ADD))
                return tt(o, o, m8[:, 1], ADD)

            for q in range(1, NCTX):
                then(scan_step((q, NCTX - 1 - q), (q - 1, NCTX - q)))
            then(dve.tensor_copy(Vb[:, :, :, NCH], Vb[:, :, :, 0]))
            for q in range(NCTX, NCH):
                ins = scan_step((q, NCH - 1 - (q - NCTX)), (q - 1, NCH - (q - NCTX)))
                if q < NCH - 1:
                    then(ins)
            ins.then_inc(sem["scanned"], 1)
            for bl in range(2, 6):
                filled(dve, "ys", bl - 2)
                make_ca(dve, then, bl, g1, "ca_by_dve", 2 * (bl - 2) + 2)
            for i in range(2):
                taken(dve, "z", 6 + i)
                tt(zT[:, 6 + i, :], zT[:, 6 + i, :], ubT[:, i, :], MUL).then_inc(sem["fnet_gated"], 1)
            for i in range(6):
                taken(dve, "glu", i)
                if i == 0:
                    for k in range(6):
                        dve.wait_ge(sem[f"ys_out{k}"], 16)
                then(tt(hT[:, i, :], yg[:, i, :], sg[:, i % 2, :], MUL))
                tt(hT[:, i, :], hT[:, i, :], zT[:, i, :], MUL).then_inc(sem["glu_gated"], 1)

            def add_gated(stage, layer):
                for i in range(DT):
                    ps = filled(dve, stage, i)
                    dve.scalar_tensor_tensor(out=xT[:, i, :], in0=ps[:, :], scalar=ada[:, layer, 16 + i, 0:1],
                                             in1=xT[:, i, :], op0=MUL, op1=ADD).then_inc(TD, 1)

            add_gated("eo", 0)
            taken(dve, "eo", 7)
            modulated("od", 2)
            dve.memset(gb[:, :, 0:8], 0.0)
            dve.memset(cx[:, :, 0:1], 0.0)
            dve.memset(cx[:, :, SEQ + 1:SEQ + 2], 0.0)
            then(dve.memset(gb[:, :, 8 + SEQ:], 0.0))
            dve.wait_ge(sem["rc_in"], 16)
            for i in range(4):
                taken(dve, "pool", i)
                b = gb[:, i, :]
                n = SEQ + 16
                then(tt(sw[:, 0, 1:n], b[:, 0:n - 1], b[:, 1:n], ADD))
                for k in range(i):
                    e = 1 << k
                    then(tt(sw[:, (k + 1) % 2, 2 * e:n - 2 * e], sw[:, k % 2, e:n - 3 * e], sw[:, k % 2, 3 * e:n - e], ADD))
                then(tt(sw[:, i % 2, 8:8 + SEQ], sw[:, i % 2, 8:8 + SEQ], rc[:, i, :], MUL))
                tt(pooled[:, i, :], sw[:, i % 2, 8:8 + SEQ], b[:, 8:8 + SEQ], SUB).then_inc(sem["pooled"], 1)
                dve.wait_ge(sem["pooled"], i + 1)
            for i in range(4):
                taken(dve, "cg", i)
                ps = filled(dve, "xp", i)
                tt(cx[:, i, 1:SEQ + 1], cgT[:, i, :], ps[:, :], MUL).then_inc(TD, 1)
            for i in range(4):
                taken(dve, "xp", i)
                o = cgT[:, i, :]
                then(dve.tensor_scalar(o, cx[:, i, 0:SEQ], g("conv_w_2", i), None, MUL))
                for k in (1, 2):
                    then(dve.scalar_tensor_tensor(out=o, in0=cx[:, i, k:k + SEQ], scalar=g("conv_w_2", 4 * k + i), in1=o,
                                                  op0=MUL, op1=ADD))
                taken(dve, "bg", i)
                then(tt(o, o, bgT[:, i, :], MUL))
            for i in range(4):
                taken(dve, "zo", i)
                ps = filled(dve, "pm", i)
                dve.scalar_tensor_tensor(out=yT[:, i, :], in0=ps[:, :], scalar=g("pool_scale_2", i), in1=zoT[:, i, :],
                                         op0=MUL, op1=MUL).then_inc(TD, 1)
            for i in range(4):
                taken(dve, "zo", 4 + i)
                tt(yT[:, 4 + i, :], cgT[:, i, :], zoT[:, 4 + i, :], MUL).then_inc(sem["odd_gated"], 1)
            add_gated("oo", 1)
            taken(dve, "oo", 7)
            norm("end", "final_g_2")


INPUTS = ["x", "mem", "norm_mix_g", "w_in", "kv_norm_g", "w_uk", "w_uv", "w_out", "norm_cross_g", "norm_mem_g",
          "w_q_cross", "w_kv_cross", "w_o_cross", "norm_mlp_g", "w_up", "w_down", "norm_final_g", "c_2", "ctx_2",
          "c_ctx_2", "norm_g_2", "ada_w_2", "ada_b_2", "even_w_in_2", "even_w_out_2", "s5_lam_re_2", "s5_lam_im_2",
          "s5_log_step_2", "s5_b_re_2", "s5_b_im_2", "s5_c_re_2", "s5_c_im_2", "s5_d_2", "s5_glu_w_2", "s5_glu_b_2",
          "fnet_w_2", "odd_w_in_2", "odd_w_out_2", "pool_w_2", "pool_scale_2", "conv_w_2", "final_g_2"]


def kernel(**inputs):
    import concourse.bacc as bacc
    from concourse.bass_utils import run_bass_kernel_spmd

    nc = bacc.Bacc("TRN2", target_bir_lowering=False, num_devices=1)
    arrays, args = {}, {}
    for name, a in [(n, inputs[n]) for n in INPUTS] + list(constants().items()):
        a = np.ascontiguousarray(a)
        arrays["in_" + name] = a
        args[name] = nc.dram_tensor("in_" + name, a.shape, mybir.dt.from_np(a.dtype), kind="ExternalInput").ap()
    out = nc.dram_tensor("out_0", (1, SEQ, D), F32, kind="ExternalOutput").ap()
    build(nc, args, out)
    r = run_bass_kernel_spmd(nc, [arrays], core_ids=[0])
    return r.results[0]["out_0"]
```

```python
from contextlib import ExitStack

import numpy as np
import concourse.bass as bass
from concourse import mybir

ALU = mybir.AluOpType
ACT = mybir.ActivationFunctionType
AX = mybir.AxisListType.X
F32 = mybir.dt.float32
F32R = mybir.dt.float32r

P = 128
D = 1024
DT = D // P
SEQ = 512
TT = SEQ // P
MEM = 256
CTX = 256
HEADS = 8
TOPK = 128
EPS = 1e-6
OFF = -1e30
TAKEN = -3e38
SLOTS = 3
ARENA = 29696
OUTPUTS_END = 16984
RING = 6
SCALE_A = float(96) ** -0.5
SCALE_B = float(64) ** -0.5
SCALE_C = float(256) ** -0.5

GRID_W = 64
POOL_WINDOWS = (2, 4, 8, 16)
GROUPS = 48
PAIRS = GROUPS // 2
DK = 2 * PAIRS
CH = 8
NCH = (CTX + SEQ) // CH
NCTX = CTX // CH
NLAT = SEQ // CH
TWO_PI = (6.28125, 0.0019350051879882812, 2 * np.pi - 6.28125 - 0.0019350051879882812)
ROUND = 12582912.0

VEC_ROWS = [("norm_mix_g", 8), ("norm_cross_g", 8), ("norm_mem_g", 8), ("norm_mlp_g", 8), ("norm_final_g", 8),
            ("norm_g_2", 16), ("final_g_2", 8), ("pool_scale_2", 4), ("s5_glu_b_2", 6), ("conv_w_2", 12),
            ("c_2", 8), ("c_ctx_2", 8)]
VEC = {}
for _n, _r in VEC_ROWS:
    VEC[_n] = sum(r for _, r in VEC_ROWS[:len(VEC)])
VEC_N = sum(r for _, r in VEC_ROWS)


def constants():
    f = np.float32
    out = {"k_ident": np.eye(P, dtype=f)}
    t = np.arange(SEQ, dtype=f)
    tabs = []
    for d in (64, 32):
        inv = (f(10000.0) ** (-np.arange(0, d, 2, dtype=f) / f(d))).astype(f)
        p = np.arange(P)
        ang = (t[None, :] * inv[p % (d // 2)][:, None]).astype(f)
        sign = np.where((p % d) < d // 2, -1.0, 1.0)[:, None]
        tabs += [np.cos(ang.astype(np.float64)), sign * np.sin(ang.astype(np.float64))]
    out["k_rope"] = np.stack(tabs, 1).astype(f)
    perm = np.zeros((P, 2, P), f)
    for n, d in enumerate((64, 32)):
        for p in range(P):
            perm[(p // d) * d + (p % d + d // 2) % d, n, p] = 1
    out["k_perm"] = perm
    q, k = np.arange(P)[:, None], np.arange(P)[None, :]
    out["k_causal"] = np.where(k <= q, 0.0, OFF).astype(f)
    tiles = []
    for delta in (3, 2, 1, 0):
        d = delta * P + q - k
        c = ((d >= 0) & (d <= 128)) * 1.0 + ((d >= 0) & (d % 4 == 0)) + ((d >= 0) & (d % 16 == 0))
        tiles.append(np.where(c > 0, np.log(np.maximum(c, 1)) / SCALE_B, OFF))
    out["k_dilated"] = np.concatenate(tiles, 1).astype(f)
    quarter = D // 4
    omega = f(10000.0) ** (-np.arange(quarter, dtype=f) / f(quarter))
    rr = (np.arange(SEQ) // GRID_W).astype(f)[:, None] * omega
    cc = (np.arange(SEQ) % GRID_W).astype(f)[:, None] * omega
    rr, cc = rr.astype(np.float64), cc.astype(np.float64)
    out["k_pos"] = np.concatenate([np.sin(rr), np.cos(rr), np.sin(cc), np.cos(cc)], 1).T.astype(f).copy()
    t = np.arange(SEQ)
    a = 2 * np.pi * (np.outer(t, t) % SEQ) / SEQ
    out["k_dft"] = np.stack([np.cos(a), -np.sin(a)], 1).astype(np.float64) / np.sqrt(SEQ * 64)
    out["k_dft"] = out["k_dft"].astype(f)
    c = np.arange(64)
    a = 2 * np.pi * (np.outer(c, c) % 64) / 64
    two = np.eye(2)
    out["k_dftc"] = np.concatenate([np.kron(two, np.cos(a)), np.kron(two, np.sin(a))], 1).astype(f)
    rc = [1.0 / (np.minimum(t + w // 2, SEQ) - np.maximum(t - w // 2, 0)) for w in POOL_WINDOWS]
    out["k_rcount"] = np.stack(rc).astype(f)
    return out


class Tiles:

    def __init__(self):
        self.index, self.owner, self.count = {}, [], []
        self.totals = {"act": 0, "dve": 0}

    def add(self, stage, n, owner, start=0):
        for i in range(start, start + n):
            self.index[stage, i] = len(self.owner)
            self.owner.append(owner)
            self.totals[owner] += 1
            self.count.append(self.totals[owner])
            if isinstance(stage, tuple) and stage[0] in ("up", "down", "ada"):
                self.index[stage] = self.index[stage, i]


def units():
    return [(kind, b, h) for kind in "BA" for b in range(TT) for h in range(HEADS)]


LAG_T, LAG_V = 2, 4


def plan_tiles():
    t = Tiles()
    t.add("vec", 3, "act")
    t.add("xin", DT, "act")
    t.add("mix_ssq", 1, "act")
    t.add("ckv", TT, "act")
    t.add("kir", 2, "act")
    t.add("kirp", 2, "dve")
    t.add("ckvT", 1, "act")
    rope_pair(t, "qi", 4)
    t.add("idx", 24, "act")
    rope_pair(t, "qr", 2)
    t.add("qn", 4, "act")
    rope_pair(t, "qb", 4)
    rope_pair(t, "kb", 4)
    t.add("vb", TT, "act")
    t.add("qlat", HEADS, "act")
    us = units()
    for s in range(len(us) + LAG_V):
        if s < len(us):
            t.add(("S", s), 1, "dve")
        if 0 <= s - LAG_T < len(us):
            t.add(("T", s - LAG_T), 1, "act")
    t.add("oa", 4, "act")
    t.add("out", DT, "dve")
    t.add("memT", DT, "dve")
    t.add("kc", 4, "act")
    t.add("cross_ssq", 1, "act")
    t.add("kc", 4, "act", start=4)
    t.add("vc", 4, "act")
    t.add("qc", DT, "act")
    for s in range(16 + 3):
        if s < 16:
            t.add(("CS", s), 1, "dve")
        if 0 <= s - 2 < 16:
            t.add(("CT", s - 2), 1, "act")
    t.add("oc", DT, "dve")
    t.add("mlp_ssq", 1, "act")
    for i in range(8):
        for j in range(4):
            t.add(("up", 4 * i + j), 1, "act")
        t.add(("ada", ADA_AFTER_UP[i]), 1, "dve")
        for m in range(DT if i else 0):
            t.add(("down", 8 * (i - 1) + m), 1, "dve")
        if i in ADA_AFTER_DOWN:
            t.add(("ada", ADA_AFTER_DOWN[i]), 1, "dve")
        if i == 1:
            t.add("cT", 3, "act")
            t.add("lamT", 2, "act")
        if i >= 2:
            t.add(("kk", i - 2), 1, "dve")
        if i == 5:
            t.add("ctxT", 4, "act")
            t.add("ctx_ssq", 1, "act")
    for m in range(DT):
        t.add(("down", 56 + m), 1, "dve")
    t.add("fin_ssq", 1, "act")
    t.add("uc", 6, "act")
    t.add("ev_ssq", 1, "act")
    t.add("ul", 6, "act")
    t.add("ub", 2, "act")
    for bl in range(7):
        if bl < 6:
            for q in range(4):
                t.add(("wt", 4 * bl + q), 1, "act")
        if bl >= 1:
            for q in range(4):
                t.add(("v", 4 * (bl - 1) + q), 1, "act")
    t.add("pq", TT, "act")
    t.add("ft", 2, "act")
    t.add("yb", 2, "act")
    t.add("z", DT, "act")
    t.add("ys", 6, "act")
    t.add("glu", 6, "act")
    t.add("eo", DT, "dve")
    t.add("od_ssq", 1, "act")
    t.add("pool", 4, "act")
    t.add("cg", 4, "act")
    t.add("xp", 4, "dve")
    t.add("bg", 4, "act")
    t.add("pm", 4, "dve")
    t.add("zo", DT, "act")
    t.add("oo", DT, "dve")
    t.add("end_ssq", 1, "act")
    t.add("yout", DT, "act")
    return t


ADA_AFTER_UP = [0, 1, 2, 3, 4, 6, 8, 10]
ADA_AFTER_DOWN = {4: 5, 5: 7, 6: 9, 7: 11}


def rope_pair(t, stage, n):
    for i in range(n + 1):
        if i < n:
            t.index[stage, i] = len(t.owner)
            t.owner.append("act"); t.totals["act"] += 1; t.count.append(t.totals["act"])
        if i >= 1:
            t.index[stage + "p", i - 1] = len(t.owner)
            t.owner.append("dve"); t.totals["dve"] += 1; t.count.append(t.totals["dve"])


CHUNKS = ["kv", "qi", "qr", "qn", "qb", "kb", "vb", "mla", "out0", "out1", "kc0", "kc1", "vc0", "vc1",
          "qc0", "qc1", "oc0", "oc1"]
for _i in range(8):
    CHUNKS += [f"up{_i}", f"ad{ADA_AFTER_UP[_i]}"] + ([f"dn{_i - 1}"] if _i else [])
    CHUNKS += [f"ad{ADA_AFTER_DOWN[_i]}"] if _i in ADA_AFTER_DOWN else []
CHUNKS += ["dn7", "pos", "ev0", "ev1", "fch", "dft"]
CHUNKS += ["none"] * (-len(CHUNKS) % SLOTS)
CHUNKS += ["wbuf", "none", "none", "ev2", "ev3", "none", "Ta", "Tb", "sbuf", "glu0", "glu1", "eo0", "eo1"] + [f"od{_i}" for _i in range(4)] + ["pw", "od4", "od5", "oo0", "oo1"]



def occupant(n):
    n -= SLOTS
    while CHUNKS[n] == "none":
        n -= SLOTS
    return CHUNKS[n]


LAST_TILE = {"kv": ("kir", 1), "qi": ("qi", 3), "qr": ("qr", 1), "qn": ("qn", 3), "qb": ("qb", 3), "kb": ("kb", 3),
             "vb": ("vb", 3), "mla": ("oa", 3), "vc0": ("vc", 1), "vc1": ("vc", 3)}
for _s in ("out", "kc", "qc", "oc", "up"):
    LAST_TILE.update({f"{_s}{_i}": (_s, 4 * _i + 3) for _i in range(8 if _s == "up" else 2)})
LAST_TILE.update({f"dn{_i}": ("down", 8 * _i + 7) for _i in range(8)})
LAST_TILE.update({"ev0": ("ul", 3), "ev1": ("ub", 1), "ev2": ("z", 3), "ev3": ("z", 7), "fch": ("yb", 1),
                  "dft": ("ft", 1), "wbuf": (("v", 23), 0), "sbuf": ("ys", 5),
                  "glu0": ("glu", 2), "glu1": ("glu", 5), "eo0": ("eo", 3), "eo1": ("eo", 7), "pw": ("pm", 3),
                  "od0": ("pool", 3), "od1": ("cg", 3), "od2": ("xp", 3), "od3": ("bg", 3), "od4": ("zo", 3),
                  "od5": ("zo", 7), "oo0": ("oo", 3), "oo1": ("oo", 7)})

SPLITS = {"heads": ["qr:0", "qn:0", "qn:1", "qb:0", "qb:1", "kb:0", "kb:1", "vb:0", "vb:1"],
          "cross": ["kc0", "kc1", "vc0", "vc1", "qc0", "qc1", "oc0", "oc1"],
          "mlp": ["dn1:0", "dn1:1"]
          + [f"{_s}:{_h}" for _i in range(3, 8) for _s in (f"up{_i}", f"dn{_i - 1}") for _h in range(2)]
          + ["dn7:0", "dn7:1"],
          "inputs": ["ev0:0", "ev0:1", "ev1:0", "ev1:1"],
          "even": ["eo0", "eo1"],
          "odd": [f"od{_i}" for _i in range(6)] + ["oo0", "oo1"]}
HIGH_AT = {"heads": (17408, 19456), "cross": (15360, 19456), "mlp": (4096, 6144), "inputs": (9264, 11312),
           "even": (4656, 25176), "odd": (21080, 25176)}
SPLIT_ORDER = [_s for _names in SPLITS.values() for _s in _names]
LOW_BY_DVE = ["vc1", "qc1"]
POOL_BACKS = (3, 5)
LOW_BY_POOL = [_s for _s in SPLIT_ORDER if _s not in LOW_BY_DVE]

LAST_TILE.update({_s: (_s[:2], 3 if _s[:2] == "vb" else 2 * int(_s[3]) + 1) for _s in SPLITS["heads"]})
for _i in range(8):
    for _h in range(2):
        LAST_TILE.update({f"up{_i}:{_h}": ("up", 4 * _i + 2 * _h + 1), f"dn{_i}:{_h}": ("down", 8 * _i + 4 * _h + 3)})
LAST_TILE.update({"ev0:0": ("ul", 1), "ev0:1": ("ul", 3), "ev1:0": ("ul", 5), "ev1:1": ("ub", 1)})

ROPES = [("kir", i) for i in range(2)] + [("qi", i) for i in range(4)] + [("qr", i) for i in range(2)] \
    + [("qb", i) for i in range(4)] + [("kb", i) for i in range(4)]


def build(nc, A, out):
    T = plan_tiles()
    u_dram = nc.dram_tensor("u_dram", (768, CH, NCH), F32, kind="Internal").ap()
    k_dram = nc.dram_tensor("k_dram", (16, GROUPS, 2 * CH - 1, 16), F32, kind="Internal").ap()
    y_dram = nc.dram_tensor("y_dram", (6, P, 512), F32, kind="Internal").ap()

    def chunk_sources():
        win = A["w_in"][0].rearrange("(j p) n -> p j n", p=P)

        def cols(w, a, n):
            return [(lambda s: s.rearrange("p (j n) -> p j n", j=DT)[:, :, 0:n],
                     w.rearrange("(j p) n -> p j n", p=P)[:, :, a:a + n])]

        def put(a, n, src):
            return (lambda s: s.rearrange("p (j n) -> p j n", j=DT)[:, :, a:a + n], src)

        c = {}
        c["kv"] = [put(0, 128, win[:, :, 768:896]), put(128, 8, win[:, :, 1504:1512])]
        c["kv"] += [put(136 + 64 * i, 64, win[:, :, 1440:1504]) for i in range(2)]
        c["kv"] += [put(264 + 32 * i, 32, win[:, :, 896:928]) for i in range(4)]
        c["qi"] = [put(0, 512, win[:, :, 928:1440])]
        c["qr"] = [put(0, 256, win[:, :, 512:768])]
        c["qn"] = [put(0, 512, win[:, :, 0:512])]
        for i, n in enumerate(("qb", "kb", "vb")):
            c[n] = [put(0, 512, win[:, :, 1512 + 512 * i:2024 + 512 * i])]
        c["mla"] = [(lambda s: s[:, 0:512].rearrange("p (g c) -> p g c", g=4),
                     A["w_uk"][0].rearrange("(g e) n c -> (e n) g c", e=2)),
                    (lambda s: s[:, 512:1024].rearrange("p (h v) -> p h v", h=HEADS),
                     A["w_uv"][0].rearrange("h c v -> c h v"))]
        for i in range(2):
            c[f"out{i}"] = cols(A["w_out"][0], 512 * i, 512)
            c[f"qc{i}"] = cols(A["w_q_cross"][0], 512 * i, 512)
            c[f"oc{i}"] = cols(A["w_o_cross"][0], 512 * i, 512)
            c[f"kc{i}"] = cols(A["w_kv_cross"][0], 512 * i, 512)
            c[f"vc{i}"] = cols(A["w_kv_cross"][0], 1024 + 512 * i, 512)
        for i in range(8):
            c[f"up{i}"] = cols(A["w_up"][0], 512 * i, 512)
        for i in range(8):
            c[f"dn{i}"] = [(lambda s: s.rearrange("p (j n) -> p j n", j=4),
                            A["w_down"][0, 512 * i:512 * i + 512].rearrange("(j p) n -> p j n", p=P))]
        for i in range(12):
            c[f"ad{i}"] = cols(A["ada_w_2"][i // 6], 512 * (i % 6), 512)
        c["pos"] = [put(0, 512, A["k_pos"].rearrange("(j p) n -> p j n", p=P))]
        for i in range(4):
            c[f"ev{i}"] = cols(A["even_w_in_2"][0], 512 * i, 512)
        c["fch"] = [(lambda s: s[:, 0:256], A["k_dftc"])]
        for e in range(2):
            c["fch"].append((lambda s, e=e: s[64 * e:64 * e + 64, 256:512].rearrange("p (i d) -> p i d", i=2)
                             [:, :, 64 * e:64 * e + 64],
                             A["fnet_w_2"][0].rearrange("(i e) c d -> e c i d", e=2)[e]))
        c["dft"] = [(lambda s: s.rearrange("p (t w n) -> p t w n", t=TT, w=2),
                     A["k_dft"].rearrange("(t p) w n -> p t w n", p=P))]
        c["wbuf"], c["none"], c["sbuf"] = [], [], []
        for name, lo, hi in (("Ta", 0, 32), ("Tb", 32, GROUPS)):
            c[name] = [(lambda s, tau=tau, lo=lo, hi=hi: s[16 * tau:16 * tau + 16, 0:P * (hi - lo)]
                        .rearrange("h (g n) -> h g n", n=P),
                        k_dram[:, lo:hi, tau:tau + CH, :].rearrange("h g t n -> h g (t n)")) for tau in range(CH)]
        for i in range(2):
            c[f"glu{i}"] = [(lambda s: s[:, 0:2304].rearrange("p (j n) -> p j n", j=6),
                             A["s5_glu_w_2"][0].rearrange("(j p) n -> p j n", p=P)[:, :, 384 * i:384 * i + 384])]
            c[f"eo{i}"] = cols(A["even_w_out_2"][0], 512 * i, 512)
            c[f"oo{i}"] = cols(A["odd_w_out_2"][0], 512 * i, 512)
        for i in range(6):
            c[f"od{i}"] = cols(A["odd_w_in_2"][0], 512 * i, 512)
        c["pw"] = [(lambda s: s[:, 0:512].rearrange("p (g d) -> p g d", g=4), A["pool_w_2"][0].rearrange("g c d -> c g d"))]
        return c

    sources = chunk_sources()
    chunk_at = {n: i for i, n in enumerate(CHUNKS)}
    landed, so_far = [], [0] * SLOTS
    for i, n in enumerate(CHUNKS):
        so_far[i % SLOTS] += 16 * len(sources[n])
        landed.append(so_far[i % SLOTS])

    with ExitStack() as ctx:
        def sb(name, shape):
            return ctx.enter_context(nc.sbuf_tensor(name, shape, F32))

        class Sems(dict):
            def __missing__(self, name):
                self[name] = ctx.enter_context(nc.semaphore(name))
                return self[name]

        sem = Sems()
        ident = sb("ident", [P, P])
        ones = sb("ones", [P, P])
        vec = sb("vec", [P, P])
        vecT = sb("vecT", [P, P])
        adab = sb("adab", [48, P])
        adabT = sb("adabT", [P, 48])
        skip = sb("skip", [GROUPS, 16])
        skipT = sb("skipT", [16, GROUPS])
        eps = sb("eps", [P, 1])
        stat = sb("stat", [P, 4, 64])
        std2 = sb("std2", [P, CTX])
        cond = sb("cond", [P, 2, DT])
        part = sb("part", [P, 2, SEQ])
        ada = sb("ada", [P, 2, 24, 2])
        gsc = sb("gsc", [P, 3, DT])
        stepn = sb("stepn", [DK, 2])
        xT = sb("xT", [P, DT, SEQ])
        shapes = (("hT", [P, DT, SEQ]), ("std", [P, SEQ]), ("ring", [P, SLOTS, 4096]), ("arena", [P, ARENA]))
        with ExitStack() as plain:
            hT, std, ring, arena = [plain.enter_context(nc.sbuf_tensor(name, shape, F32)) for name, shape in shapes]
        with ExitStack() as short:
            for name, shape in shapes[:3]:
                short.enter_context(nc.sbuf_tensor(name + "_space", shape, F32R))
            outputs_r = short.enter_context(nc.sbuf_tensor("outputs_r", [P, OUTPUTS_END], F32R))
        rounded = {name: ctx.enter_context(nc.sbuf_tensor(name + "_r", shape, F32R)) for name, shape in shapes}
        bank = [ctx.enter_context(nc.psum_tensor(f"bank{i}", [P, 512], F32)) for i in range(8)]

        def area(at, *shape):
            n = int(np.prod(shape))
            names = "abcd"[:len(shape)]
            v = arena[:, at:at + n]
            if len(shape) == 1:
                return v
            pat = f"p ({' '.join(names)}) -> p {' '.join(names)}"
            return v.rearrange(pat, **dict(zip(names, shape)))

        qnT = area(0, 4, SEQ)
        qiT = area(2048, 4, SEQ)
        olatT = area(0, HEADS, SEQ)
        qlatT = area(4096, HEADS, SEQ)
        xnat = area(4096, TT, D)
        qrT = area(8192, 2, SEQ)
        krT = area(9216, SEQ)
        kiT = area(9728, SEQ)
        qbT = area(10240, 4, SEQ)
        kbT = area(12288, 4, SEQ)
        vnat = area(14336, TT, 512)
        ckvn = area(16384, TT, P)
        ckvT = area(16896, SEQ)
        PTA = area(17408, TT, HEADS, P)
        perm = part[:, 0, 0:2 * P].rearrange("p (w n) -> p w n", w=2)
        nHi = area(4096, DT, SEQ)
        work = area(21504, 3, SEQ)
        pick = area(23040, 3, SEQ)
        rope = area(24576, 4, SEQ)
        prob = area(24576, 4, SEQ)
        tmp = area(26624, 4, SEQ)
        PTB = area(26624, 2, SEQ)
        dilated = area(28672, SEQ)
        causal = area(29184, P)
        wnat = area(29312, TT, HEADS)
        top8 = area(29344, 8)
        kvg = area(29352, P)
        memn = area(0, 2, D)
        mT = area(2048, DT, MEM)
        kcT = area(4096, DT, MEM)
        vcn = area(6144, 2, D)
        qcT = area(8192, DT, SEQ)
        cprob = area(12288, 4, MEM)
        CPT = area(13312, 2, 2, SEQ)
        cHi = area(23552, DT, SEQ)
        mHi = area(27648, DT, MEM)
        uT = area(0, 2, 4, SEQ)
        pwn = area(4096, 20, P)[0:DK]
        cn = area(6656, 12, P)
        kt = area(8192, GROUPS, 16)
        k0 = area(8960, GROUPS, 16)
        K = area(9728, 2, 768)
        bin_ = area(11264, 2, DK, 16)
        tmpn = area(11264, 16, P)
        hidHi = [area(8192 + SEQ * j, SEQ) for j in range(3)] + [std[:, :]]
        uHi = area(11264, DT, SEQ)
        Gk = area(15408, 2, 8, P)
        ctxn = area(17456, 2, D)
        hcT = area(17456, DT, CTX)
        ctxT = area(19504, DT, CTX)
        cb = area(21552, DK, 2, 32)
        g1 = area(24624, 8, 8, 16)
        pwT = area(25664, 20, DK)
        bbar = area(26624, 2, DK, 16)
        cc = area(28160, 2, DK, 16)
        uP = area(0, 6, CH, NCH)
        U = area(4656, GROUPS, NCH)
        zT = area(9264, DT, SEQ)
        G = area(13360, 2, 2, 8, P)
        CA = G
        g2 = area(22112, 8, 8, 16)
        ubT = area(23136, 2, SEQ)
        m8 = area(24160, 2, 2, 2, PAIRS)
        V_AT = (0, 17456)
        VC = NCH + 1
        Vf, Vb = [area(at, 2, PAIRS, VC) for at in V_AT]
        hflat = hT[:, :, :].rearrange("p a b -> p (a b)")
        vHi = area(17456, DT, SEQ)
        pq = ring[:, chunk_at["fch"] % SLOTS, 512:2560].rearrange("p (t i n) -> p t i n", t=TT, i=2)
        ftT = ring[:, chunk_at["fch"] % SLOTS, 2560:3584].rearrange("p (i n) -> p i n", i=2)
        Y = hflat[:, 0:3072].rearrange("p (g n) -> p g n", g=GROUPS)
        yP = area(4656, 6, SEQ)
        pairS = ring[:, chunk_at["sbuf"] % SLOTS, :].rearrange("p (r d c k e n) -> p r d c k e n", r=2, d=2, c=2, k=4, e=2)
        yg = area(17456, 6, SEQ)
        sg = area(13360, 2, SEQ)
        eHi = area(0, DT, SEQ)
        rc = area(0, 4, SEQ)
        gb = area(2048, 4, SEQ + 16)
        sw = [area(4160, SEQ + 16), part[:, :, :].rearrange("p a n -> p (a n)")[:, 0:SEQ + 16]]
        pooled = area(4688, 4, SEQ)
        cgT = area(6736, 4, SEQ)
        cx = area(8784, 4, SEQ + 2)
        bgT = area(10840, 4, SEQ)
        zoT = area(12888, DT, SEQ)
        onat = area(21080, TT, D)
        hHi = area(16984, DT, SEQ)
        yHi = area(0, DT, SEQ)

        def bank_free(eng, stage, i=0):
            n = T.index[stage, i]
            if n >= RING:
                eng.wait_ge(sem["taken_by_" + T.owner[n - RING]], T.count[n - RING])
            return bank[n % RING]

        def filled(eng, stage, i=0):
            n = T.index[stage, i]
            eng.wait_ge(sem["tile_filled"], n + 1)
            return bank[n % RING]

        def taken(eng, stage, i=0):
            n = T.index[stage, i]
            eng.wait_ge(sem["taken_by_" + T.owner[n]], T.count[n])

        def chunk_used(eng, name):
            if name == "pos":
                eng.wait_ge(sem["pos_added"], DT)
            elif name in ("Ta", "Tb"):
                eng.wait_ge(sem["chunk_products_done"], 1)
            elif name[:2] == "ad":
                eng.wait_ge(sem["ada_summed"], int(name[2:]) + 1)
            else:
                eng.wait_ge(sem["tile_filled"], T.index[LAST_TILE[name]] + 1)

        def weights(eng, name):
            n = chunk_at[name]
            eng.wait_ge(sem[f"slot{n % SLOTS}_landed"], landed[n])
            return ring[:, n % SLOTS, :]

        def high(name):
            phase = next(k for k, names in SPLITS.items() if name in names)
            at = HIGH_AT[phase][SPLITS[phase].index(name) % len(HIGH_AT[phase])]
            if name[:2] == "dn":
                return area(at, 4, 512)
            return area(at, DT, 256 if ":" in name else 512)

        def unsplit(name):
            chunk, _, half = name.partition(":")
            if name[:2] == "dn":
                w = ring[:, chunk_at[chunk] % SLOTS, :].rearrange("p (j n) -> p j n", n=D)
                return w[:, :, 512 * int(half):512 * int(half) + 512]
            w = ring[:, chunk_at[chunk] % SLOTS, :].rearrange("p (j n) -> p j n", n=512)
            return w[:, :, 256 * int(half):256 * int(half) + 256] if half else w

        def r(view):
            if view.dtype == F32R:
                return view
            return bass.AP(tensor=rounded[view.tensor.name], offset=view.offset, ap=view.ap)

        def ro(view):
            if view.dtype == F32R:
                return view
            return bass.AP(tensor=outputs_r, offset=view.offset, ap=[[OUTPUTS_END, P]] + list(view.ap)[1:])

        def hid_r(i, j):
            if i == 7:
                return ro(uHi[:, j, :])
            return ro(hidHi[j]) if j < 3 else r(hidHi[j])

        def back(view):
            return (view if view.dtype == F32R else r(view)).bitcast(F32)

        def weights_low(eng, name):
            eng.wait_ge(sem["weights_high"], SPLIT_ORDER.index(name) + 1)
            if name in SPLITS["inputs"][:3]:
                filled(eng, "uc", 2 * SPLITS["inputs"].index(name) + 1)
            w = unsplit(name)
            eng.tensor_tensor(out=r(w), in0=w, in1=back(high(name)), op=ALU.subtract)\
                .then_inc(sem["low_by_dve" if name in LOW_BY_DVE else "low_by_pool"], 1)

        def roped(eng, n):
            stage, i = ROPES[n]
            taken(eng, stage + "p", i)

        def g(name, j=0):
            return vecT[:, VEC[name] + j:VEC[name] + j + 1]

        def powers(d, lo, n, m):
            v = pwT[:, 2 * lo:2 * lo + 16, PAIRS * d + m:PAIRS * d + m + n].rearrange("p (j c) k -> p c k j", c=2)
            if d == 0:
                v = v[:, :, :, ::-1]
            return [v[:, c, :, :].unsqueeze(3).broadcast_to([P, n, 8, 16]) for c in range(2)]

        def input_matrices(bl, c):
            if bl % 3 < 2:
                return G[:, bl % 3, c, :, :]
            if c == 0:
                return area(21552, 8, P)
            return part[:, :, :].rearrange("p a n -> p (a n)").rearrange("p (k n) -> p k n", n=P)

        def output_matrices(bl, c):
            if bl % 3 < 2:
                return CA[:, bl % 3, c, :, :]
            if c == 0:
                return hflat[:, 3072:4096].rearrange("p (k n) -> p k n", n=P)
            return area(26624, 8, P)

        def make_ca(eng, then, bl, temp, name, n):
            for d in range(2):
                pr, pi = powers(d, 1, 4, 4 * bl)
                c_r, c_i = [cc[:, c, PAIRS * d + 4 * bl:PAIRS * d + 4 * bl + 4, :].unsqueeze(2)
                            .broadcast_to([P, 4, 8, 16]) for c in range(2)]
                re, im = [output_matrices(bl, c)[:, 4 * d:4 * d + 4, :].rearrange("p k (j h) -> p k j h", h=16)
                          for c in range(2)]
                t_r, t_i = temp[:, 0:4], temp[:, 4:8]
                eng.tensor_tensor(out=t_r, in0=pr, in1=c_r, op=ALU.mult)
                eng.tensor_tensor(out=re, in0=pi, in1=c_i, op=ALU.mult)
                eng.tensor_tensor(out=t_i, in0=pr, in1=c_i, op=ALU.mult)
                then(eng.tensor_tensor(out=im, in0=pi, in1=c_r, op=ALU.mult))
                eng.tensor_tensor(out=re, in0=t_r, in1=re, op=ALU.subtract).then_inc(sem[name], 1)
                then(eng.tensor_tensor(out=im, in0=t_i, in1=im, op=ALU.add))
                eng.tensor_scalar(im, im, -1.0, None, ALU.mult).then_inc(sem[name], 1)
                eng.wait_ge(sem[name], 2 * (n - 1 + d))

        block = ctx.enter_context(nc.Block())
        us = units()

        def u_back(eng, i):
            eng.wait_ge(sem["k_out"], 16 * (2 * CH - 1))
            eng.wait_ge(sem[f"u_out{i}"], 16)
            for tau in range(CH):
                eng.dma_start(U[16 * tau:16 * tau + 16, 8 * i:8 * i + 8, :],
                              u_dram[P * i:P * i + P, tau, :].rearrange("(g h) c -> h g c", h=16))\
                    .then_inc(sem[f"u_in{i}"], 16)

        def y_back(sp, i):
            sp.wait_ge(sem[f"ys_out{i}"], 16)
            for k in range(CH):
                sp.dma_start(yP[16 * k:16 * k + 16, i, :].rearrange("h (t c) -> h t c", t=CH),
                             y_dram[i].rearrange("(t h) (g c) -> g h t c", t=CH, g=8)[k]).then_inc(sem[f"ys_in{i}"], 16)

        @block.sync
        def _(sp):

            sp.dma_start(ident[:, :], A["k_ident"]).then_inc(sem["ident_in"], 16)
            rows = 0
            for name, r in VEC_ROWS:
                src = A[name]
                flat = src.rearrange({1: "(r n) -> r n", 2: "a (r n) -> (a r) n",
                                      3: "a b (r n) -> (a b r) n"}[len(src.shape)], n=P)
                sp.dma_start(vec[rows:rows + r, :], flat).then_inc(sem["vec_in"], 16)
                rows += r
            sp.dma_start(adab[:, :], A["ada_b_2"].rearrange("a (r n) -> (a r) n", n=P)).then_inc(sem["vec_in"], 16)
            sp.dma_start(skip[:, :], A["s5_d_2"][0]).then_inc(sem["vec_in"], 16)
            sp.dma_start(perm, A["k_perm"]).then_inc(sem["tables_in"], 16)
            sp.dma_start(rope, A["k_rope"]).then_inc(sem["tables_in"], 16)
            sp.dma_start(dilated, A["k_dilated"]).then_inc(sem["tables_in"], 16)
            sp.dma_start(causal, A["k_causal"]).then_inc(sem["tables_in"], 16)
            sp.dma_start(kvg, A["kv_norm_g"].broadcast_to([P, P])).then_inc(sem["tables_in"], 16)
            for n, name in enumerate(CHUNKS):
                if name == "none":
                    continue
                if n >= SLOTS:
                    chunk_used(sp, occupant(n))
                if name == "kc0":
                    taken(sp, "oa", 3)
                    sp.dma_start(memn, A["mem"][0].rearrange("(t p) n -> p t n", p=P)).then_inc(sem["mem_in"], 16)
                if name == "ad0":
                    taken(sp, "oc", 7)
                    sp.dma_start(ctxn, A["ctx_2"][0].rearrange("(t p) n -> p t n", p=P)).then_inc(sem["ctx_in"], 16)
                    for e in range(2):
                        for c, b in enumerate(("s5_b_re_2", "s5_b_im_2")):
                            sp.dma_start(bin_[64 * e:64 * e + 64, c, :, :],
                                         A[b][0].rearrange("d (k e) p h -> e p (d k) h", e=2)[e]).then_inc(sem["b_in"], 16)
                    for c, b in enumerate(("s5_lam_re_2", "s5_lam_im_2")):
                        sp.dma_start(pwn[:, 18 + c, :], A[b][0].rearrange("d (k e) p -> (d k) (e p)", e=2))\
                            .then_inc(sem["lam_in"], 16)
                    for c, b in enumerate(("s5_c_re_2", "s5_c_im_2")):
                        for i in range(12):
                            d, kb, e = i // 6, i // 2 % 3, i % 2
                            sp.dma_start(cn[:, 6 * c + 3 * d + kb, 64 * e:64 * e + 64],
                                         A[b][0, d, 16 * kb:16 * kb + 16].rearrange("(k e) h p -> e k h p", e=2)[e])\
                                .then_inc(sem["c_in"], 16)
                    sp.dma_start(stepn[:, :], A["s5_log_step_2"][0].rearrange("d (k e) -> (d k) e", e=2))\
                        .then_inc(sem["lam_in"], 16)
                if name == "Ta":
                    sp.wait_ge(sem["k_out"], 16 * (2 * CH - 1))
                if name == "od2":
                    taken(sp, "eo", 7)
                    sp.dma_start(rc, A["k_rcount"].rearrange("(a w) n -> a w n", a=1).broadcast_to([P, 4, SEQ]))\
                        .then_inc(sem["rc_in"], 16)
                for view, src in sources[name]:
                    sp.dma_start(view(ring[:, n % SLOTS, :]), src).then_inc(sem[f"slot{n % SLOTS}_landed"], 16)
                if name == "fch":
                    for i in range(6):
                        taken(sp, "uc", i)
                        taken(sp, "ul", i)
                        sp.dma_start(u_dram[P * i:P * i + P], uP[:, i, :, :]).then_inc(sem[f"u_out{i}"], 16)
                        if i >= 1 and i - 1 not in POOL_BACKS:
                            u_back(sp, i - 1)
                    if 5 not in POOL_BACKS:
                        u_back(sp, 5)
                if name == "glu1":
                    for i in range(6):
                        taken(sp, "ys", i)
                        sp.dma_start(y_dram[i], Y[:, 8 * i:8 * i + 8, :]).then_inc(sem[f"ys_out{i}"], 16)
                        if i % 2:
                            y_back(sp, i)
            for t in range(TT):
                taken(sp, "yout", 2 * t + 1)
                sp.dma_start(out[0, P * t:P * t + P, :], onat[:, t, :]).then_inc(sem["y_out"], 16)
            sp.wait_ge(sem["y_out"], 16 * TT)

        @block.gpsimd
        def _(pool):
            pool.memset(ones[:, :], 1.0).then_inc(sem["ones_set"], 1)
            pool.memset(eps[:, :], EPS).then_inc(sem["ones_set"], 1)

            def split_low(phase):
                for name in SPLITS[phase]:
                    if name not in LOW_BY_DVE:
                        weights_low(pool, name)

            split_low("heads")
            split_low("cross")
            taken(pool, "oc", 7)
            pool.memset(cb, 0.0).then_inc(sem["cb_zero"], 1)
            split_low("mlp")
            taken(pool, ("kk", 5))
            pool.dma_start(kt[0:16], K[112:128, 0, :].rearrange("p (g h) -> p g h", h=16)).then_inc(sem["k_moved"], 16)
            for i in range(CH - 1):
                for d in range(2):
                    rows = 16 * (i + d)
                    pool.dma_start(k_dram[:, :, CH * d + i, :],
                                   K[rows:rows + 16, d, :].rearrange("h (g n) -> h g n", n=16)).then_inc(sem["k_out"], 16)
            pool.wait_ge(sem["k0_ready"], 1)
            pool.dma_start(k_dram[:, :, CH - 1, :], k0[0:16]).then_inc(sem["k_out"], 16)
            split_low("inputs")
            for i in POOL_BACKS:
                u_back(pool, i)
            pool_steps = [0]

            def then(ins):
                pool_steps[0] += 1
                ins.then_inc(sem["pool_step"], 1)
                pool.wait_ge(sem["pool_step"], pool_steps[0])

            filled(pool, ("wt", 23))
            for bl in range(3):
                if bl == 2:
                    filled(pool, "z", 7)
                    pool.memset(ring[:, chunk_at["sbuf"] % SLOTS, :], 0.0).then_inc(sem["states_zero"], 1)
                make_ca(pool, then, bl, g2, "ca_by_pool", 2 * bl + 2)
            for i in (0, 2, 4):
                y_back(pool, i)
            split_low("even")
            split_low("odd")

        @block.tensor
        def _(pe):
            def mm(o, l, r, first, last):
                return pe.matmul(o, l, r, start=first, stop=last)

            def linear(stage, i, w, col, m, rhs, ready=None, kt=DT, stride=512):
                ps = bank_free(pe, stage, i)
                wv = w.rearrange("p (j n) -> p j n", n=stride)
                for j in range(kt):
                    if ready is not None:
                        ready(j)
                    ins = mm(ps[0:m, :], wv[:, j, col:col + m], rhs(j), j == 0, j == kt - 1)
                return ins.then_inc(sem["tile_filled"], 1)

            def parts(name):
                for engine, names in (("dve", LOW_BY_DVE), ("pool", LOW_BY_POOL)):
                    if name in names:
                        pe.wait_ge(sem["low_by_" + engine], names.index(name) + 1)
                return r(high(name)), r(unsplit(name))

            def split_linear(stage, i, name, col, hi, lo, ready):
                ps = bank_free(pe, stage, i)
                w_hi, w_lo = parts(name)
                o = ps[:, 0:hi.shape[2]]
                for j in range(DT):
                    ready(j)
                    mm(o, w_hi[:, j, col:col + P], r(hi[:, j, :]), j == 0, False)
                    mm(o, w_hi[:, j, col:col + P], r(lo(j)), False, False)
                    ins = mm(o, w_lo[:, j, col:col + P], r(hi[:, j, :]), False, j == DT - 1)
                return ins.then_inc(sem["tile_filled"], 1)

            def natural(stage, i, w, n, lhs, ready=None):
                ps = bank_free(pe, stage, i)
                wv = w.rearrange("p (j n) -> p j n", n=512)
                for j in range(DT):
                    if ready is not None:
                        ready(j)
                    ins = mm(ps[:, 0:n], lhs(j), wv[:, j, 0:n], j == 0, j == DT - 1)
                return ins.then_inc(sem["tile_filled"], 1)

            def ssq(name, of=hT):
                ps = bank_free(pe, name + "_ssq")
                pe.wait_ge(sem["ones_set"], 2)
                for j in range(DT):
                    pe.wait_ge(sem[name + "_squares"], j + 1)
                    ins = mm(ps[:, :], ones[:, :], of[:, j, :], j == 0, j == DT - 1)
                ins.then_inc(sem["tile_filled"], 1)

            def normed(name):
                return lambda j: pe.wait_ge(sem[name + "_normed"], j + 1)

            def h(j):
                return hT[:, j, :]

            pe.wait_ge(sem["ident_in"], 16)
            pe.wait_ge(sem["vec_in"], 16 * (len(VEC_ROWS) + 2))
            for i, (rows, n) in enumerate(((vec, VEC_N), (adab, 48), (skip, GROUPS))):
                ps = bank_free(pe, "vec", i)
                pe.transpose(ps[0:rows.shape[1], 0:n], rows[0:n, :], ident[0:n, 0:n]).then_inc(sem["tile_filled"], 1)
            pe.wait_ge(sem["x_in"], 16 * TT)
            for j in range(DT):
                ps = bank_free(pe, "xin", j)
                for t in range(TT):
                    ins = pe.transpose(ps[:, P * t:P * t + P], xnat[:, t, P * j:P * j + P], ident[:, :])
                ins.then_inc(sem["tile_filled"], 1)
            ssq("mix")
            w = weights(pe, "kv")
            for t in range(TT):
                natural("ckv", t, w, 136, lambda j: hT[:, j, P * t:P * t + P], normed("mix"))
            for i in range(2):
                linear("kir", i, w, 136 + 128 * i, P, h)
            pe.wait_ge(sem["tables_in"], 16 * 5)

            def swap(stage, i, raw, which):
                taken(pe, stage, i)
                ps = bank_free(pe, stage + "p", i)
                mm(ps[:, :], perm[:, which, :], raw, True, True).then_inc(sem["tile_filled"], 1)

            for i in range(2):
                swap("kir", i, tmp[:, i, :], i)
            pe.wait_ge(sem["ckv_normed"], TT)
            ps = bank_free(pe, "ckvT")
            for t in range(TT):
                ins = pe.transpose(ps[:, P * t:P * t + P], ckvn[:, t, :], ident[:, :])
            ins.then_inc(sem["tile_filled"], 1)

            def mix_low(j):
                pe.wait_ge(sem["mix_low"], j + 1)

            def rope_proj(stage, n, which, base):
                w = weights(pe, stage)
                for i in range(n + 1):
                    if i < n:
                        if stage == "qi":
                            linear(stage, i, w, 128 * i, P, h)
                        else:
                            split_linear(stage, i, f"{stage}:{i // 2}", 128 * (i % 2), nHi, h, mix_low)
                    if i >= 1:
                        swap(stage, i - 1, tmp[:, (base + i - 1) % 4, :], which)

            rope_proj("qi", 4, 0, 2)
            for n in range(24):
                b, hd = 1 + n // 8, n % 8
                if n == 0:
                    taken(pe, "qip", 3)
                    taken(pe, "kirp", 1)
                ps = bank_free(pe, "idx", n)
                rows = slice(64 * (hd % 2), 64 * (hd % 2) + 64)
                mm(ps[:, 0:P * (b + 1)], qiT[rows, hd // 2, P * b:P * b + P], kiT[rows, 0:P * (b + 1)], True, True)\
                    .then_inc(sem["tile_filled"], 1)
            rope_proj("qr", 2, 1, 6)
            for i in range(4):
                split_linear("qn", i, f"qn:{i // 2}", 128 * (i % 2), nHi, h, mix_low)
            rope_proj("qb", 4, 0, 8)
            rope_proj("kb", 4, 0, 12)
            for t in range(TT):
                ps = bank_free(pe, "vb", t)
                for half in range(2):
                    w_hi, w_lo = parts(f"vb:{half}")
                    o = ps[:, 256 * half:256 * half + 256]
                    for j in range(DT):
                        h_hi, h_lo = [r(v[:, j, P * t:P * t + P]) for v in (nHi, hT)]
                        mm(o, h_hi, w_hi[:, j, :], j == 0, False)
                        mm(o, h_lo, w_hi[:, j, :], False, False)
                        ins = mm(o, h_hi, w_lo[:, j, :], False, j == DT - 1)
                ins.then_inc(sem["tile_filled"], 1)
            w = weights(pe, "mla")
            for hd in range(HEADS):
                taken(pe, "qn", hd // 2)
                ps = bank_free(pe, "qlat", hd)
                rows = slice(64 * (hd % 2), 64 * (hd % 2) + 64)
                mm(ps[:, :], w[rows, 128 * (hd // 2):128 * (hd // 2) + 128], qnT[rows, hd // 2, :], True, True)\
                    .then_inc(sem["tile_filled"], 1)

            taken(pe, "kbp", 3)
            taken(pe, "vb", 3)
            for s in range(len(us) + LAG_V):
                if s < len(us):
                    kind, b, hd = us[s]
                    keys = P * (b + 1)
                    ps = bank_free(pe, ("S", s))
                    if kind == "B":
                        rows = slice(64 * (hd % 2), 64 * (hd % 2) + 64)
                        mm(ps[:, 0:keys], qbT[rows, hd // 2, P * b:P * b + P], kbT[rows, hd // 2, 0:keys], True, True)\
                            .then_inc(sem["tile_filled"], 1)
                    else:
                        if b == 0:
                            taken(pe, "qlat", hd)
                        rows = slice(32 * (hd % 4), 32 * (hd % 4) + 32)
                        mm(ps[:, 0:keys], qlatT[:, hd, P * b:P * b + P], ckvT[:, 0:keys], True, False)
                        pe.matmul(ps[:, 0:keys], qrT[rows, hd // 4, P * b:P * b + P], krT[rows, 0:keys], start=False,
                                  stop=True, tile_position=(32 * (hd % 4), 0)).then_inc(sem["tile_filled"], 1)
                u = s - LAG_T
                if 0 <= u < len(us):
                    pe.wait_ge(sem["prob_scaled"], u + 1)
                    ps = bank_free(pe, ("T", u))
                    for kb in range(us[u][1] + 1):
                        ins = pe.transpose(ps[:, P * kb:P * kb + P], prob[:, u % 4, P * kb:P * kb + P], ident[:, :])
                    ins.then_inc(sem["tile_filled"], 1)
                u = s - LAG_V
                if u < 0:
                    continue
                kind, b, hd = us[u]
                if kind == "B":
                    taken(pe, ("T", u))
                    if hd == 0 and b >= 2:
                        pe.wait_ge(sem["dilated_taken"], b - 1)
                    rows = slice(64 * (hd % 2), 64 * (hd % 2) + 64)
                    for kb in range(b + 1):
                        ins = mm(bank[6 + b % 2][rows, P * (hd // 2):P * (hd // 2) + P],
                                 vnat[:, kb, 64 * hd:64 * hd + 64], PTB[:, u % 2, P * kb:P * kb + P], kb == 0, kb == b)
                    ins.then_inc(sem["dilated_out"], 1)
                elif hd % 4 == 3:
                    n = 2 * b + hd // 4
                    taken(pe, ("T", u))
                    if n < 2:
                        pe.wait_ge(sem["dilated_taken"], 3 + n)
                    else:
                        pe.wait_ge(sem["latent_taken"], n - 1)
                    for kb in range(b + 1):
                        ins = mm(bank[6 + n % 2][:, :], ckvn[:, kb, :],
                                 PTA[:, kb, hd - 3:hd + 1, :], kb == 0, kb == b)
                    ins.then_inc(sem["latent_out"], 1)
            pe.wait_ge(sem["latent_taken"], 8)
            for i in range(4):
                ps = bank_free(pe, "oa", i)
                for e in range(2):
                    ins = mm(ps[64 * e:64 * e + 64, :], w[:, 512 + 64 * (2 * i + e):576 + 64 * (2 * i + e)],
                             olatT[:, 2 * i + e, :], True, True)
                ins.then_inc(sem["tile_filled"], 1)
            taken(pe, "oa", 3)

            def proj(stage, names, rhs, ready=None):
                for i in range(DT):
                    if i % 4 == 0:
                        w = weights(pe, names[i // 4])
                    linear(stage, i, w, 128 * (i % 4), P, rhs, ready if i == 0 else None)

            proj("out", ("out0", "out1"), h)
            pe.wait_ge(sem["mem_scaled"], 2)
            for j in range(DT):
                ps = bank_free(pe, "memT", j)
                for t in range(2):
                    ins = pe.transpose(ps[:, P * t:P * t + P], memn[:, t, P * j:P * j + P], ident[:, :])
                ins.then_inc(sem["tile_filled"], 1)
            for i in range(DT):
                if i == 4:
                    ssq("cross")
                split_linear("kc", i, f"kc{i // 4}", 128 * (i % 4), mHi, lambda j: mT[:, j, :], lambda j: taken(pe, "memT", j))
            for c in range(2):
                w_hi, w_lo = parts(f"vc{c}")
                for t in range(2):
                    ps = bank_free(pe, "vc", 2 * c + t)
                    for j in range(DT):
                        m_hi, m_lo = [r(v[:, j, P * t:P * t + P]) for v in (mHi, mT)]
                        mm(ps[:, :], m_hi, w_hi[:, j, :], j == 0, False)
                        mm(ps[:, :], m_lo, w_hi[:, j, :], False, False)
                        ins = mm(ps[:, :], m_hi, w_lo[:, j, :], False, j == DT - 1)
                    ins.then_inc(sem["tile_filled"], 1)
            for i in range(DT):
                split_linear("qc", i, f"qc{i // 4}", 128 * (i % 4), cHi, lambda j: hT[:, j, :], lambda j: pe.wait_ge(sem["cross_low"], j + 1))
            for s in range(16 + 3):
                if s < 16:
                    hd, b = s // 4, s % 4
                    taken(pe, "qc", 2 * hd + 1)
                    taken(pe, "kc", 7)
                    ps = bank_free(pe, ("CS", s))
                    for e in range(2):
                        ins = mm(ps[:, 0:MEM], qcT[:, 2 * hd + e, P * b:P * b + P], kcT[:, 2 * hd + e, :], e == 0, e == 1)
                    ins.then_inc(sem["tile_filled"], 1)
                u = s - 2
                if 0 <= u < 16:
                    pe.wait_ge(sem["cross_scaled"], u + 1)
                    ps = bank_free(pe, ("CT", u))
                    for kb in range(2):
                        ins = pe.transpose(ps[:, P * kb:P * kb + P], cprob[:, u % 4, P * kb:P * kb + P], ident[:, :])
                    ins.then_inc(sem["tile_filled"], 1)
                u = s - 3
                if u >= 0 and u % 4 == 3:
                    hd = u // 4
                    taken(pe, ("CT", u))
                    if hd >= 1:
                        pe.wait_ge(sem["cross_taken"], 2 * hd)
                    for e in range(2):
                        for kb in range(2):
                            ins = mm(bank[6 + e][:, :], vcn[:, kb, 256 * hd + 128 * e:256 * hd + 128 * e + 128],
                                     CPT[:, hd % 2, kb, :], kb == 0, kb == 1)
                        ins.then_inc(sem["cross_out"], 1)
            pe.wait_ge(sem["cross_taken"], 8)
            for i in range(DT):
                split_linear("oc", i, f"oc{i // 4}", 128 * (i % 4), cHi, lambda j: hT[:, j, :], lambda j: None)
            ssq("mlp")
            def ada_tile(n):
                ps = bank_free(pe, ("ada", n))
                conds = 2 if n < 6 else 1
                pe.wait_ge(sem["ada_summed"], n + 1)
                for q in range(4):
                    for c in range(conds):
                        ins = mm(ps[:, 2 * q + c:2 * q + c + 1], part[:, c, P * q:P * q + P], ones[:, 0:1], True, True)
                ins.then_inc(sem["tile_filled"], 1)

            def down(i):
                w = weights(pe, f"dn{i}").rearrange("p (j n) -> p j n", n=D)
                for m in range(DT):
                    ps = bank_free(pe, ("down", 8 * i + m))
                    for j in range(4):
                        if m == 0:
                            pe.wait_ge(sem["relu_squared"], 4 * i + j + 1)
                        ins = mm(ps[:, :], w[:, j, P * m:P * m + P], uT[:, i % 2, j, :], j == 0, j == 3)
                    ins.then_inc(sem["tile_filled"], 1)

            def split_down(i):
                for m in range(DT):
                    w_hi, w_lo = parts(f"dn{i}:{m // 4}")
                    ps = bank_free(pe, ("down", 8 * i + m))
                    at = slice(P * (m % 4), P * (m % 4) + P)
                    for j in range(4):
                        if m == 0:
                            pe.wait_ge(sem["hidden_low"], 4 * (i - 1) + j + 1)
                        mm(ps[:, :], w_hi[:, j, at], hid_r(i, j), j == 0, False)
                        mm(ps[:, :], w_hi[:, j, at], ro(uT[:, i % 2, j, :]), False, False)
                        ins = mm(ps[:, :], w_lo[:, j, at], hid_r(i, j), False, j == 3)
                    ins.then_inc(sem["tile_filled"], 1)

            for i in range(8):
                for j in range(4):
                    if i < 3:
                        linear(("up", 4 * i + j), 0, weights(pe, f"up{i}"), 128 * j, P, h, normed("mlp"))
                    else:
                        split_linear(("up", 4 * i + j), 0, f"up{i}:{j // 2}", 128 * (j % 2), uHi, lambda j: hT[:, j, :],
                                     lambda j: pe.wait_ge(sem["mlp_low"], j + 1))
                ada_tile(ADA_AFTER_UP[i])
                if i >= 2:
                    split_down(i - 1)
                elif i:
                    down(i - 1)
                if i in ADA_AFTER_DOWN:
                    ada_tile(ADA_AFTER_DOWN[i])
                if i == 1:
                    pe.wait_ge(sem["c_in"], 16 * 24)
                    for q in range(3):
                        ps = bank_free(pe, "cT", q)
                        for k in range(4):
                            ins = pe.transpose(ps[:, P * k:P * k + P], cn[:, 4 * q + k, :], ident[:, :])
                        ins.then_inc(sem["tile_filled"], 1)
                    pe.wait_ge(sem["poles_ready"], 1)
                    for q in range(2):
                        ps = bank_free(pe, "lamT", q)
                        for k in range(10):
                            ins = pe.transpose(ps[:, DK * k:DK * k + DK], pwn[:, 10 * q + k, :], ident[0:DK, 0:DK])
                        ins.then_inc(sem["tile_filled"], 1)
                if i >= 2:
                    bl = i - 2
                    pe.wait_ge(sem["cb_ready"], 4)
                    pe.wait_ge(sem["g_ready"], bl + 1)
                    ps = bank_free(pe, ("kk", bl))
                    for k in range(8):
                        for c in range(2):
                            ins = mm(ps[:, 32 * k:32 * k + 32], Gk[:, c, k, :], cb[:, 8 * bl + k, c, :],
                                     c == 0, c == 1)
                    ins.then_inc(sem["tile_filled"], 1)
                if i == 5:
                    pe.wait_ge(sem["ctx_in"], 16)
                    for q in range(4):
                        ps = bank_free(pe, "ctxT", q)
                        for k in range(4):
                            j, t = 2 * q + k // 2, k % 2
                            ins = pe.transpose(ps[:, P * k:P * k + P], ctxn[:, t, P * j:P * j + P], ident[:, :])
                        ins.then_inc(sem["tile_filled"], 1)
                    ps = bank_free(pe, "ctx_ssq")
                    for j in range(DT):
                        pe.wait_ge(sem["ctx_squares"], j + 1)
                        ins = mm(ps[:, 0:CTX], ones[:, :], hcT[:, j, :], j == 0, j == DT - 1)
                    ins.then_inc(sem["tile_filled"], 1)
            split_down(7)

            ssq("fin")
            for i in range(6):
                w = weights(pe, f"ev{i // 4}").rearrange("p (j n) -> p j n", n=512)
                ps = bank_free(pe, "uc", i)
                for j in range(DT):
                    pe.wait_ge(sem["ctx_normed"], j + 1)
                    ins = mm(ps[:, 0:CTX], w[:, j, 128 * (i % 4):128 * (i % 4) + 128], hcT[:, j, :], j == 0, j == DT - 1)
                ins.then_inc(sem["tile_filled"], 1)
            ssq("ev")
            for i in range(8):
                stage, k = ("ul", i) if i < 6 else ("ub", i - 6)
                split_linear(stage, k, f"ev{i // 4}:{i // 2 % 2}", 128 * (i % 2), vHi, h,
                             lambda j: pe.wait_ge(sem["ev_low"], j + 1))
            W = weights(pe, "wbuf").rearrange("p (r k c n) -> p r k c n", r=2, k=8, c=2)
            for bl in range(7):
                if bl < 6:
                    pe.wait_ge(sem["g_ready"], 7 + bl)
                    for q in range(4):
                        ps = bank_free(pe, ("wt", 4 * bl + q))
                        for i in range(4):
                            k, c = 2 * q + i // 2, i % 2
                            ins = pe.transpose(ps[:, P * i:P * i + P], input_matrices(bl, c)[:, k, :], ident[:, :])
                        ins.then_inc(sem["tile_filled"], 1)
                if bl >= 1:
                    for i in range(2):
                        pe.wait_ge(sem[f"u_in{2 * ((bl - 1) % 3) + i}"], 16 * CH)
                    for q in range(4):
                        taken(pe, ("wt", 4 * (bl - 1) + q))
                        ps = bank_free(pe, ("v", 4 * (bl - 1) + q))
                        for k in (2 * q, 2 * q + 1):
                            pair = (8 * (bl - 1) + k) % PAIRS
                            for c in range(2):
                                for e in range(2):
                                    at = 192 * (k % 2) + 96 * c
                                    ins = mm(ps[64 * e:64 * e + 64, at:at + NCH], W[:, (bl - 1) % 2, k, c, 64 * e:64 * e + 64],
                                             U[:, 2 * pair + e, :], True, True)
                        ins.then_inc(sem["tile_filled"], 1)
            w = weights(pe, "fch")
            pe.wait_ge(sem["fch_zero"], 1)
            for t in range(TT):
                ps = bank_free(pe, "pq", t)
                for i in range(2):
                    taken(pe, "ub", i)
                    ins = mm(ps[:, 256 * i:256 * i + 256], ubT[:, i, P * t:P * t + P], w[:, 0:256], True, True)
                ins.then_inc(sem["tile_filled"], 1)
            d = weights(pe, "dft").rearrange("p (t w n) -> p t w n", t=TT, w=2)
            for i in range(2):
                ps = bank_free(pe, "ft", i)
                for t in range(TT):
                    taken(pe, "pq", t)
                    for c in range(2):
                        ins = mm(ps[:, :], pq[:, t, i, P * c:P * c + P], d[:, t, c, :], t == 0 and c == 0,
                                 t == TT - 1 and c == 1)
                ins.then_inc(sem["tile_filled"], 1)
            for i in range(2):
                taken(pe, "ft", i)
                ps = bank_free(pe, "yb", i)
                mm(ps[:, :], w[:, 256 + P * i:256 + P * i + P], ftT[:, i, :], True, True).then_inc(sem["tile_filled"], 1)
            pe.wait_ge(sem["h_restored"], DT)
            for i in range(DT):
                linear("z", i, weights(pe, f"ev{2 + i // 4}"), 128 * (i % 4), P, h)
            span = ring[:, 0:2, :].rearrange("p s n -> p (s n)")[:, 0:CH * 768].rearrange("p (g n) -> p g n", g=GROUPS)
            for bl in range(6):
                ps = bank_free(pe, "ys", bl)
                weights(pe, "Ta" if bl < 4 else "Tb")
                for k in range(8):
                    ins = mm(ps[:, NLAT * k:NLAT * k + NLAT], span[:, 8 * bl + k, :], U[:, 8 * bl + k, NCTX:], k == 0, False)
            ins.then_inc(sem["chunk_products_done"], 1)
            for bl in range(6):
                ps = bank_free(pe, "ys", bl)
                pe.wait_ge(sem["states_placed"], 4 * (bl + 1))
                if bl < 3:
                    pe.wait_ge(sem["ca_by_pool"], 4 * (bl + 1))
                else:
                    pe.wait_ge(sem["ca_by_dve"], 4 * (bl - 2))
                for k in range(4):
                    for d in range(2):
                        for c in range(2):
                            ins = pe.matmul(ps[:, P * k:P * k + P], output_matrices(bl, c)[:, 4 * d + k, :],
                                            pairS[:, bl % 2, d, c, k, :, :].rearrange("p e n -> p (e n)"),
                                            start=False, stop=(k == 3 and d == 1 and c == 1))
                ins.then_inc(sem["tile_filled"], 1)
            for i in range(6):
                w = weights(pe, f"glu{i // 3}")
                linear("glu", i, w[:, 0:2304], 128 * (i % 3), P, lambda j: yg[:, j, :],
                       lambda j: pe.wait_ge(sem["gelu_done"], j + 1), kt=6, stride=384)

            for i in range(DT):
                split_linear("eo", i, f"eo{i // 4}", 128 * (i % 4), ro(eHi), lambda j: hT[:, j, :] if j < 6 else ro(zT[:, j, :]),
                             lambda j: pe.wait_ge(sem["e_low"], 2 + j + 1 if j < 6 else j - 5))
            ssq("od")
            for n, (stage, k) in enumerate((("pool", 4), ("cg", 4), ("xp", 4), ("bg", 4), ("zo", 8))):
                if stage == "zo":
                    w = weights(pe, "pw")
                    for i in range(4):
                        pe.wait_ge(sem["pooled"], i + 1)
                        ps = bank_free(pe, "pm", i)
                        mm(ps[:, :], w[:, P * i:P * i + P], pooled[:, i, :], True, True).then_inc(sem["tile_filled"], 1)
                for i in range(k):
                    split_linear(stage, i, f"od{n + i // 4}", 128 * (i % 4), hHi, lambda j: hT[:, j, :],
                                 lambda j: pe.wait_ge(sem["od_low"], j + 1))
            for i in range(DT):
                split_linear("oo", i, f"oo{i // 4}", 128 * (i % 4), ro(yHi), lambda j: ro(zoT[:, j, :]),
                             lambda j: pe.wait_ge(sem["y_low"], j + 1))
            ssq("end", hHi)
            for q in range(DT):
                t, half = q // 2, q % 2
                ps = bank_free(pe, "yout", q)
                for i in range(4):
                    j = 4 * half + i
                    pe.wait_ge(sem["end_normed"], j + 1)
                    ins = pe.transpose(ps[:, P * i:P * i + P], hT[:, j, P * t:P * t + P], ident[:, :])
                ins.then_inc(sem["tile_filled"], 1)

        @block.scalar
        def _(act):
            TA = sem["taken_by_act"]

            def split_high(name):
                phase = next(k for k, names in SPLITS.items() if name in names)
                n = SPLITS[phase].index(name)
                if n >= len(HIGH_AT[phase]):
                    chunk_used(act, SPLITS[phase][n - len(HIGH_AT[phase])])
                weights(act, name.partition(":")[0])
                act.activation(r(high(name)), unsplit(name), ACT.Copy).then_inc(sem["weights_high"], 1)

            def squares(name, ready, to=hT):
                for j in range(DT):
                    ready(j)
                    act.activation(to[:, j, :], xT[:, j, :], ACT.Square).then_inc(sem[name + "_squares"], 1)

            def root(name):
                ps = filled(act, name + "_ssq")
                act.activation(std[:, :], ps[:, :], ACT.Sqrt, scale=1.0 / D, bias=eps[:, 0:1]).then_inc(TA, 1)

            def copy(stage, i, dst, scale=1.0, m=P, n=512):
                ps = filled(act, stage, i)
                act.activation(dst, ps[0:m, 0:n], ACT.Copy, scale=scale).then_inc(TA, 1)

            for t in range(TT):
                act.dma_start(xnat[:, t, :], A["x"][0, P * t:P * t + P, :]).then_inc(sem["x_in"], 16)
            copy("vec", 0, vecT[:, 0:VEC_N], n=VEC_N)
            copy("vec", 1, adabT[:, :], n=48)
            copy("vec", 2, skipT[:, :], m=16, n=GROUPS)
            for j in range(DT):
                copy("xin", j, xT[:, j, :])
            act.wait_ge(sem["ones_set"], 2)
            squares("mix", lambda j: taken(act, "xin", j))
            root("mix")
            for t in range(TT):
                ps = filled(act, "ckv", t)
                act.activation(wnat[:, t, :], ps[:, 128:136], ACT.Copy, scale=float(8 ** -0.5 * 64 ** -0.5))
                act.activation(ckvn[:, t, :], ps[:, 0:128], ACT.Copy).then_inc(TA, 1)
            for i in range(2):
                copy("kir", i, tmp[:, i, :])
            for t in range(TT):
                taken(act, "ckv", t)
                if t >= 1:
                    act.wait_ge(sem["ckv_squares"], t)
                act.activation(tmp[:, 3, 0:128], ckvn[:, t, :], ACT.Square, accum_out=stat[:, 0, t:t + 1])\
                    .then_inc(sem["ckv_squares"], 1)
            act.wait_ge(sem["ckv_squares"], TT)
            act.activation(stat[:, 1, 0:TT], stat[:, 0, 0:TT], ACT.Sqrt, scale=1.0 / 128, bias=eps[:, 0:1])\
                .then_inc(sem["ckv_root"], 1)
            copy("ckvT", 0, ckvT)

            def rope_copy(stage, n, base):
                for i in range(n):
                    if base + i >= 4:
                        roped(act, base + i - 4)
                    copy(stage, i, tmp[:, (base + i) % 4, :])
                    if stage != "qi" and i % 2:
                        next_high()

            heads_left = SPLITS["heads"][2:]

            def next_high():
                if heads_left:
                    split_high(heads_left.pop(0))

            for j in range(DT):
                act.wait_ge(sem["mix_normed"], j + 1)
                act.activation(r(nHi[:, j, :]), hT[:, j, :], ACT.Copy).then_inc(sem["mix_high"], 1)
            rope_copy("qi", 4, 2)
            split_high("qr:0")
            for n in range(24):
                b = 1 + n // 8
                ps = filled(act, "idx", n)
                if n < 4:
                    roped(act, 2 + n)
                else:
                    act.wait_ge(sem["index_added"], n - 3)
                act.activation(tmp[:, n % 4, 0:P * (b + 1)], ps[:, 0:P * (b + 1)], ACT.Relu).then_inc(TA, 1)
                if n == 8:
                    split_high("qn:0")
            act.wait_ge(sem["index_added"], 24)
            rope_copy("qr", 2, 6)
            for i in range(4):
                copy("qn", i, qnT[:, i, :])
                if i % 2:
                    next_high()
            rope_copy("qb", 4, 8)
            rope_copy("kb", 4, 12)
            for t in range(TT):
                copy("vb", t, vnat[:, t, :])
            for hd in range(HEADS):
                copy("qlat", hd, qlatT[:, hd, :])
            for s in range(len(us) + LAG_V):
                u = s - 1
                if 0 <= u < len(us):
                    kind, b, hd = us[u]
                    keys = P * (b + 1)
                    act.wait_ge(sem["neg_max"], u + 1)
                    act.activation(prob[:, u % 4, 0:keys], prob[:, u % 4, 0:keys], ACT.Exp, bias=stat[:, 1, u:u + 1],
                                   scale=SCALE_A if kind == "A" else SCALE_B,
                                   accum_out=stat[:, 2, u:u + 1]).then_inc(sem["exp_done"], 1)
                u = s - LAG_T
                if 0 <= u < len(us):
                    kind, b, hd = us[u]
                    ps = filled(act, ("T", u))
                    if kind == "B":
                        if u >= 2:
                            act.wait_ge(sem["dilated_out"], u - 1)
                        else:
                            roped(act, 15)
                        dst = PTB[:, u % 2, 0:P * (b + 1)]
                        act.activation(dst, ps[:, 0:P * (b + 1)], ACT.Copy).then_inc(TA, 1)
                    else:
                        if b >= 1:
                            act.wait_ge(sem["latent_out"], 2 * b - 1 + hd // 4)
                        dst = PTA[:, 0:b + 1, hd, :]
                        act.activation(dst, ps[:, 0:P * (b + 1)].rearrange("p (k q) -> p k q", q=P), ACT.Copy)\
                            .then_inc(TA, 1)
            for i in range(4):
                copy("oa", i, hT[:, i, :])
            act.wait_ge(sem["mem_in"], 16)
            taken(act, "oa", 3)
            for t in range(2):
                if t:
                    act.wait_ge(sem["mem_squares"], t)
                act.activation(area(8192, D), memn[:, t, :], ACT.Square, accum_out=stat[:, 0, t:t + 1])\
                    .then_inc(sem["mem_squares"], 1)
            act.wait_ge(sem["mem_squares"], 2)
            act.activation(stat[:, 1, 0:2], stat[:, 0, 0:2], ACT.Sqrt, scale=1.0 / D, bias=eps[:, 0:1])\
                .then_inc(sem["mem_root"], 1)
            act.wait_ge(sem["mem_rstd"], 1)
            for t in range(2):
                act.activation(memn[:, t, :], memn[:, t, :], ACT.Copy, scale=stat[:, 2, t:t + 1])\
                    .then_inc(sem["mem_scaled"], 1)
            split_high("kc0")
            split_high("kc1")
            filled(act, "out", 7)
            squares("cross", lambda j: taken(act, "out", j))
            for i in range(DT):
                copy("kc", i, kcT[:, i, :], n=MEM)
                if i == 3:
                    root("cross")
                    split_high("vc0")
                    for j in range(DT):
                        act.wait_ge(sem["cross_normed"], j + 1)
                        act.activation(r(cHi[:, j, :]), hT[:, j, :], ACT.Copy).then_inc(sem["cross_high"], 1)
            split_high("vc1")
            for c in range(2):
                for t in range(2):
                    copy("vc", 2 * c + t, vcn[:, t, 512 * c:512 * c + 512])
                split_high(f"qc{c}")
            for i in range(DT):
                copy("qc", i, qcT[:, i, :])
                if i % 4 == 3:
                    split_high(f"oc{i // 4}")
            for s in range(16 + 3):
                u = s - 1
                if 0 <= u < 16:
                    act.wait_ge(sem["cross_neg_max"], u + 1)
                    act.activation(cprob[:, u % 4, :], cprob[:, u % 4, :], ACT.Exp, bias=stat[:, 1, u:u + 1],
                                   scale=SCALE_C, accum_out=stat[:, 2, u:u + 1]).then_inc(sem["cross_exp"], 1)
                u = s - 2
                if 0 <= u < 16:
                    hd, b = u // 4, u % 4
                    ps = filled(act, ("CT", u))
                    if hd >= 2:
                        act.wait_ge(sem["cross_out"], 2 * (hd - 1))
                    act.activation(CPT[:, hd % 2, :, P * b:P * b + P], ps[:, 0:MEM].rearrange("p (k q) -> p k q", q=P),
                                   ACT.Copy).then_inc(TA, 1)
            filled(act, "oc", 7)
            squares("mlp", lambda j: taken(act, "oc", j))
            root("mlp")
            act.activation(cond[:, 0, :], vecT[:, VEC["c_2"]:VEC["c_2"] + DT], ACT.Silu)
            act.activation(cond[:, 1, :], vecT[:, VEC["c_ctx_2"]:VEC["c_ctx_2"] + DT], ACT.Silu)\
                .then_inc(sem["cond_ready"], 1)
            def hidden(i):
                for j in range(4):
                    ps = filled(act, ("up", 4 * i + j))
                    if i >= 2:
                        filled(act, ("down", 8 * (i - 2) + 7))
                    act.activation(uT[:, i % 2, j, :], ps[:, :], ACT.Relu).then_inc(TA, 1)
                    if i >= 3 and j % 2:
                        split_high(f"dn{i - 1}:{j // 2}")

            def shift(name, buf, layer, c):
                for j in range(DT):
                    act.wait_ge(sem[name + "_scaled"], j + 1)
                    act.activation(buf[:, j, :], buf[:, j, :], ACT.Identity, bias=ada[:, layer, j, c:c + 1])\
                        .then_inc(sem[name + "_normed"], 1)

            def hidden_high(i):
                if 2 <= i < 7:
                    filled(act, ("down", 8 * (i - 1) + 7))
                for j in range(4):
                    act.wait_ge(sem["relu_squared"], 4 * i + j + 1)
                    act.activation(hid_r(i, j), uT[:, i % 2, j, :], ACT.Copy).then_inc(sem["hidden_high"], 1)

            for i in range(8):
                if i == 2:
                    split_high("dn1:0")
                    split_high("dn1:1")
                if i >= 2:
                    hidden_high(i - 1)
                hidden(i)
                if i == 2:
                    act.wait_ge(sem["bbar_ready"], 1)
                    for j in range(DT):
                        act.activation(r(uHi[:, j, :]), hT[:, j, :], ACT.Copy).then_inc(sem["mlp_high"], 1)
                if 2 <= i < 7:
                    split_high(f"up{i + 1}:0")
                    split_high(f"up{i + 1}:1")
                if i == 0:
                    act.wait_ge(sem["lam_in"], 16 * 3)
                    act.activation(stepn[:, :], stepn[:, :], ACT.Exp).then_inc(sem["step_ready"], 1)
                    act.wait_ge(sem["angle_ready"], 1)
                    act.activation(tmpn[0:DK, 2, :], tmpn[0:DK, 0, :], ACT.Exp)
                    act.activation(tmpn[0:DK, 3, :], tmpn[0:DK, 1, :], ACT.Sin, scale=0.5)
                    act.activation(tmpn[0:DK, 4, :], tmpn[0:DK, 1, :], ACT.Sin).then_inc(sem["sines_ready"], 1)
                if i == 1:
                    for q in range(3):
                        copy("cT", q, area(28160 + 512 * q, 512))
                    for q in range(2):
                        copy("lamT", q, area(25664 + 480 * q, 480), n=480)
                if i == 5:
                    for q in range(4):
                        copy("ctxT", q, ctxT[:, 2 * q:2 * q + 2, :].rearrange("p a n -> p (a n)"))
                    for j in range(DT):
                        taken(act, "ctxT", j // 2)
                        act.activation(hcT[:, j, :], ctxT[:, j, :], ACT.Square).then_inc(sem["ctx_squares"], 1)
                    ps = filled(act, "ctx_ssq")
                    act.activation(std2[:, :], ps[:, 0:CTX], ACT.Sqrt, scale=1.0 / D, bias=eps[:, 0:1]).then_inc(TA, 1)
            split_high("dn7:0")
            hidden_high(7)
            split_high("dn7:1")
            shift("ctx", hcT, 0, 1)
            squares("fin", lambda j: taken(act, ("down", 56 + j)))
            root("fin")
            act.wait_ge(sem["k_out"], 16 * (2 * CH - 1))
            split_high("ev0:0")
            split_high("ev0:1")

            def chunked(stage, i, at, n):
                ps = filled(act, stage, i)
                act.activation(uP[:, i, :, at:at + n], ps[:, 0:CH * n].rearrange("p (c t) -> p t c", t=CH), ACT.Copy)\
                    .then_inc(TA, 1)

            for i in range(6):
                chunked("uc", i, 0, NCTX)
            filled(act, "fin_ssq")
            squares("ev", lambda j: act.wait_ge(sem["pos_added"], j + 1))
            root("ev")
            for j in range(DT):
                act.wait_ge(sem["ev_scaled"], j + 1)
                act.activation(r(vHi[:, j, :]), hT[:, j, :], ACT.Identity, bias=ada[:, 0, j, 0:1])\
                    .then_inc(sem["ev_high"], 1)
            for i in range(6):
                chunked("ul", i, NCTX, NLAT)
                if i in (1, 3):
                    split_high(f"ev1:{i // 2}")
            for i in range(2):
                copy("ub", i, ubT[:, i, :])
            W = ring[:, chunk_at["wbuf"] % SLOTS, :].rearrange("p (r n) -> p r n", r=2)
            chunk_used(act, occupant(chunk_at["wbuf"]))
            for i in range(6):
                act.wait_ge(sem[f"u_out{i}"], 16)
            for bl in range(7):
                if bl < 6:
                    for q in range(4):
                        if bl >= 2:
                            filled(act, ("v", 4 * (bl - 2) + q))
                        copy(("wt", 4 * bl + q), 0, W[:, bl % 2, 512 * q:512 * q + 512])
                if bl >= 1:
                    for q in range(4):
                        ps = filled(act, ("v", 4 * (bl - 1) + q))
                        dk = 8 * (bl - 1) + 2 * q
                        V = Vf if dk < PAIRS else Vb
                        if dk == PAIRS:
                            act.wait_ge(sem["h_restored"], DT)
                        act.activation(V[:, :, dk % PAIRS:dk % PAIRS + 2, 0:NCH],
                                       ps[:, 0:384].rearrange("p (k c n) -> p c k n", k=2, c=2), ACT.Copy).then_inc(TA, 1)
            for t in range(TT):
                ps = filled(act, "pq", t)
                act.activation(pq[:, t, :, :].rearrange("p a n -> p (a n)"), ps[:, :], ACT.Copy).then_inc(TA, 1)
            for i in range(2):
                copy("ft", i, ftT[:, i, :])
            for i in range(2):
                copy("yb", i, ubT[:, i, :])
            act.wait_ge(sem["k_out"], 16 * (2 * CH - 1))
            for i in range(DT):
                ps = filled(act, "z", i)
                act.activation(zT[:, i, :], ps[:, :], ACT.Silu).then_inc(TA, 1)
            def place_states(bl):
                for e in range(2):
                    rows = slice(64 * e, 64 * e + 64)
                    for d, (V, at) in enumerate(((Vf, NCTX - 1), (Vb, NCTX + 1))):
                        act.activation(pairS[rows, bl % 2, d, :, :, e, :], V[rows, :, 4 * bl:4 * bl + 4, at:at + NLAT],
                                       ACT.Copy).then_inc(sem["states_placed"], 1)

            act.wait_ge(sem["scanned"], 1)
            act.wait_ge(sem["states_zero"], 1)
            place_states(0)
            place_states(1)
            for bl in range(6):
                ps = filled(act, "ys", bl)
                act.activation(Y[:, 8 * bl:8 * bl + 8, :], ps[:, :].rearrange("p (k n) -> p k n", k=8), ACT.Copy)\
                    .then_inc(TA, 1)
                if bl + 2 < 6:
                    place_states(bl + 2)
            for i in range(6):
                act.wait_ge(sem[f"ys_in{i}"], 16 * CH)
                act.activation(yg[:, i, :].rearrange("p (c t) -> p t c", t=CH)[:, ::-1, :],
                               yP[:, i, :].rearrange("p (t c) -> p t c", t=CH), ACT.Gelu_apprx_tanh)\
                    .then_inc(sem["gelu_done"], 1)
            for i in range(6):
                ps = filled(act, "glu", i)
                if i >= 2:
                    act.wait_ge(sem["glu_gated"], i - 1)
                act.activation(sg[:, i % 2, :], ps[:, :], ACT.Sigmoid, bias=g("s5_glu_b_2", i)).then_inc(TA, 1)
                if i == 0:
                    act.wait_ge(sem["ca_by_dve"], 12)
                    split_high("eo0")
                    act.wait_ge(sem["fnet_gated"], 2)
                    for j in (6, 7):
                        act.activation(ro(eHi[:, j, :]), zT[:, j, :], ACT.Copy).then_inc(sem["e_high"], 1)
                if i == 2:
                    split_high("eo1")
                if i >= 2:
                    act.activation(ro(eHi[:, i - 2, :]), hT[:, i - 2, :], ACT.Copy).then_inc(sem["e_high"], 1)
            for i in (4, 5):
                act.wait_ge(sem["glu_gated"], i + 1)
                act.activation(ro(eHi[:, i, :]), hT[:, i, :], ACT.Copy).then_inc(sem["e_high"], 1)

            split_high("od0")
            filled(act, "eo", 7)
            squares("od", lambda j: taken(act, "eo", j))
            root("od")
            for j in range(DT):
                act.wait_ge(sem["od_scaled"], j + 1)
                act.activation(r(hHi[:, j, :]), hT[:, j, :], ACT.Identity, bias=ada[:, 1, j, 0:1])\
                    .then_inc(sem["od_high"], 1)
            chunk_used(act, "eo1")
            split_high("od1")
            for i in range(4):
                copy("pool", i, gb[:, i, 8:8 + SEQ])
            for i in range(4):
                copy("cg", i, cgT[:, i, :])
                if i == 0:
                    split_high("od2")
            filled(act, "xp", 0)
            split_high("od3")
            for i in range(4):
                copy("bg", i, bgT[:, i, :])
                if i == 0:
                    split_high("od4")
            for i in range(DT):
                ps = filled(act, "zo", i)
                act.activation(zoT[:, i, :], ps[:, :], ACT.Silu).then_inc(TA, 1)
                if i == 0:
                    split_high("od5")
                if i == 4:
                    split_high("oo0")
                if i >= 1:
                    act.wait_ge(sem["odd_gated"], i)
                    act.activation(ro(yHi[:, i - 1, :]), zoT[:, i - 1, :], ACT.Copy).then_inc(sem["y_high"], 1)
            act.wait_ge(sem["odd_gated"], DT)
            act.activation(ro(yHi[:, DT - 1, :]), zoT[:, DT - 1, :], ACT.Copy).then_inc(sem["y_high"], 1)
            split_high("oo1")
            squares("end", lambda j: taken(act, "oo", j), hHi)
            root("end")
            for q in range(DT):
                t, half = q // 2, q % 2
                ps = filled(act, "yout", q)
                act.activation(onat[:, t, 512 * half:512 * half + 512], ps[:, :], ACT.Copy).then_inc(TA, 1)

        @block.vector
        def _(dve):
            TD = sem["taken_by_dve"]
            steps = [0]

            def mark(ins):
                steps[0] += 1
                ins.then_inc(sem["dve_step"], 1)
                return steps[0]

            def then(ins):
                dve.wait_ge(sem["dve_step"], mark(ins))

            def norm(name, gain, k=0, low=None):
                taken(dve, name + "_ssq")
                then(dve.reciprocal(std[:, :], std[:, :]))
                taken(dve, "vec", 2)
                for j in range(DT):
                    dve.scalar_tensor_tensor(out=hT[:, j, :], in0=xT[:, j, :], scalar=g(gain, k + j), in1=std[:, :],
                                             op0=ALU.mult, op1=ALU.mult).then_inc(sem[name + "_normed"], 1)
                    if low and j >= 2:
                        low(j - 2)
                if low:
                    low(DT - 2)
                    low(DT - 1)

            norm("mix", "norm_mix_g")
            dve.wait_ge(sem["tables_in"], 16 * 5)

            def rotate(stage, i, n, which, dst):
                raw = tmp[:, n % 4, :]
                taken(dve, stage, i)
                n = mark(dve.tensor_tensor(out=dst, in0=raw, in1=rope[:, 2 * which, :], op=ALU.mult))
                ps = filled(dve, stage + "p", i)
                dve.wait_ge(sem["dve_step"], n)
                then(dve.tensor_tensor(out=raw, in0=rope[:, 2 * which + 1, :], in1=ps[:, :], op=ALU.mult))
                dve.tensor_tensor(out=dst, in0=dst, in1=raw, op=ALU.add).then_inc(TD, 1)

            for i in range(2):
                rotate("kir", i, i, i, (kiT, krT)[i])
            dve.wait_ge(sem["ckv_root"], 1)
            then(dve.reciprocal(stat[:, 2, 0:TT], stat[:, 1, 0:TT]))
            for t in range(TT):
                dve.scalar_tensor_tensor(out=ckvn[:, t, :], in0=ckvn[:, t, :], scalar=stat[:, 2, t:t + 1], in1=kvg,
                                         op0=ALU.mult, op1=ALU.mult).then_inc(sem["ckv_normed"], 1)
            for i in range(4):
                rotate("qi", i, 2 + i, 0, qiT[:, i, :])
            for n in range(24):
                b, hd = 1 + n // 8, n % 8
                keys = P * (b + 1)
                taken(dve, "idx", n)
                o = work[:, b - 1, 0:keys]
                if hd == 0:
                    ins = dve.tensor_scalar(o, tmp[:, n % 4, 0:keys], wnat[:, b, hd:hd + 1], None, ALU.mult)
                else:
                    dve.wait_ge(sem["index_added"], n)
                    ins = dve.scalar_tensor_tensor(out=o, in0=tmp[:, n % 4, 0:keys], scalar=wnat[:, b, hd:hd + 1],
                                                   in1=o, op0=ALU.mult, op1=ALU.add)
                ins.then_inc(sem["index_added"], 1)

            for j in range(DT):
                dve.wait_ge(sem["mix_high"], j + 1)
                dve.tensor_tensor(out=r(hT[:, j, :]), in0=hT[:, j, :], in1=back(nHi[:, j, :]), op=ALU.subtract)\
                    .then_inc(sem["mix_low"], 1)

            def topk():
                for b in range(1, TT):
                    keys = P * (b + 1)
                    o = work[:, b - 1, 0:keys]
                    diag = work[:, b - 1, P * b:keys]
                    dve.wait_ge(sem["index_added"], 8 * b)
                    then(dve.tensor_tensor(out=diag, in0=diag, in1=causal, op=ALU.add))
                    for r in range(TOPK // 8):
                        then(dve.max(top8, o))
                        then(dve.match_replace(o, top8, o, TAKEN))
                        yield
                    then(dve.tensor_scalar(pick[:, b - 1, 0:keys], o, -2e38, OFF, ALU.is_ge, ALU.mult))

            rounds = topk()

            def some_rounds(n):
                for _ in range(n):
                    next(rounds, None)

            for i in range(2):
                rotate("qr", i, 6 + i, 1, qrT[:, i, :])
                some_rounds(4)
            for st, dst, base in (("qb", qbT, 8), ("kb", kbT, 12)):
                for i in range(4):
                    rotate(st, i, base + i, 0, dst[:, i, :])
                    some_rounds(5)
            for _ in rounds:
                pass

            def soften(u):
                keys = P * (us[u][1] + 1)
                dve.wait_ge(sem["exp_done"], u + 1)
                then(dve.reciprocal(stat[:, 3, u:u + 1], stat[:, 2, u:u + 1]))
                dve.tensor_scalar(prob[:, u % 4, 0:keys], prob[:, u % 4, 0:keys], stat[:, 3, u:u + 1], None, ALU.mult)\
                    .then_inc(sem["prob_scaled"], 1)

            for s in range(len(us) + LAG_V):
                if s < len(us):
                    kind, b, hd = us[s]
                    keys = P * (b + 1)
                    if s == 0:
                        taken(dve, "kbp", 3)
                    if s >= 4:
                        filled(dve, ("T", s - 4))
                    ps = filled(dve, ("S", s))
                    if kind == "B":
                        bias = dilated[:, P * (3 - b):512]
                    else:
                        bias = causal if b == 0 else pick[:, b - 1, 0:keys]
                    dve.tensor_tensor_reduce(prob[:, s % 4, 0:keys], bias, ps[:, 0:keys], 1.0, -3e38, ALU.add, ALU.max,
                                             stat[:, 0, s:s + 1]).then_inc(TD, 1)
                    taken(dve, ("S", s))
                    dve.tensor_scalar(stat[:, 1, s:s + 1], stat[:, 0, s:s + 1],
                                      -(SCALE_A if kind == "A" else SCALE_B), None, ALU.mult).then_inc(sem["neg_max"], 1)
                if 1 <= s <= len(us):
                    soften(s - 1)
                u = s - LAG_V
                if u < 0:
                    continue
                kind, b, hd = us[u]
                if kind == "B" and hd == 7:
                    dve.wait_ge(sem["dilated_out"], 8 * (b + 1))
                    dve.tensor_copy(hT[:, 4:8, P * b:P * b + P],
                                    bank[6 + b % 2][:, :].rearrange("p (g q) -> p g q", q=P))\
                        .then_inc(sem["dilated_taken"], 1)
                elif kind == "A" and hd % 4 == 3:
                    n = 2 * b + hd // 4
                    dve.wait_ge(sem["latent_out"], n + 1)
                    dve.tensor_copy(olatT[:, hd - 3:hd + 1, P * b:P * b + P],
                                    bank[6 + n % 2][:, :].rearrange("p (g q) -> p g q", q=P))\
                        .then_inc(sem["latent_taken"], 1)

            def add_residual(stage):
                for i in range(DT):
                    ps = filled(dve, stage, i)
                    dve.tensor_tensor(out=xT[:, i, :], in0=xT[:, i, :], in1=ps[:, :], op=ALU.add).then_inc(TD, 1)

            dve.wait_ge(sem["mem_root"], 1)
            dve.reciprocal(stat[:, 2, 0:2], stat[:, 1, 0:2]).then_inc(sem["mem_rstd"], 1)
            add_residual("out")
            for j in range(DT):
                ps = filled(dve, "memT", j)
                if j == 0:
                    taken(dve, "oa", 3)
                then(dve.tensor_scalar(r(mHi[:, j, :]), ps[:, 0:MEM], g("norm_mem_g", j), None, ALU.mult))
                dve.scalar_tensor_tensor(out=r(mT[:, j, :]), in0=ps[:, 0:MEM], scalar=g("norm_mem_g", j), in1=back(mHi[:, j, :]),
                                         op0=ALU.mult, op1=ALU.subtract).then_inc(TD, 1)
            taken(dve, "out", 7)

            def cross_low(j):
                dve.wait_ge(sem["cross_high"], j + 1)
                dve.tensor_tensor(out=r(hT[:, j, :]), in0=hT[:, j, :], in1=back(cHi[:, j, :]), op=ALU.subtract)\
                    .then_inc(sem["cross_low"], 1)

            norm("cross", "norm_cross_g", low=cross_low)
            weights_low(dve, "vc1")
            weights_low(dve, "qc1")
            for s in range(16 + 3):
                if s < 16:
                    if s >= 4:
                        filled(dve, ("CT", s - 4))
                    ps = filled(dve, ("CS", s))
                    dve.tensor_scalar(cprob[:, s % 4, :], ps[:, 0:MEM], 1.0, None, ALU.mult).then_inc(TD, 1)
                    taken(dve, ("CS", s))
                    then(dve.tensor_reduce(stat[:, 0, s:s + 1], cprob[:, s % 4, :], AX, ALU.max))
                    dve.tensor_scalar(stat[:, 1, s:s + 1], stat[:, 0, s:s + 1], -SCALE_C, None, ALU.mult)\
                        .then_inc(sem["cross_neg_max"], 1)
                u = s - 1
                if 0 <= u < 16:
                    dve.wait_ge(sem["cross_exp"], u + 1)
                    then(dve.reciprocal(stat[:, 3, u:u + 1], stat[:, 2, u:u + 1]))
                    dve.tensor_scalar(cprob[:, u % 4, :], cprob[:, u % 4, :], stat[:, 3, u:u + 1], None, ALU.mult)\
                        .then_inc(sem["cross_scaled"], 1)
                u = s - 3
                if u >= 0 and u % 4 == 3:
                    for e in range(2):
                        dve.wait_ge(sem["cross_out"], 2 * (u // 4) + e + 1)
                        k = 2 * (u // 4) + e
                        then(dve.tensor_copy(r(cHi[:, k, :]), bank[6 + e][:, :]))
                        dve.tensor_tensor(out=r(hT[:, k, :]), in0=bank[6 + e][:, :], in1=back(cHi[:, k, :]), op=ALU.subtract)\
                            .then_inc(sem["cross_taken"], 1)
            add_residual("oc")
            taken(dve, "oc", 7)
            norm("mlp", "norm_mlp_g")
            def sum_ada(n):
                w = weights(dve, f"ad{n}").rearrange("p (j n) -> p j n", n=512)
                dve.wait_ge(sem["cond_ready"], 1)
                conds = range(2 if n < 6 else 1)
                for j in range(DT):
                    for c in conds:
                        if j == 0:
                            ins = dve.tensor_scalar(part[:, c, :], w[:, j, :], cond[:, c, j:j + 1], None, ALU.mult)
                        else:
                            ins = dve.scalar_tensor_tensor(out=part[:, c, :], in0=w[:, j, :], scalar=cond[:, c, j:j + 1],
                                                           in1=part[:, c, :], op0=ALU.mult, op1=ALU.add)
                        if j < DT - 1:
                            step = mark(ins)
                    if j < DT - 1:
                        dve.wait_ge(sem["dve_step"], step)
                ins.then_inc(sem["ada_summed"], 1)

            def add_ada(n):
                layer, at = n // 6, 4 * (n % 6)
                conds = 2 if n < 6 else 1
                ps = filled(dve, ("ada", n))
                bias = adabT[:, 24 * layer + at:24 * layer + at + 4].unsqueeze(2).broadcast_to([P, 4, conds])
                dve.tensor_tensor(out=ada[:, layer, at:at + 4, 0:conds], in0=bias,
                                  in1=ps[:, 0:8].rearrange("p (a c) -> p a c", c=2)[:, :, 0:conds], op=ALU.add)\
                    .then_inc(TD, 1)

            def square_hidden(i):
                for j in range(4):
                    taken(dve, ("up", 4 * i + j))
                    u = uT[:, i % 2, j, :]
                    dve.tensor_tensor(out=u, in0=u, in1=u, op=ALU.mult).then_inc(sem["relu_squared"], 1)

            def add_down(i):
                for m in range(DT):
                    ps = filled(dve, ("down", 8 * i + m))
                    dve.tensor_tensor(out=xT[:, m, :], in0=xT[:, m, :], in1=ps[:, :], op=ALU.add).then_inc(TD, 1)

            sum_ada(0)
            square_hidden(0)
            add_ada(0)
            sum_ada(1)
            lr, li = pwn[:, 18, :], pwn[:, 19, :]
            x = [tmpn[0:DK, i, :] for i in range(16)]
            MUL, ADD, SUB = ALU.mult, ALU.add, ALU.subtract

            def tt(o, a, b, op):
                return dve.tensor_tensor(out=o, in0=a, in1=b, op=op)

            dve.wait_ge(sem["b_in"], 64)
            then(dve.tensor_copy(bbar, bin_))
            dve.wait_ge(sem["step_ready"], 1)
            step = stepn[:, :].unsqueeze(2).broadcast_to([DK, 2, 64])
            two = lambda v: v.rearrange("p (e n) -> p e n", e=2)
            then(tt(two(x[0]), two(lr), step, MUL))
            then(tt(two(x[5]), two(li), step, MUL))
            then(dve.tensor_scalar(x[6], x[5], float(1 / (2 * np.pi)), ROUND, MUL, ADD))
            then(dve.tensor_scalar(x[6], x[6], ROUND, None, SUB))
            for piece in TWO_PI:
                then(dve.scalar_tensor_tensor(out=x[5], in0=x[6], scalar=-float(piece), in1=x[5], op0=MUL, op1=ADD))
            dve.tensor_scalar(x[1], x[5], 3.1415925, -3.1415925, ALU.min, ALU.max).then_inc(sem["angle_ready"], 1)
            dve.wait_ge(sem["sines_ready"], 1)
            then(tt(x[3], x[3], x[3], MUL))
            then(dve.tensor_scalar(x[3], x[3], -2.0, 1.0, MUL, ADD))
            dve.memset(pwn[:, 0, :], 1.0)
            dve.memset(pwn[:, 1, :], 0.0)
            tt(pwn[:, 2, :], x[2], x[3], MUL)
            then(tt(pwn[:, 3, :], x[2], x[4], MUL))
            ar, ai = pwn[:, 2, :], pwn[:, 3, :]

            def times(o_r, o_i, a, b, c, d, sign=1):
                tt(x[7], a, c, MUL)
                tt(x[8], b, d, MUL)
                tt(x[9], a, d, MUL)
                then(tt(x[10], b, c, MUL))
                tt(o_r, x[7], x[8], SUB if sign > 0 else ADD)
                then(tt(o_i, x[10], x[9], ADD if sign > 0 else SUB))

            for n in range(2, 9):
                times(pwn[:, 2 * n, :], pwn[:, 2 * n + 1, :], pwn[:, 2 * n - 2, :], pwn[:, 2 * n - 1, :], ar, ai)
            tt(x[11], lr, lr, MUL)
            then(tt(x[12], li, li, MUL))
            then(tt(x[11], x[11], x[12], ADD))
            then(dve.reciprocal(x[11], x[11]))
            then(dve.tensor_scalar(x[12], ar, -1.0, None, ADD))
            times(x[13], x[14], x[12], ai, lr, li, -1)
            tt(pwn[:, 18, :], x[13], x[11], MUL)
            tt(pwn[:, 19, :], x[14], x[11], MUL).then_inc(sem["poles_ready"], 1)

            def gain(n, layer, c):
                then(dve.scalar_tensor_tensor(out=gsc[:, n, :], in0=ada[:, layer, 8:16, c], scalar=1.0,
                                              in1=vecT[:, VEC["norm_g_2"] + 8 * layer:VEC["norm_g_2"] + 8 * layer + 8],
                                              op0=ADD, op1=MUL))

            def context():
                gain(0, 0, 0)
                gain(1, 0, 1)
                taken(dve, "ctx_ssq")
                then(dve.reciprocal(std2[:, :], std2[:, :]))
                for j in range(DT):
                    dve.scalar_tensor_tensor(out=hcT[:, j, :], in0=ctxT[:, j, :], scalar=gsc[:, 1, j:j + 1],
                                             in1=std2[:, :], op0=MUL, op1=MUL).then_inc(sem["ctx_scaled"], 1)

            def make_g(places, bl, n):
                d, m = bl // 3, 8 * (bl % 3)
                pr, pi = powers(d, 0, 8, m)
                b_r, b_i = [bbar[:, c, 8 * bl:8 * bl + 8, :].unsqueeze(2).broadcast_to([P, 8, 8, 16]) for c in range(2)]
                re, im = [places[c].rearrange("p k (j h) -> p k j h", h=16) for c in range(2)]
                tt(g1, pr, b_r, MUL)
                then(tt(re, pi, b_i, MUL))
                then(tt(re, g1, re, SUB))
                tt(g1, pr, b_i, MUL)
                then(tt(im, pi, b_r, MUL))
                tt(im, g1, im, ADD).then_inc(sem["g_ready"], 1)
                dve.wait_ge(sem["g_ready"], n)

            def hidden_low(i):
                for j in range(4):
                    dve.wait_ge(sem["hidden_high"], 4 * (i - 1) + j + 1)
                    u = uT[:, i % 2, j, :]
                    tt(ro(u), u, back(hid_r(i, j)), SUB).then_inc(sem["hidden_low"], 1)

            for i in range(1, 8):
                if i >= 2:
                    sum_ada(ADA_AFTER_UP[i])
                    hidden_low(i - 1)
                square_hidden(i)
                add_ada(ADA_AFTER_UP[i])
                if i == 2:
                    taken(dve, "cT", 2)
                    dve.wait_ge(sem["cb_zero"], 1)
                    for e in range(2):
                        rows = slice(64 * e, 64 * e + 64)
                        for c in range(2):
                            dve.tensor_scalar(cb[rows, :, c, 16 * e:16 * e + 16], cc[rows, c, :, :], 1.0 - 2 * c, None, MUL)\
                                .then_inc(sem["cb_ready"], 1)
                    taken(dve, "lamT", 1)
                    fr, fi = [pwT[:, 18 + c, :].unsqueeze(2).broadcast_to([P, DK, 16]) for c in range(2)]
                    br, bi = bbar[:, 0, :, :], bbar[:, 1, :, :]
                    t1, t2 = bin_[:, 0, :, :], bin_[:, 1, :, :]
                    then(tt(t1, br, fi, MUL))
                    then(tt(t2, bi, fr, MUL))
                    then(tt(t1, t1, t2, ADD))
                    then(tt(t2, bi, fi, MUL))
                    then(tt(br, br, fr, MUL))
                    tt(br, br, t2, SUB)
                    ins = dve.tensor_copy(bi, t1)
                    ins.then_inc(sem["bbar_ready"], 1)
                    dve.wait_ge(sem["bbar_ready"], 1)
                if i >= 2:
                    make_g([Gk[:, c, :, :] for c in range(2)], i - 2, i - 1)
                if i == 2:
                    for j in range(DT):
                        dve.wait_ge(sem["mlp_high"], j + 1)
                        tt(r(hT[:, j, :]), hT[:, j, :], back(uHi[:, j, :]), SUB).then_inc(sem["mlp_low"], 1)
                if i in ADA_AFTER_DOWN:
                    sum_ada(ADA_AFTER_DOWN[i])
                add_down(i - 1)
                if i in ADA_AFTER_DOWN:
                    add_ada(ADA_AFTER_DOWN[i])
                if i >= 2:
                    ps = filled(dve, ("kk", i - 2))
                    dve.tensor_copy(K[:, (i - 2) // 3, 256 * ((i - 2) % 3):256 * ((i - 2) % 3) + 256], ps[:, 0:256])\
                        .then_inc(TD, 1)
                if i == 5:
                    taken(dve, ("ada", 3))
                    context()
            hidden_low(7)
            dve.wait_ge(sem["k_moved"], 16)
            then(tt(k0[0:16], kt[0:16], K[0:16, 1, :].rearrange("p (g h) -> p g h", h=16), ADD))
            then(tt(kt[0:16], ident[0:16, 0:16].unsqueeze(1).broadcast_to([16, GROUPS, 16]),
                    skipT[:, :].unsqueeze(2).broadcast_to([16, GROUPS, 16]), MUL))
            tt(k0[0:16], k0[0:16], kt[0:16], ADD).then_inc(sem["k0_ready"], 1)
            add_down(7)
            taken(dve, ("ada", 11))
            gain(2, 1, 0)
            taken(dve, "fin_ssq")
            then(dve.reciprocal(std[:, :], std[:, :]))
            pos = weights(dve, "pos").rearrange("p (j n) -> p j n", j=DT)
            for j in range(DT):
                n = mark(dve.scalar_tensor_tensor(out=xT[:, j, :], in0=xT[:, j, :], scalar=g("norm_final_g", j),
                                                  in1=std[:, :], op0=MUL, op1=MUL))
                dve.wait_ge(sem["dve_step"], n)
                tt(xT[:, j, :], xT[:, j, :], pos[:, j, :], ADD).then_inc(sem["pos_added"], 1)

            def modulated(name, k, low=None):
                taken(dve, name + "_ssq")
                then(dve.reciprocal(std[:, :], std[:, :]))
                for j in range(DT):
                    dve.scalar_tensor_tensor(out=hT[:, j, :], in0=xT[:, j, :], scalar=gsc[:, k, j:j + 1], in1=std[:, :],
                                             op0=MUL, op1=MUL).then_inc(sem[name + "_scaled"], 1)
                    if low and j >= 2:
                        low(j - 2)
                if low:
                    low(DT - 2)
                    low(DT - 1)

            def ev_low(j):
                dve.wait_ge(sem["ev_high"], j + 1)
                dve.scalar_tensor_tensor(out=r(hT[:, j, :]), in0=hT[:, j, :], scalar=ada[:, 0, j, 0:1], in1=back(vHi[:, j, :]),
                                         op0=ADD, op1=SUB).then_inc(sem["ev_low"], 1)

            def od_low(j):
                dve.wait_ge(sem["od_high"], j + 1)
                dve.scalar_tensor_tensor(out=r(hT[:, j, :]), in0=hT[:, j, :], scalar=ada[:, 1, j, 0:1], in1=back(hHi[:, j, :]),
                                         op0=ADD, op1=SUB).then_inc(sem["od_low"], 1)

            dve.wait_ge(sem["pos_added"], DT)
            modulated("ev", 0, ev_low)
            n = chunk_at["fch"]
            chunk_used(dve, occupant(n))
            fw = ring[:, n % SLOTS, 256:512].rearrange("p (i d) -> p i d", i=2)
            dve.memset(fw[0:64, :, 64:128], 0.0)
            dve.memset(fw[64:128, :, 0:64], 0.0).then_inc(sem["fch_zero"], 1)
            for bl in range(6):
                if bl >= 3:
                    filled(dve, ("wt", 4 * (bl - 3) + 3))
                make_g([input_matrices(bl, c) for c in range(2)], bl, 7 + bl)
                if bl == 2:
                    filled(dve, "ub", 1)
                    for j in range(DT):
                        tt(hT[:, j, :], back(vHi[:, j, :]), back(hT[:, j, :]), ADD).then_inc(sem["h_restored"], 1)
            taken(dve, ("v", 23))

            def both(qf, qb, swap=False):
                at, other = V_AT[0] + qf, V_AT[1] + qb
                c = PAIRS * VC
                if swap:
                    return bass.AP(tensor=arena, offset=at + c, ap=[[ARENA, P], [other - at, 2], [-c, 2], [VC, PAIRS]])
                return bass.AP(tensor=arena, offset=at, ap=[[ARENA, P], [other - at, 2], [c, 2], [VC, PAIRS]])

            a8 = area(24352, 2, 2, 2, PAIRS)
            for d in range(2):
                for c in range(2):
                    dve.tensor_copy(a8[:, 0, d, c, :], pwT[:, 16, PAIRS * d:PAIRS * d + PAIRS])
                    n = mark(dve.tensor_scalar(a8[:, 1, d, c, :], pwT[:, 17, PAIRS * d:PAIRS * d + PAIRS],
                                               2.0 * c - 1, None, MUL))
            dve.wait_ge(sem["dve_step"], n)

            def scan_step(now, before):
                first = mark(tt(m8[:, 0], both(*before), a8[:, 0], MUL))
                mark(tt(m8[:, 1], both(*before, swap=True), a8[:, 1], MUL))
                o = both(*now)
                dve.wait_ge(sem["dve_step"], first)
                then(tt(o, o, m8[:, 0], ADD))
                return tt(o, o, m8[:, 1], ADD)

            for q in range(1, NCTX):
                then(scan_step((q, NCTX - 1 - q), (q - 1, NCTX - q)))
            then(dve.tensor_copy(Vb[:, :, :, NCH], Vb[:, :, :, 0]))
            for q in range(NCTX, NCH):
                ins = scan_step((q, NCH - 1 - (q - NCTX)), (q - 1, NCH - (q - NCTX)))
                if q < NCH - 1:
                    then(ins)
            ins.then_inc(sem["scanned"], 1)
            for bl in range(3, 6):
                filled(dve, "ys", bl - 3)
                make_ca(dve, then, bl, g1, "ca_by_dve", 2 * (bl - 3) + 2)
            for i in range(2):
                taken(dve, "z", 6 + i)
                tt(zT[:, 6 + i, :], zT[:, 6 + i, :], ubT[:, i, :], MUL).then_inc(sem["fnet_gated"], 1)

            def e_low(j):
                dve.wait_ge(sem["e_high"], j + 3 if j < 6 else j - 5)
                o = hT[:, j, :] if j < 6 else zT[:, j, :]
                tt(r(o) if j < 6 else ro(o), o, back(ro(eHi[:, j, :])), SUB).then_inc(sem["e_low"], 1)

            for i in range(6):
                taken(dve, "glu", i)
                if i == 0:
                    for k in range(6):
                        dve.wait_ge(sem[f"ys_out{k}"], 16)
                then(tt(hT[:, i, :], yg[:, i, :], sg[:, i % 2, :], MUL))
                tt(hT[:, i, :], hT[:, i, :], zT[:, i, :], MUL).then_inc(sem["glu_gated"], 1)
                if i == 0:
                    e_low(6)
                    e_low(7)
                if i >= 2:
                    e_low(i - 2)
            e_low(4)
            e_low(5)

            def add_gated(stage, layer):
                for i in range(DT):
                    ps = filled(dve, stage, i)
                    dve.scalar_tensor_tensor(out=xT[:, i, :], in0=ps[:, :], scalar=ada[:, layer, 16 + i, 0:1],
                                             in1=xT[:, i, :], op0=MUL, op1=ADD).then_inc(TD, 1)

            add_gated("eo", 0)
            taken(dve, "eo", 7)
            modulated("od", 2, od_low)
            dve.memset(gb[:, :, 0:8], 0.0)
            dve.memset(cx[:, :, 0:1], 0.0)
            dve.memset(cx[:, :, SEQ + 1:SEQ + 2], 0.0)
            then(dve.memset(gb[:, :, 8 + SEQ:], 0.0))
            dve.wait_ge(sem["rc_in"], 16)
            for i in range(4):
                taken(dve, "pool", i)
                b = gb[:, i, :]
                n = SEQ + 16
                then(tt(sw[0][:, 1:n], b[:, 0:n - 1], b[:, 1:n], ADD))
                for k in range(i):
                    e = 1 << k
                    then(tt(sw[(k + 1) % 2][:, 2 * e:n - 2 * e], sw[k % 2][:, e:n - 3 * e], sw[k % 2][:, 3 * e:n - e], ADD))
                then(tt(sw[i % 2][:, 8:8 + SEQ], sw[i % 2][:, 8:8 + SEQ], rc[:, i, :], MUL))
                tt(pooled[:, i, :], sw[i % 2][:, 8:8 + SEQ], b[:, 8:8 + SEQ], SUB).then_inc(sem["pooled"], 1)
                dve.wait_ge(sem["pooled"], i + 1)
            for i in range(4):
                taken(dve, "cg", i)
                ps = filled(dve, "xp", i)
                tt(cx[:, i, 1:SEQ + 1], cgT[:, i, :], ps[:, :], MUL).then_inc(TD, 1)
            for i in range(4):
                taken(dve, "xp", i)
                o = cgT[:, i, :]
                then(dve.tensor_scalar(o, cx[:, i, 0:SEQ], g("conv_w_2", i), None, MUL))
                for k in (1, 2):
                    then(dve.scalar_tensor_tensor(out=o, in0=cx[:, i, k:k + SEQ], scalar=g("conv_w_2", 4 * k + i), in1=o,
                                                  op0=MUL, op1=ADD))
                taken(dve, "bg", i)
                then(tt(o, o, bgT[:, i, :], MUL))
            for i in range(4):
                ps = filled(dve, "pm", i)
                dve.tensor_scalar(pooled[:, i, :], ps[:, :], g("pool_scale_2", i), None, MUL).then_inc(TD, 1)
            taken(dve, "pm", 3)

            def y_low(j):
                dve.wait_ge(sem["y_high"], j + 1)
                tt(ro(zoT[:, j, :]), zoT[:, j, :], back(ro(yHi[:, j, :])), SUB).then_inc(sem["y_low"], 1)

            for i in range(DT):
                taken(dve, "zo", i)
                tt(zoT[:, i, :], zoT[:, i, :], pooled[:, i, :] if i < 4 else cgT[:, i - 4, :], MUL)\
                    .then_inc(sem["odd_gated"], 1)
                if i >= 2:
                    y_low(i - 2)
            y_low(DT - 2)
            y_low(DT - 1)
            add_gated("oo", 1)
            taken(dve, "oo", 7)
            norm("end", "final_g_2")


INPUTS = ["x", "mem", "norm_mix_g", "w_in", "kv_norm_g", "w_uk", "w_uv", "w_out", "norm_cross_g", "norm_mem_g",
          "w_q_cross", "w_kv_cross", "w_o_cross", "norm_mlp_g", "w_up", "w_down", "norm_final_g", "c_2", "ctx_2",
          "c_ctx_2", "norm_g_2", "ada_w_2", "ada_b_2", "even_w_in_2", "even_w_out_2", "s5_lam_re_2", "s5_lam_im_2",
          "s5_log_step_2", "s5_b_re_2", "s5_b_im_2", "s5_c_re_2", "s5_c_im_2", "s5_d_2", "s5_glu_w_2", "s5_glu_b_2",
          "fnet_w_2", "odd_w_in_2", "odd_w_out_2", "pool_w_2", "pool_scale_2", "conv_w_2", "final_g_2"]


def kernel(**inputs):
    import concourse.bacc as bacc
    from concourse.bass_utils import run_bass_kernel_spmd

    nc = bacc.Bacc("TRN2", target_bir_lowering=False, num_devices=1)
    arrays, args = {}, {}
    for name, a in [(n, inputs[n]) for n in INPUTS] + list(constants().items()):
        a = np.ascontiguousarray(a)
        arrays["in_" + name] = a
        args[name] = nc.dram_tensor("in_" + name, a.shape, mybir.dt.from_np(a.dtype), kind="ExternalInput").ap()
    out = nc.dram_tensor("out_0", (1, SEQ, D), F32, kind="ExternalOutput").ap()
    build(nc, args, out)
    r = run_bass_kernel_spmd(nc, [arrays], core_ids=[0])
    return r.results[0]["out_0"]
```
